# Optimizing a Trainium2 kernel written in Bass

```python
import jax
import jax.numpy as jnp
from jax import lax
import numpy as np

D_MODEL = 1024
BATCH = 1
SEQ = 256
DEPTH = 1
DEC_BATCH = 8
DEC_SEQ = 1
PAST_LEN = 2048
PAGE_SIZE = 128

EPS = 1e-6
GDN_HEADS = 8
GDN_DK = 128
GDN_DV = 128
CONV_W = 4
GDN_CHUNK = 64
MLA_HEADS = 8
Q_LORA = 512
KV_LORA = 512
NOPE_DIM = 128
ROPE_DIM = 64
V_DIM = 128
ROPE_THETA = 10000.0
Q_BLOCK = 128
MLA_SCALE = (NOPE_DIM + ROPE_DIM) ** -0.5
D_FF = 4 * D_MODEL
QKV_WIDTH = GDN_HEADS * (2 * GDN_DK + GDN_DV)
Z_WIDTH = GDN_HEADS * GDN_DV
LATENT_WIDTH = KV_LORA + ROPE_DIM
GATE_WIDTH = 2 * D_MODEL
OFF_Z = QKV_WIDTH
OFF_BETA = OFF_Z + Z_WIDTH
OFF_DECAY = OFF_BETA + GDN_HEADS
OFF_QDOWN = OFF_DECAY + GDN_HEADS
OFF_KVDOWN = OFF_QDOWN + Q_LORA
OFF_GATES = OFF_KVDOWN + LATENT_WIDTH
IN_WIDTH = OFF_GATES + GATE_WIDTH
IN_SPLITS = (OFF_Z, OFF_BETA, OFF_DECAY, OFF_QDOWN, OFF_KVDOWN, OFF_GATES)

kernel_name = 'hybrid_gdn_mla_gated_decoder_step'

def rms_norm(x, g):
    xf = x.astype(jnp.float32)
    y = xf * lax.rsqrt(jnp.mean(jnp.square(xf), axis=-1, keepdims=True) + EPS)
    return (y * g.astype(jnp.float32)).astype(x.dtype)

def l2_normalize(x):
    xf = x.astype(jnp.float32)
    return xf * lax.rsqrt(jnp.sum(jnp.square(xf), axis=-1, keepdims=True) + EPS)

def apply_rope(x, pos):
    inv = jnp.power(ROPE_THETA, -jnp.arange(0, ROPE_DIM, 2, dtype=jnp.float32) / ROPE_DIM)
    ang = pos.astype(jnp.float32)[:, None] * inv[None, :]
    cos, sin = jnp.cos(ang), jnp.sin(ang)
    if x.ndim == 4:
        cos, sin = cos[:, None, :], sin[:, None, :]
    xf = x.astype(jnp.float32)
    x1, x2 = xf[..., :ROPE_DIM // 2], xf[..., ROPE_DIM // 2:]
    return jnp.concatenate([x1 * cos - x2 * sin, x1 * sin + x2 * cos], axis=-1).astype(x.dtype)

def causal_conv(buf, x, w):
    xpad = jnp.concatenate([buf.astype(x.dtype), x], axis=1)
    t = x.shape[1]
    y = xpad[:, 0:t] * w[0]
    for i in range(1, CONV_W):
        y = y + xpad[:, i:i + t] * w[i]
    return jax.nn.silu(y), xpad[:, -(CONV_W - 1):]

def gdn_inputs(qkv_raw, b, a, conv_buf, conv_w, a_log, dt_bias):
    bsz, t = qkv_raw.shape[:2]
    qkv, new_buf = causal_conv(conv_buf, qkv_raw, conv_w)
    q, k, v = jnp.split(qkv, [GDN_HEADS * GDN_DK, 2 * GDN_HEADS * GDN_DK], axis=-1)
    q = l2_normalize(q.reshape(bsz, t, GDN_HEADS, GDN_DK)) * (GDN_DK ** -0.5)
    k = l2_normalize(k.reshape(bsz, t, GDN_HEADS, GDN_DK))
    v = v.reshape(bsz, t, GDN_HEADS, GDN_DV).astype(jnp.float32)
    beta = jax.nn.sigmoid(b.astype(jnp.float32))
    g = -jnp.exp(a_log.astype(jnp.float32)) * jax.nn.softplus(
        a.astype(jnp.float32) + dt_bias.astype(jnp.float32))
    return q, k, v, g, beta, new_buf

def gdn_chunked(q, k, v, g, beta, s0):
    bsz, t, h, dk = q.shape
    dv = v.shape[-1]
    n = t // GDN_CHUNK

    def to_chunks(arr):
        return jnp.moveaxis(arr, 1, 2).reshape(bsz, h, n, GDN_CHUNK, *arr.shape[3:])

    q, k, v, g, beta = (to_chunks(arr) for arr in (q, k, v, g, beta))
    G = jnp.cumsum(g, axis=-1)
    idx = jnp.arange(GDN_CHUNK)
    incl = idx[:, None] >= idx[None, :]
    strict = idx[:, None] > idx[None, :]
    diff = G[..., :, None] - G[..., None, :]
    decay = jnp.where(incl, jnp.exp(jnp.where(incl, diff, 0.0)), 0.0)
    kb = k * beta[..., None]
    vb = v * beta[..., None]
    L = jnp.where(strict, jnp.einsum('bhnid,bhnjd->bhnij', kb, k) * decay, 0.0)
    rhs = jnp.concatenate([vb, kb * jnp.exp(G)[..., None]], axis=-1)
    sol = lax.linalg.triangular_solve(L, rhs, left_side=True, lower=True, unit_diagonal=True)
    u0, w = sol[..., :dv], sol[..., dv:]
    aqk = jnp.einsum('bhnid,bhnjd->bhnij', q, k) * decay
    qg = q * jnp.exp(G)[..., None]
    kd = k * jnp.exp(G[..., -1:] - G)[..., None]
    g_end = jnp.exp(G[..., -1])
    xs = tuple(jnp.moveaxis(arr, 2, 0) for arr in (u0, w, qg, aqk, kd, g_end))

    def step(s, inp):
        u0_n, w_n, qg_n, aqk_n, kd_n, g_end_n = inp
        u = u0_n - jnp.einsum('bhik,bhkv->bhiv', w_n, s)
        o = jnp.einsum('bhik,bhkv->bhiv', qg_n, s) + jnp.einsum('bhij,bhjv->bhiv', aqk_n, u)
        s = g_end_n[..., None, None] * s + jnp.einsum('bhik,bhiv->bhkv', kd_n, u)
        return s, o

    s, o = lax.scan(step, s0.astype(jnp.float32), xs)
    o = jnp.moveaxis(o, 0, 2).reshape(bsz, h, t, dv)
    return jnp.moveaxis(o, 1, 2), s

def gdn_recurrent(q, k, v, g, beta, s0):
    xs = tuple(jnp.moveaxis(arr, 1, 0) for arr in (q, k, v, g, beta))

    def step(s, inp):
        q_t, k_t, v_t, g_t, b_t = inp
        s = jnp.exp(g_t)[..., None, None] * s
        u = b_t[..., None] * (v_t - jnp.einsum('bhk,bhkv->bhv', k_t, s))
        s = s + jnp.einsum('bhk,bhv->bhkv', k_t, u)
        return s, jnp.einsum('bhk,bhkv->bhv', q_t, s)

    s, o = lax.scan(step, s0.astype(jnp.float32), xs)
    return jnp.moveaxis(o, 0, 1), s

def gdn_output(o, z, gdn_norm):
    bsz, t = o.shape[:2]
    zf = z.reshape(bsz, t, GDN_HEADS, GDN_DV).astype(jnp.float32)
    y = rms_norm(o, gdn_norm) * jax.nn.silu(zf)
    return y.reshape(bsz, t, Z_WIDTH).astype(z.dtype)

def mla_queries_and_latent(q_down, kv_down, pos, q_a_norm, w_uq, kv_a_norm,
                           q_norm_nope, q_norm_rope, k_norm_rope):
    bsz, t = q_down.shape[:2]
    q = (rms_norm(q_down, q_a_norm) @ w_uq).reshape(bsz, t, MLA_HEADS, NOPE_DIM + ROPE_DIM)
    qn = rms_norm(q[..., :NOPE_DIM], q_norm_nope)
    qr = apply_rope(rms_norm(q[..., NOPE_DIM:], q_norm_rope), pos)
    c = rms_norm(kv_down[..., :KV_LORA], kv_a_norm)
    kr = apply_rope(rms_norm(kv_down[..., KV_LORA:], k_norm_rope), pos)
    return qn, qr, jnp.concatenate([c, kr], axis=-1)

def mla_keys(latent, w_uk, w_uv, k_norm_nope):
    bsz, s = latent.shape[:2]
    c = latent[..., :KV_LORA].astype(w_uk.dtype)
    kr = latent[..., KV_LORA:].astype(w_uk.dtype)
    kn = rms_norm((c @ w_uk).reshape(bsz, s, MLA_HEADS, NOPE_DIM), k_norm_nope)
    v = (c @ w_uv).reshape(bsz, s, MLA_HEADS, V_DIM)
    return kn, kr, v

def mla_scores(qn, qr, kn, kr):
    s = jnp.einsum('bqhd,bkhd->bhqk', qn, kn) + jnp.einsum('bqhr,bkr->bhqk', qr, kr)
    return s.astype(jnp.float32) * MLA_SCALE

def mla_prompt_attention(qn, qr, kn, kr, v):
    bsz, t = qn.shape[:2]
    nb = t // Q_BLOCK
    kpos = jnp.arange(t)

    def blocks(arr):
        return jnp.moveaxis(arr.reshape(bsz, nb, Q_BLOCK, *arr.shape[2:]), 1, 0)

    def attend(inp):
        qn_b, qr_b, i = inp
        s = mla_scores(qn_b, qr_b, kn, kr)
        qpos = i * Q_BLOCK + jnp.arange(Q_BLOCK)
        s = jnp.where(kpos[None, :] <= qpos[:, None], s, -jnp.inf)
        p = jax.nn.softmax(s, axis=-1).astype(v.dtype)
        return jnp.einsum('bhqk,bkhd->bqhd', p, v)

    o = lax.map(attend, (blocks(qn), blocks(qr), jnp.arange(nb)))
    return jnp.moveaxis(o, 0, 1).reshape(bsz, t, MLA_HEADS * V_DIM)

def partial_softmax(s, v):
    m = jnp.max(s, axis=-1)
    p = jnp.exp(s - m[..., None])
    acc = jnp.einsum('bhqk,bkhd->bhqd', p.astype(v.dtype), v).astype(jnp.float32)
    return m, jnp.sum(p, axis=-1), acc

def mla_sample_attention(qn, qr, new_latent, cache_l, page_table, w_uk, w_uv, k_norm_nope):
    bsz, t = qn.shape[:2]

    def page_block(phys):
        kn, kr, v = mla_keys(cache_l[phys], w_uk, w_uv, k_norm_nope)
        return partial_softmax(mla_scores(qn, qr, kn, kr), v)

    m_p, l_p, a_p = lax.map(page_block, page_table.T)
    kn, kr, v = mla_keys(new_latent, w_uk, w_uv, k_norm_nope)
    causal = jnp.tril(jnp.ones((t, t), dtype=bool))
    s = jnp.where(causal, mla_scores(qn, qr, kn, kr), -jnp.inf)
    m_s, l_s, a_s = partial_softmax(s, v)
    m = jnp.concatenate([m_p, m_s[None]], axis=0)
    l = jnp.concatenate([l_p, l_s[None]], axis=0)
    a = jnp.concatenate([a_p, a_s[None]], axis=0)
    wgt = jnp.exp(m - jnp.max(m, axis=0))
    o = jnp.sum(wgt[..., None] * a, axis=0) / jnp.sum(wgt * l, axis=0)[..., None]
    return jnp.moveaxis(o, 1, 2).reshape(bsz, t, MLA_HEADS * V_DIM).astype(qn.dtype)

def merge_and_mlp(x, y_a, y_b, gates, w_ya, w_yb, w_o, norm_mlp, w_up, w_down):
    g_a, g_b = jnp.split(jax.nn.sigmoid(gates), 2, axis=-1)
    x = x + (g_a * (y_a @ w_ya) + g_b * (y_b @ w_yb)) @ w_o
    h = jnp.square(jax.nn.relu(rms_norm(x, norm_mlp) @ w_up))
    return x + h @ w_down

def decoder_layer(x_p, x_s, cache_l, gdn_state_l, conv_state_l, page_table,
                  norm_mix, w_in, conv_w, a_log, dt_bias, gdn_norm,
                  q_a_norm, w_uq, kv_a_norm, w_uk, w_uv,
                  q_norm_nope, q_norm_rope, k_norm_nope, k_norm_rope,
                  w_ya, w_yb, w_o, norm_mlp, w_up, w_down):
    def run_group(x, pos, conv_buf, s0, gdn_core, mla_attend):
        qkv_raw, z, b, a, q_down, kv_down, gates = jnp.split(
            rms_norm(x, norm_mix) @ w_in, IN_SPLITS, axis=-1)
        q, k, v, g, beta, new_buf = gdn_inputs(qkv_raw, b, a, conv_buf, conv_w, a_log, dt_bias)
        o_a, s_new = gdn_core(q, k, v, g, beta, s0)
        y_a = gdn_output(o_a, z, gdn_norm)
        qn, qr, latent = mla_queries_and_latent(q_down, kv_down, pos, q_a_norm, w_uq, kv_a_norm,
                                                q_norm_nope, q_norm_rope, k_norm_rope)
        y_b = mla_attend(qn, qr, latent)
        y = merge_and_mlp(x, y_a, y_b, gates, w_ya, w_yb, w_o, norm_mlp, w_up, w_down)
        return y, latent, s_new, new_buf

    bp, tp = x_p.shape[:2]
    y_p, rows_p, s_p, buf_p = run_group(
        x_p, jnp.arange(tp),
        jnp.zeros((bp, CONV_W - 1, QKV_WIDTH), x_p.dtype),
        jnp.zeros((bp, GDN_HEADS, GDN_DK, GDN_DV), jnp.float32),
        gdn_chunked,
        lambda qn, qr, lat: mla_prompt_attention(qn, qr, *mla_keys(lat, w_uk, w_uv, k_norm_nope)))
    past_len = page_table.shape[1] * PAGE_SIZE
    y_s, rows_s, s_s, buf_s = run_group(
        x_s, past_len + jnp.arange(x_s.shape[1]),
        conv_state_l, gdn_state_l,
        gdn_recurrent,
        lambda qn, qr, lat: mla_sample_attention(qn, qr, lat, cache_l, page_table, w_uk, w_uv, k_norm_nope))
    return y_p, y_s, rows_p, s_p, buf_p, rows_s, s_s, buf_s

def setup_inputs(seed: int = 0) -> dict:
    key = jax.random.key(seed)
    k = jax.random.split(key, 32)
    f32 = jnp.float32
    n_pages = PAST_LEN // PAGE_SIZE
    n_used = DEC_BATCH * n_pages
    n_phys = n_used + n_used // 4

    def dense(kk, fan_in, fan_out):
        return jax.random.normal(kk, (DEPTH, fan_in, fan_out), f32) * fan_in ** -0.5

    def gain(kk, n):
        return 1.0 + 0.02 * jax.random.normal(kk, (DEPTH, n), f32)

    dt = jax.random.uniform(k[8], (DEPTH, GDN_HEADS), f32, 0.001, 0.1)
    return {
        'x_prompt': jax.random.normal(k[0], (BATCH, SEQ, D_MODEL), f32),
        'x_sample': jax.random.normal(k[1], (DEC_BATCH, DEC_SEQ, D_MODEL), f32),
        'cache_mla': jax.random.normal(k[2], (DEPTH, n_phys, PAGE_SIZE, LATENT_WIDTH), f32),
        'state_gdn': jax.random.normal(k[3], (DEPTH, DEC_BATCH, GDN_HEADS, GDN_DK, GDN_DV), f32) * GDN_DK ** -0.5,
        'state_conv': jax.random.normal(k[4], (DEPTH, DEC_BATCH, CONV_W - 1, QKV_WIDTH), f32),
        'page_table': jax.random.permutation(k[5], n_phys)[:n_used].reshape(DEC_BATCH, n_pages).astype(jnp.int32),
        'norm_mix': gain(k[6], D_MODEL),
        'w_in': dense(k[7], D_MODEL, IN_WIDTH),
        'conv_w': jax.random.normal(k[9], (DEPTH, CONV_W, QKV_WIDTH), f32) * CONV_W ** -0.5,
        'a_log': jnp.log(jax.random.uniform(k[10], (DEPTH, GDN_HEADS), f32, 1.0, 16.0)),
        'dt_bias': dt + jnp.log(-jnp.expm1(-dt)),
        'gdn_norm': gain(k[11], GDN_DV),
        'q_a_norm': gain(k[12], Q_LORA),
        'w_uq': dense(k[13], Q_LORA, MLA_HEADS * (NOPE_DIM + ROPE_DIM)),
        'kv_a_norm': gain(k[14], KV_LORA),
        'w_uk': dense(k[15], KV_LORA, MLA_HEADS * NOPE_DIM),
        'w_uv': dense(k[16], KV_LORA, MLA_HEADS * V_DIM),
        'q_norm_nope': gain(k[17], NOPE_DIM),
        'q_norm_rope': gain(k[18], ROPE_DIM),
        'k_norm_nope': gain(k[19], NOPE_DIM),
        'k_norm_rope': gain(k[20], ROPE_DIM),
        'w_ya': dense(k[21], Z_WIDTH, D_MODEL),
        'w_yb': dense(k[22], MLA_HEADS * V_DIM, D_MODEL),
        'w_o': dense(k[23], D_MODEL, D_MODEL),
        'norm_mlp': gain(k[24], D_MODEL),
        'w_up': dense(k[25], D_MODEL, D_FF),
        'w_down': dense(k[26], D_FF, D_MODEL),
    }

def reference(x_prompt, x_sample, cache_mla, state_gdn, state_conv, page_table,
              norm_mix, w_in, conv_w, a_log, dt_bias, gdn_norm,
              q_a_norm, w_uq, kv_a_norm, w_uk, w_uv,
              q_norm_nope, q_norm_rope, k_norm_nope, k_norm_rope,
              w_ya, w_yb, w_o, norm_mlp, w_up, w_down):
    x_p, x_s = x_prompt, x_sample
    rows_p, gdn_p, conv_p, rows_s, gdn_s, conv_s = [], [], [], [], [], []
    for l in range(DEPTH):
        x_p, x_s, rp, sp, bp, rs, ss, bs = decoder_layer(
            x_p, x_s, cache_mla[l], state_gdn[l], state_conv[l], page_table,
            norm_mix[l], w_in[l], conv_w[l], a_log[l], dt_bias[l], gdn_norm[l],
            q_a_norm[l], w_uq[l], kv_a_norm[l], w_uk[l], w_uv[l],
            q_norm_nope[l], q_norm_rope[l], k_norm_nope[l], k_norm_rope[l],
            w_ya[l], w_yb[l], w_o[l], norm_mlp[l], w_up[l], w_down[l])
        rows_p.append(rp)
        gdn_p.append(sp)
        conv_p.append(bp)
        rows_s.append(rs)
        gdn_s.append(ss)
        conv_s.append(bs)
    return (x_p, x_s, jnp.stack(rows_p), jnp.stack(gdn_p), jnp.stack(conv_p),
            jnp.stack(rows_s), jnp.stack(gdn_s), jnp.stack(conv_s))


_drawn_inputs = setup_inputs


def setup_inputs(seed=0):
    import zlib

    import numpy as np

    out = dict(_drawn_inputs(seed))
    spreads = {}
    factors = {'cache_mla': 2.699,
     'gdn_norm': 21.072,
     'q_a_norm': 8.0,
     'kv_a_norm': 3.169,
     'q_norm_nope': 8.0,
     'q_norm_rope': 8.0,
     'k_norm_nope': 8.0,
     'k_norm_rope': 8.0,
     'norm_mlp': 8.925}
    for name, (base, spread) in spreads.items():
        noise = np.random.default_rng([zlib.crc32(name.encode()), seed]).standard_normal(out[name].shape)
        drawn = base * np.exp(spread * noise) if base else spread * noise
        out[name] = jnp.asarray(drawn.astype(out[name].dtype))
    for name, factor in factors.items():
        out[name] = (out[name] * factor).astype(out[name].dtype)
    return out
```

```python
from contextlib import ExitStack

import numpy as np
import concourse.bass as bass
from concourse import mybir

F32 = mybir.dt.float32
F32R = mybir.dt.float32r
I32 = mybir.dt.int32
ALU = mybir.AluOpType
ACT = mybir.ActivationFunctionType
AX = mybir.AxisListType.X
RMAX = bass.bass_isa.ReduceOp.max

P = 128
D = 1024
TP = 256
NS = 8
T = TP + NS
KC = D // P
H = 8
EPS = 1e-6
SCALE = (128 + 64) ** -0.5
LAT = 512
ROPE = 64
LW = LAT + ROPE
PAST = 2048
PAGE = 128
PAGES = PAST // PAGE
NT = NS * PAGES
NG = NT // 4
OFF_BETA = 4096
OFF_QDOWN = OFF_BETA + 16
OFF_KV = OFF_QDOWN + 512
OFF_ROPE = OFF_KV + LAT
OFF_GATES = OFF_KV + LW
CONVW = 4
FF = 4 * D
CH = 128
LEVELS = 7

_at = 0


def _col(n):
    global _at
    a = _at
    _at += n
    return slice(a, _at)


C_ID, C_BD, C_ROT, C_ONE = _col(P), _col(P), _col(P), _col(P)
C_COS, C_SIN = _col(T), _col(T)
C_INCL, C_STRICT = _col(P), _col(P)
C_LVL = [_col(P) for _ in range(LEVELS)]
C_NEG = _col(3 * P)
C_II = _col(16)
C_ZW = _col(32)
C_ZP = _col(16)
C_RSC = _col(1)
C_RSG = _col(1)
C_ALL = _at


def constants():
    c = np.zeros((P, C_ALL), np.float32)
    k, m = np.arange(P)[:, None], np.arange(P)[None, :]
    c[:, C_ID] = k == m
    c[:, C_BD] = k // 64 == m // 64
    c[:, C_ROT] = np.where((k == m + 32) & (m % 64 < 32), -1.0, 0) + ((k == m - 32) & (m % 64 >= 32))
    c[:, C_ONE] = 1.0
    inv = np.power(np.float32(10000.0), -np.arange(0, ROPE, 2, dtype=np.float32) / np.float32(ROPE)).astype(np.float32)
    pos = np.concatenate([np.arange(TP), np.full(NS, PAST)]).astype(np.float32)
    ang = (pos[:, None] * inv[None, :]).astype(np.float32)
    c[:, C_COS] = np.tile(np.cos(ang).T, (4, 1))
    c[:, C_SIN] = np.tile(np.sin(ang).T, (4, 1))
    c[:, C_INCL] = k <= m
    c[:, C_STRICT] = k < m
    for s, at in enumerate(C_LVL):
        b = 1 << s
        c[:, at] = (k // (2 * b) == m // (2 * b)) & (k % (2 * b) >= b) & (m % (2 * b) < b)
    neg = np.where(m > k, np.float32(-1e30), np.float32(0.0))
    c[:, C_NEG] = np.concatenate([neg, np.zeros((P, P)), neg], 1)
    for r in range(8):
        c[r, C_II.start + r] = c[8 + r, C_II.start + r] = 1
        c[32 + r, C_II.start + 8 + r] = c[40 + r, C_II.start + 8 + r] = 1
    c[:, C_ZW.start + 15] = 1
    c[0:64, C_ZP.start + 6] = c[64:128, C_ZP.start + 7] = 1
    c[0:8, C_RSC] = SCALE
    c[8:16, C_RSC] = 1
    c[0:8, C_RSG] = 128 ** -0.5
    c[8:16, C_RSG] = 1
    return c


PR_CONV, PR_MIX, PR_QA, PR_KVA, PR_MLP, PR_GDN, PR_QN, PR_KN, PR_QR, PR_KR, PR_ALL = 0, 96, 104, 108, 112, 120, 121, 122, 123, 124, 125

SIDE = (["params", "x_sum", "rope_raw", "decay_raw", "kv_sum", "kr_sum", "kr_rot", "qd_sum", "nope_rows", "rope_rows"]
        + [f"nope{h}" for h in range(16)] + [f"rope{p}" for p in range(4)] + [f"rot{p}" for p in range(4)]
        + [f"row{k}" for k in range(6)])

SIDE_A = (["bg0", "bg1"] + [f"br{h}" for h in range(H)] + [f"gr{h}" for h in range(H)] + ["l2rows"] + [f"l2b{c}" for c in range(16)]
          + [f"qk{g}" for g in range(4)] + [f"kk{g}" for g in range(4)] + [f"kt{g}" for g in range(4)])
for _s in range(LEVELS):
    SIDE_A += [f"x{_s}_{g}" for g in range(4)]
    for _g in range(4):
        SIDE_A += ([f"t{_s}_{_g}"] if _s < LEVELS - 1 else []) + [f"u{_s}_{_g}"]
for _n in ("uu0", "o0", "s0", "ks", "uu1", "o1", "s1"):
    SIDE_A += [f"{_n}_0", f"{_n}_1"]
SIDE_A += ["kqs", "qks", "krow", "urow"] + [f"out{b}_{g}" for b in range(NS) for g in range(2)] + ["orows"]
SIDE_A += [f"ob{h}" for h in range(H)] + ["x2_sum"] + [f"y{k}" for k in range(6)]
SIDE_B = [f"cs{g}" for g in range(6)] + [f"rw{g}" for g in range(6)] + [f"vt{g}" for g in range(4)]


def a_count(name):
    return SIDE_A.index(name) + 1


def b_count(name):
    return SIDE_B.index(name) + 1


def side(name):
    return SIDE.index(name) + 1


FRONT_DONE = [("qeff_ready", 3), ("snew_ready", 1), ("yb_read", H), ("rows_out", 32)]


def build(nc, I, O):
    C_in, ctx = I["consts"], ExitStack()
    with ctx:
        sems = {}

        def S(name):
            if name not in sems:
                sems[name] = ctx.enter_context(nc.semaphore(name))
            return sems[name]

        taken = {}
        tens, f32r = {}, set()

        def place(name, shape, dt, off):
            off = (off + 31) // 32 * 32
            n = int(np.prod(shape[1:])) * 4
            taken[name] = (off, off + n)
            with ExitStack() as scope:
                if off:
                    scope.enter_context(nc.sbuf_tensor(f"below_{name}", [P, off // 4], F32))
                tens[name] = scope.enter_context(nc.sbuf_tensor(name, shape, dt))
            if dt == F32R:
                f32r.add(name)
            return tens[name], off + n

        o = 0
        consts, o = place("consts_sb", [P, C_ALL], F32, o)
        par, o = place("par", [P, P], F32, o)
        xT, o = place("xT", [P, KC, T], F32, o)
        Ah, o = place("Ah", [P, KC, T], F32R, o)
        Al, o = place("Al", [P, KC, T], F32R, o)
        krT, o = place("krT", [P, T], F32, o)
        decay_raw, o = place("decay_raw", [64, T], F32, o)
        qeff, o = place("qeff", [P, NS, 5, H], F32, o)
        cnew, o = place("cnew", [P, 4, NS], F32, o)
        snew, o = place("snew", [P, 64], F32, o)
        ab, o = place("ab", [64, 4], F32, o)
        ptab, o = place("ptab", [1, NS * PAGES], I32, o)
        rsq, o = place("rsq", [P, 3, T], F32, o)
        yb, o = place("yb", [P, KC, T], F32, o)
        PERSIST = o
        ukh, o = place("ukh", [P, 4, D], F32R, o)
        ukl, o = place("ukl", [P, 4, D], F32R, o)
        ATT = o
        wraw, o = place("wraw", [P, 4, 4, 512], F32, o)
        wh, o = place("wh", [P, 2, 4, 512], F32R, o)
        wl, o = place("wl", [P, 2, 4, 512], F32R, o)
        kv, o = place("kv", [P, 4, T], F32, o)
        ch, o = place("ch", [P, 4, T], F32R, o)
        cl, o = place("cl", [P, 4, T], F32R, o)
        qd, o = place("qd", [P, 4, T], F32, o)
        QH = o
        qdh, o = place("qdh", [P, 4, T], F32R, o)
        qdl, o = place("qdl", [P, 4, T], F32R, o)
        vtok, _ = place("vtok", [P, 2, D], F32, QH)
        sq, o = place("sq", [P, 9, T], F32, o)
        XN = o
        xn, _ = place("xn", [P, KC, T], F32, o)
        qn, o = place("qn", [P, KC, T], F32, o)
        kn, o = place("kn", [P, KC, T], F32, o)
        qr, o = place("qr", [P, 4, T], F32, o)
        wmisc, _ = place("wmisc", [P, KC, 192], F32, taken["kn"][0])
        xtok, _ = place("xtok", [P, 3, D], F32, taken["ukh"][0])
        prow, _ = place("prow", [P, P], F32, taken["ukl"][0])
        assert o <= 212800, o
        o = ATT
        ukf, o = place("ukf", [P, 4, D], F32, o)
        ukT, o = place("ukT", [P, 2, 512], F32, o)
        sc, o = place("sc", [P, 2, 384], F32, o)
        pr, o = place("pr", [P, 2, 384], F32, o)
        pT, o = place("pT", [P, 2, 384], F32, o)
        mx, o = place("mx", [P, H, 2], F32, o)
        ls, o = place("ls", [P, H, 2], F32, o)
        qg, o = place("qg", [P, H, NS], F32, o)
        qk, o = place("qk", [P, 2, H, NS], F32, o)
        qr64, o = place("qr64", [P, 4, NS], F32, o)
        assert o <= taken["kv"][0]
        ltok, e = place("ltok", [P, 3, LW], F32, taken["ch"][0])
        assert e <= taken["qd"][0]
        nrow, e = place("nrow", [16, T], F32, taken["sq"][0] + 4 * T * 4)
        rrow, e = place("rrow", [8, T], F32, e)

        o = PERSIST
        scrow, o = place("scrow", [24, 3 * D], F32, o)
        crow, o = place("crow", [11, 3 * D], F32, o)
        csT, o = place("csT", [P, 24, 24], F32, o)
        ysc, o = place("ysc", [P, 4, T], F32, o)
        assert o <= ATT
        o = PERSIST
        gr, o = place("gr", [P, H, T], F32, o)
        br, o = place("br", [P, H, T], F32, o)
        eg, o = place("eg", [P, H, T], F32, o)
        sm, o = place("sm", [P, 16, 64], F32, o)
        assert o <= ATT
        rhs_, _ = place("rhs_", [P, H, CH], F32, taken["gr"][0])
        uu, _ = place("uu", [P, H, CH], F32, taken["gr"][0] + 4096)
        st, _ = place("st", [P, H, P], F32, taken["br"][0])
        urow, _ = place("urow", [64, 2, P], F32, taken["uu"][0])
        umask, _ = place("umask", [64, H, P], F32, taken["rhs_"][0])
        o = ATT
        U_, o = place("U_", [P, 16, CH], F32, o)
        aqT, o = place("aqT", [P, 16, CH], F32, o)
        vt, o = place("vt", [P, 16, CH], F32, o)
        kd, o = place("kd", [P, 16, CH], F32, o)
        LT = o
        lT, o = place("lT", [P, 16, CH], F32, o)
        T_, o = place("T_", [P, 16, CH], F32, o)
        X_, o = place("X_", [P, 16, CH], F32, o)
        dt_, o = place("dt_", [P, 16, CH], F32, o)
        assert o == taken["wl"][1]
        sst, _ = place("sst", [P, NS, H, P], F32, LT)
        gsq, _ = place("gsq", [P, 16, T], F32, taken["U_"][0])
        osq, _ = place("osq", [P, H, T], F32, taken["vt"][0])
        PROJ = o
        proj, o = place("proj", [P, 48, T], F32, o)
        oT, o = place("oT", [P, H, T], F32, o)
        rw, o = place("rw", [64, T], F32, o)
        bg, o = place("bg", [P, 2, 64], F32, o)
        cols, o = place("cols", [P, 4, 2, H], F32, o)
        assert o <= 212800, o
        gw, _ = place("gw", [64, 5, T], F32, taken["oT"][0])
        lrow, e = place("lrow", [16, T], F32, taken["gw"][1])
        sconv, e = place("sconv", [P, 24, NS], F32, e)
        assert e <= taken["oT"][1]
        orow, e = place("orow", [8, T], F32, taken["cols"][1])
        assert e <= 212800, e
        Bh, o = place("Bh", [P, KC, T], F32R, PROJ)
        Bl, o = place("Bl", [P, KC, T], F32R, o)
        mT, o = place("mT", [P, KC, T], F32, o)
        mtmp, _ = place("mtmp", [P, 4, T], F32, taken["oT"][0])
        Hh, o = place("Hh", [P, 32, T], F32R, PROJ)
        xsq, _ = place("xsq", [P, KC, T], F32, PROJ)
        x2n, _ = place("x2n", [P, KC, T], F32, PROJ + 8448)
        rel, o = place("rel", [P, 2, 4, T], F32, o)
        hsq, o = place("hsq", [P, 4, T], F32, o)
        ytok, o = place("ytok", [P, 3, D], F32, o)
        assert o <= 212800, o
        Hl, o = place("Hl", [P, 32, T], F32R, taken["yb"][0])
        assert o <= ATT

        o = ATT
        craw, o = place("craw", [P, 8, LW], F32, o)
        cTh, o = place("cTh", [P, 5, 512], F32R, o)
        cTl, o = place("cTl", [P, 5, 512], F32R, o)
        nath, o = place("nath", [P, 2, 4, 512], F32R, o)
        natl, o = place("natl", [P, 2, 4, 512], F32R, o)
        ksq, o = place("ksq", [P, 2, D], F32, o)
        qst, o = place("qst", [P, 5, P], F32R, o)
        pst, o = place("pst", [P, 2, 4, P], F32R, o)
        kss, o = place("kss", [P, 2, 4, H], F32, o)
        rk, o = place("rk", [P, 2, 4, H], F32, o)
        ssc, o = place("ssc", [P, 2, 4, H], F32, o)
        smax, o = place("smax", [P, 4, H], F32, o)
        pex, o = place("pex", [P, 2, 4, H], F32, o)
        mhalf, o = place("mhalf", [P, 4, H], F32, o)
        ssb, o = place("ssb", [48, 512], F32, o)
        pvs, o = place("pvs", [16, 512], F32, o)
        mall, o = place("mall", [P, NG, H], F32, o)
        lall, o = place("lall", [P, NG, H], F32, o)
        accT, o = place("accT", [P, NG, 4, H], F32, o)
        wall, o = place("wall", [P, NG, H], F32, o)
        mfin, o = place("mfin", [P, 3, NS, H], F32, o)
        lfin, o = place("lfin", [P, 2, NS, H], F32, o)
        gate, o = place("gate", [1, 1], F32, o)
        olat, o = place("olat", [P, NS, 4, H], F32, o)
        onew, o = place("onew", [P, NS, 4, H], F32, o)
        wuvf, o = place("wuvf", [P, 4, D], F32, o)
        assert o <= 212800, o

        ps = ctx.enter_context(nc.psum_tensor("ps", [P, 8, 512], F32))

        win = I["w_in"][0].rearrange("(c p) n -> p c n", p=P)
        wuq = I["w_uq"][0].rearrange("(c p) (h e) -> p c h e", p=P, e=192)
        wuk = I["w_uk"][0].rearrange("(c p) n -> p c n", p=P)
        wuv = I["w_uv"][0].rearrange("(c p) n -> p c n", p=P)

        front = []
        for half in range(2):
            front.append([(slice(0, 4), win[:, 4 * half:4 * half + 4, OFF_KV:OFF_KV + 512])])
        for half in range(2):
            front.append([(slice(0, 4), win[:, 4 * half:4 * half + 4, OFF_QDOWN:OFF_QDOWN + 512])])
        for g in range(2):
            front.append([(c, wuq[:, c, 4 * g:4 * g + 4, 0:128]) for c in range(4)])
        front.append([(c, wuq[:, c, :, 128:192]) for c in range(4)])
        for g in range(2):
            front.append([(slice(0, 4), wuk[:, :, 512 * g:512 * g + 512])])
        for g in range(2):
            front.append([(slice(0, 4), wuv[:, :, 512 * g:512 * g + 512])])
        NF = len(front)
        NP = NF
        NM = NP + 24
        QP = KC + 32
        QM = QP + 48
        wya, wyb, wo, wup, wdn = (I[n][0].rearrange("(c p) n -> p c n", p=P) for n in ("w_ya", "w_yb", "w_o", "w_up", "w_down"))
        UK = 7
        landed = []
        tot = [0] * 4
        for n, parts in enumerate(front):
            tot[n % 4] += 16 * len(parts)
            landed.append(tot[n % 4])
        landed_end = list(tot)

        def landed_later(ns, r):
            return landed_end[ns % 4] + 16 * ((ns - NF) // 4 + 1) + 16 * r

        def hi_of(n):
            return ukh[:, :, (n - UK) * 512:(n - UK + 1) * 512] if n in (UK, UK + 1) else wh[:, n % 2]

        def lo_of(n):
            return ukl[:, :, (n - UK) * 512:(n - UK + 1) * 512] if n in (UK, UK + 1) else wl[:, n % 2]

        trp = ps[:, 4:6, :].rearrange("p b n -> p (b n)")[:, 0:640].rearrange("p (c n) -> p c n", c=5)
        stp = ps[:, 6, 0:64].rearrange("p (t n) -> p t n", t=4)
        pvt = ps[:, 7, 0:32]

        def n_par(u):
            return u % 2

        def kps(u):
            return ps[:, 2 * (u % 2):2 * (u % 2) + 2, :]

        def wait(eng, name, value):
            if not isinstance(value, int) or value > 0:
                eng.wait_ge(S(name), value)

        block = ctx.enter_context(nc.Block())

        @block.sync
        def _(sp):
            sp.dma_start(xtok[:, 0:2, :], I["x_prompt"][0].rearrange("(t p) n -> p t n", p=P)).then_inc(S("x_landed"), 16)
            sp.dma_start(xtok[0:NS, 2, :], I["x_sample"].rearrange("b s n -> (b s) n")).then_inc(S("x_landed"), 16)
            sp.wait_ge(S("wmisc_clear"), 1)
            for c0, src in ((0, win[:, :, OFF_ROPE:OFF_ROPE + 64]), (64, win[:, :, OFF_ROPE:OFF_ROPE + 64]),
                            (128, win[:, :, OFF_BETA:OFF_BETA + 8]), (160, win[:, :, OFF_BETA + 8:OFF_BETA + 16])):
                sp.dma_start(wmisc[:, :, c0:c0 + src.shape[2]], src).then_inc(S("wmisc_landed"), 16)
            for n, parts in enumerate(front):
                if n >= 4:
                    sp.wait_ge(S("w_hi"), n - 3)
                    sp.wait_ge(S("w_lo"), n - 3)
                for at, src in parts:
                    dst = wraw[:, n % 4, at]
                    if isinstance(at, int):
                        dst = dst.rearrange("p (h e) -> p h e", h=src.shape[1])
                    sp.dma_start(dst, src).then_inc(S(f"w_landed{n % 4}"), 16)
            sp.wait_ge(S("qr_ready"), 1)
            sp.dma_start(qr64[64:128, :, :], qr[0:64, :, TP:T]).then_inc(S("qr64_landed"), 16)
            for w, val in FRONT_DONE + [("ptab_landed", 16)]:
                sp.wait_ge(S(w), val)

            def page(u, n):
                pg = sp.value_load(ptab[0:1, bass.ds(n, 1)] if not isinstance(n, int) else ptab[0:1, n:n + 1], min_val=0, max_val=I["cache_mla"].shape[1] - 1)
                sp.dma_start(craw[:, u, :], I["cache_mla"][0][bass.ds(pg, 1), :, :].rearrange("o p n -> p (o n)")).then_inc(S(f"page_landed{u}"), 16)

            for u in range(8):
                page(u, u)
            sp.dma_start(wuvf[:], wuv).then_inc(S("wuvf_landed"), 16)
            with sp.Fori(0, NT // 8 - 1) as i:
                for u in range(8):
                    sp.wait_ge(S("tr_done"), 8 * i + u + 1)
                    sp.wait_ge(S("nat_hi"), 8 * i + u + 1)
                    sp.wait_ge(S("nat_lo"), 8 * i + u + 1)
                    page(u, 8 * i + (u + 8))
            sp.wait_ge(S("yb_ready"), 1)
            sp.dma_start(scrow[:], I["state_conv"][0].rearrange("b w n -> (b w) n")).then_inc(S("scrow_landed"), 16)

            def load(ns, r, src):
                sp.wait_ge(S("w_hi"), ns - 3 + 4 * r)
                sp.wait_ge(S("w_lo"), ns - 3 + 4 * r)
                sp.dma_start(wraw[:, ns % 4], src).then_inc(S(f"w_landed{ns % 4}"), 16)

            def load_body(ns, r, w, col):
                for u in range(4):
                    load(ns + u, r, w[:, 4 * (u % 2):4 * (u % 2) + 4, bass.ds(col + 512 * (u // 2), 512)])

            with sp.Fori(0, 4) as i:
                load_body(NP, i, win, 1024 * i)
            for i in range(2):
                load_body(NP, 4 + i, win, OFF_GATES + 1024 * i)
            sp.wait_ge(S("b_read"), b_count("rw5"))
            sp.dma_start(O["conv_prompt"][0, 0], crow[0:3, :]).then_inc(S("conv_out"), 16)
            sp.dma_start(O["conv_sample"][0, :, CONVW - 2, :], crow[3:11, :]).then_inc(S("conv_out"), 16)
            sp.dma_start(O["conv_sample"][0, :, 0:CONVW - 2, :], I["state_conv"][0, :, 1:CONVW - 1, :]).then_inc(S("conv_out"), 16)
            sp.wait_ge(S("inverse_done"), 1)
            for b in range(NS):
                sp.dma_start(sst[:, b], I["state_gdn"][0, b].rearrange("h k v -> k h v")).then_inc(S("sst_landed"), 16)
            sp.wait_ge(S("a_read"), a_count("s1_1"))
            sp.dma_start(O["gdn_prompt"][0, 0].rearrange("h k v -> k h v"), st[:]).then_inc(S("gdn_out"), 16)
            for b in range(NS):
                sp.wait_ge(S("a_read"), a_count(f"out{b}_1"))
                sp.dma_start(O["gdn_sample"][0, b].rearrange("h k v -> k h v"), sst[:, b]).then_inc(S("gdn_out"), 16)
            sp.wait_ge(S("gdn_out"), 16 * (1 + NS))
            sp.wait_ge(S("ya_ready"), 1)
            load_body(NM, 0, wya, 0)
            load_body(NM, 1, wyb, 0)
            load_body(NM, 2, wo, 0)
            with sp.Fori(0, 4) as i:
                load_body(NM, 3 + i, wup, 1024 * i)
            for g in range(2):
                for u in range(8):
                    load(NM + u % 4, 7 + 2 * g + u // 4, wdn[:, 4 * u:4 * u + 4, 512 * g:512 * g + 512])
            sp.wait_ge(S("a_read"), len(SIDE_A))
            sp.dma_start(O["y_prompt"][0].rearrange("(t p) n -> p t n", p=P), ytok[:, 0:2, :]).then_inc(S("y_out"), 16)
            sp.dma_start(O["y_sample"].rearrange("b s n -> (b s) n"), ytok[0:NS, 2, :]).then_inc(S("y_out"), 16)
            sp.wait_ge(S("y_out"), 32)
            sp.wait_ge(S("conv_out"), 48)
            sp.wait_ge(S("rows_out"), 32)
            sp.wait_ge(S("ab_landed"), 32)

        @block.gpsimd
        def _(g):
            nc.gpsimd.memset(wmisc[:], 0.0).then_inc(S("wmisc_clear"), 1)
            nc.gpsimd.memset(qeff[0:64, :, 4, :], 0.0).then_inc(S("qeff_clear"), 1)
            g.wait_ge(S("side_read"), len(SIDE))
            g.dma_start(O["rows_prompt"][0, 0].rearrange("(t p) n -> p t n", p=P), ltok[:, 0:2, :]).then_inc(S("rows_out"), 16)
            g.dma_start(O["rows_sample"][0, :, 0, :], ltok[0:NS, 2, :]).then_inc(S("rows_out"), 16)
            for w, val in FRONT_DONE:
                g.wait_ge(S(w), val)
            nc.gpsimd.memset(qst[:].bitcast(F32), 0.0).then_inc(S("att_clear"), 1)
            nc.gpsimd.memset(pst[:].bitcast(F32), 0.0).then_inc(S("att_clear"), 1)
            nc.gpsimd.memset(mhalf[:], -0.5).then_inc(S("att_clear"), 1)
            g.wait_ge(S("att_clear"), 3)

            def group(gg, y):
                g.wait_ge(S("ms_ready"), gg + 1)
                nc.gpsimd.tensor_tensor(rk[:, y], kss[:, y], mhalf[:], ALU.pow).then_inc(S("rk_ready"), 1)
                g.wait_ge(S("s_ready"), gg + 1)
                nc.gpsimd.tensor_tensor(gate[:], mhalf[0:1, 0, 0:1], mhalf[0:1, 0, 0:1], ALU.add)
                nc.gpsimd.partition_all_reduce(smax[:].rearrange("p t h -> p (t h)"), ssc[:, y].rearrange("p t h -> p (t h)"), P, RMAX).then_inc(S("smax_ready"), 1)

            with g.Fori(0, NG // 2) as i:
                for y in range(2):
                    group(2 * i + y, y)
            g.wait_ge(S("yb_ready"), 1)
            nc.gpsimd.memset(rw[:], 0.0).then_inc(S("rw_clear"), 1)

        @block.scalar
        def _(act):
            act.dma_start(consts[:], C_in).then_inc(S("consts_landed"), 16)
            rows = [(PR_CONV, 96, I["conv_w"][0].rearrange("w (c p) -> (w c) p", p=P)),
                    (PR_MIX, 8, I["norm_mix"].rearrange("l (c p) -> (l c) p", p=P)),
                    (PR_QA, 4, I["q_a_norm"].rearrange("l (c p) -> (l c) p", p=P)),
                    (PR_KVA, 4, I["kv_a_norm"].rearrange("l (c p) -> (l c) p", p=P)),
                    (PR_MLP, 8, I["norm_mlp"].rearrange("l (c p) -> (l c) p", p=P)),
                    (PR_GDN, 1, I["gdn_norm"]), (PR_QN, 1, I["q_norm_nope"]), (PR_KN, 1, I["k_norm_nope"])]
            for r, n, src in rows:
                act.dma_start(prow[r:r + n, :], src).then_inc(S("params_landed"), 16)
            for r, name in ((PR_QR, "q_norm_rope"), (PR_KR, "k_norm_rope")):
                for half in range(2):
                    act.dma_start(prow[r:r + 1, 64 * half:64 * half + 64], I[name]).then_inc(S("params_landed"), 16)
            act.dma_start(ab[32:40, 0:1], I["a_log"].rearrange("l h -> h l")).then_inc(S("ab_landed"), 16)
            act.dma_start(ab[32:40, 1:2], I["dt_bias"].rearrange("l h -> h l")).then_inc(S("ab_landed"), 16)
            act.dma_start(ptab[:], I["page_table"].rearrange("b g -> (b g)").rearrange("(o n) -> o n", o=1)).then_inc(S("ptab_landed"), 16)

            def hi(n):
                act.wait_ge(S(f"w_landed{n % 4}"), landed[n])
                if n >= 2:
                    act.wait_ge(S("chunk_done"), 4 * (n - 1))
                nc.scalar.activation(hi_of(n), wraw[:, n % 4], ACT.Copy).then_inc(S("w_hi"), 1)

            def square(out, src, sem):
                nc.scalar.activation(out, src, ACT.Square).then_inc(S(sem), 1)

            def sqrt(rows_, w):
                act.wait_ge(S("side_read"), w)
                nc.scalar.activation(rsq[0:rows_, 1], rsq[0:rows_, 0], ACT.Sqrt).then_inc(S("sqrt_done"), 1)

            act.wait_ge(S("acc_read"), KC)
            square(sq[:, 0:8, :], xT[:], "sq_ready")
            sqrt(P, side("x_sum"))
            hi(0)
            hi(1)
            hi(2)
            hi(3)
            act.wait_ge(S("acc_read"), KC + 4)
            act.wait_ge(S("side_done"), side("x_sum"))
            square(sq[:, 0:4, :], kv[:], "sq_ready")
            act.wait_ge(S("side_read"), side("decay_raw"))
            square(sq[:, 8, :], krT[:], "sq_ready")
            sqrt(P, side("kv_sum"))
            sqrt(P, side("kr_sum"))
            hi(4)
            act.wait_ge(S("acc_read"), KC + 8)
            square(sq[:, 4:8, :], qd[:], "sq_ready")
            sqrt(P, side("qd_sum"))
            hi(5)
            hi(6)
            hi(7)
            hi(8)
            act.wait_ge(S("acc_read"), KC + 16)
            square(sq[:, 0:8, :], qn[:], "sq_ready")
            hi(9)
            hi(10)
            act.wait_ge(S("acc_read"), KC + 28)
            act.wait_ge(S("nope_used"), 1)
            square(sq[:, 0:8, :], kn[:], "sq_ready")
            act.wait_ge(S("side_done"), side("nope_rows"))
            square(sq[:, 0:4, :], qr[:], "sq_ready")
            sqrt(16, side("nope_rows"))
            sqrt(8, side("rope_rows"))

            for h in range(H):
                act.wait_ge(S("max_ready"), h + 1)
                if h >= 2:
                    act.wait_ge(S("pt_done"), h - 1)
                nc.scalar.activation(pr[:, h % 2, 0:128], sc[:, h % 2, 0:128], ACT.Exp, bias=mx[:, h, 0:1], accum_out=ls[:, h, 0:1])
                nc.scalar.activation(pr[:, h % 2, 128:384], sc[:, h % 2, 128:384], ACT.Exp, bias=mx[:, h, 1:2], accum_out=ls[:, h, 1:2]).then_inc(S("exp_done"), 1)
                if h >= 1:
                    act.wait_ge(S("pt_done"), h)
                    if h >= 3:
                        act.wait_ge(S("pv_done"), h - 2)
                    nc.scalar.activation(pT[:, (h - 1) % 2, :], ps[:, 2, 0:384], ACT.Copy).then_inc(S("pt_read"), 1)
            act.wait_ge(S("pt_done"), H)
            act.wait_ge(S("pv_done"), H - 2)
            nc.scalar.activation(pT[:, (H - 1) % 2, :], ps[:, 2, 0:384], ACT.Copy).then_inc(S("pt_read"), 1)

            for w, val in FRONT_DONE:
                act.wait_ge(S(w), val)

            def split_hi(i, u):
                n = 8 * i + u
                act.wait_ge(S("tr_done"), n + 1)
                nc.scalar.activation(cTh[:, :, 128 * (u % 4):128 * (u % 4) + 128], trp, ACT.Copy).then_inc(S("ct_hi"), 1)
                act.wait_ge(S(f"page_landed{u}"), 16 * i + 16)
                if u % 4 == 0:
                    wait(act, "pv_used", 2 * i + u // 4 - 1)
                nc.scalar.activation(nath[:, u // 4, u % 4, :], craw[:, u, 0:LAT], ACT.Copy).then_inc(S("nat_hi"), 1)

            def body_act(i, first, last):
                for u in range(8):
                    n, y, t = 8 * i + u, u // 4, u % 4
                    prev = not (first and y == 0)
                    if u < 7:
                        split_hi(i, u + 1)
                    elif not last:
                        split_hi(i + 1, 0)
                    if t == 1 and prev:
                        act.wait_ge(S("sub_ready"), 2 * i + y)
                        nc.scalar.activation(pex[:, 1 - y], ssc[:, 1 - y], ACT.Exp).then_inc(S("pex_ready"), 1)
                    if t == 2 and prev:
                        act.wait_ge(S("pv_used"), 2 * i + y)
                        wait(act, "pvt_done", 2 * i + y - 1)
                        nc.scalar.activation(pvs[:], ps[0:16, 7, :], ACT.Copy).then_inc(S("pvs_ready"), 1)
                    if t == 3:
                        act.wait_ge(S("qk_done"), 2 * i + y + 1)
                        nc.scalar.activation(ssb[:], ps[0:48, 6, :], ACT.Copy).then_inc(S("ssb_ready"), 1)
                    act.wait_ge(S("k_done"), n + 1)
                    wait(act, "kss_done", n - 1)
                    nc.scalar.activation(ksq[:, n_par(u)], kps(u), ACT.Square).then_inc(S("ksq_ready"), 1)

            split_hi(0, 0)
            body_act(0, True, False)
            with act.Fori(1, NG // 2 - 1) as i:
                body_act(i, False, False)
            body_act(NG // 2 - 1, False, True)
            act.wait_ge(S("sub_ready"), NG)
            nc.scalar.activation(pex[:, 1], ssc[:, 1], ACT.Exp).then_inc(S("pex_ready"), 1)
            act.wait_ge(S("pv_used"), NG)
            nc.scalar.activation(pvs[:], ps[0:16, 7, :], ACT.Copy).then_inc(S("pvs_ready"), 1)
            act.wait_ge(S("mfin_ready"), 1)
            nc.scalar.activation(wall[:], wall[:], ACT.Exp).then_inc(S("wall_ready"), 1)
            nc.scalar.activation(mfin[:, 2], mfin[:, 1], ACT.Exp).then_inc(S("wall_ready"), 1)

            def hi_at(ns, r):
                act.wait_ge(S(f"w_landed{ns % 4}"), landed_later(ns, r))
                act.wait_ge(S("chunk_done"), 4 * (ns - 1) + 16 * r)
                nc.scalar.activation(wh[:, ns % 2], wraw[:, ns % 4], ACT.Copy).then_inc(S("w_hi"), 1)

            def copy_b(name, dst, src):
                k = SIDE_B.index(name)
                act.wait_ge(S("b_done"), k + 1)
                nc.scalar.activation(dst, src(ps[:, k % 4]), ACT.Copy).then_inc(S("b_read"), 1)

            with act.Fori(0, 6) as i:
                for u in range(4):
                    hi_at(NP + u, i)
            act.wait_ge(S("ab_landed"), 32)
            nc.scalar.activation(ab[32:40, 2:3], ab[32:40, 0:1], ACT.Exp).then_inc(S("ea_ready"), 1)
            act.wait_ge(S("nabs_ready"), 1)
            nc.scalar.activation(gw[32:40, 3], gw[32:40, 2], ACT.Exp).then_inc(S("ea_ready"), 1)
            act.wait_ge(S("ea_ready"), 2)
            nc.scalar.activation(gw[32:40, 4], gw[32:40, 3], ACT.Ln, bias=1.0).then_inc(S("ln_ready"), 1)
            act.wait_ge(S("rw_clear"), 1)
            nc.scalar.activation(rw[0:8, :], decay_raw[0:8, :], ACT.Sigmoid).then_inc(S("beta_ready"), 1)
            act.wait_ge(S("acc_read"), QP + 48)
            nc.scalar.activation(proj[:, 32:48, :], proj[:, 32:48, :], ACT.Sigmoid).then_inc(S("gates_ready"), 1)
            for g in range(6):
                copy_b(f"cs{g}", csT[:, 4 * g:4 * g + 4, :].rearrange("p c n -> p (c n)"), lambda b: b[:, 0:96])
            for g in range(6):
                copy_b(f"rw{g}", crow[:, 512 * g:512 * g + 512], lambda b: b[0:11])
            for c in range(24):
                act.wait_ge(S("conv_done"), c + 1)
                nc.scalar.activation(proj[:, c, 0:TP], ysc[:, c % 4, 0:TP], ACT.Silu).then_inc(S("silu_done"), 1)
            act.wait_ge(S("sconv_done"), 1)
            nc.scalar.activation(proj[:, 0:24, TP:T], proj[:, 0:24, TP:T], ACT.Silu).then_inc(S("qkv_ready"), 1)
            nc.scalar.activation(proj[:, 24:32, :], proj[:, 24:32, :], ACT.Silu).then_inc(S("z_ready"), 1)
            act.wait_ge(S("silu_done"), 24)
            act.wait_ge(S("qkv_ready"), 1)
            nc.scalar.activation(gsq[:], proj[:, 0:16, :], ACT.Square).then_inc(S("gsq_ready"), 1)
            act.wait_ge(S("a_read"), a_count("l2rows"))
            nc.scalar.activation(rsq[0:16, 1], rsq[0:16, 0], ACT.Sqrt).then_inc(S("sqrt_done"), 1)
            act.wait_ge(S("gr_ready"), 1)
            nc.scalar.activation(eg[:], gr[:], ACT.Exp).then_inc(S("eg_ready"), 1)
            act.wait_ge(S("kdiff_ready"), 1)
            nc.scalar.activation(cols[:, 0:2], cols[:, 0:2], ACT.Exp).then_inc(S("cols_ready"), 1)
            act.wait_ge(S("dt_ready"), 1)
            nc.scalar.activation(dt_[:], dt_[:], ACT.Exp).then_inc(S("dt_exp"), 1)
            for g in range(4):
                copy_b(f"vt{g}", vt[:, 4 * g:4 * g + 4, :].rearrange("p u n -> p (u n)"), lambda b: b)
            act.wait_ge(S("oT_ready"), 3)
            nc.scalar.activation(osq[:], oT[:], ACT.Square).then_inc(S("osq_ready"), 1)
            act.wait_ge(S("a_read"), a_count("orows"))
            nc.scalar.activation(rsq[0:8, 1], rsq[0:8, 0], ACT.Sqrt).then_inc(S("sqrt_done"), 1)

            for u in range(2):
                hi_at(NM + u, 0)

            def body_hi(r):
                for u in range(4):
                    hi_at(NM + (u + 2) % 4, r + (u + 2) // 4)

            body_hi(0)
            body_hi(1)
            body_hi(2)
            act.wait_ge(S("acc_read"), QM + 24)
            nc.scalar.activation(xsq[:], xT[:], ACT.Square).then_inc(S("xsq_ready"), 1)
            act.wait_ge(S("a_read"), a_count("x2_sum"))
            nc.scalar.activation(rsq[:, 1], rsq[:, 0], ACT.Sqrt).then_inc(S("sqrt_done"), 1)

            def relu_group(g, i):
                for j in range(4):
                    act.wait_ge(S("chunk_done"), 4 * (NM + 12 + 2 * g + 1) + j + 1 + 16 * i)
                    if j == 0:
                        act.wait_ge(S("h_split"), 2 * i + g + 1)
                    nc.scalar.activation(rel[:, g, j, :], ps[:, j, 0:T], ACT.Relu).then_inc(S("acc_read"), 1)

            with act.Fori(0, 4) as i:
                for g in range(2):
                    hi_at(NM + 2 * g + (2 if g == 0 else -2), (3 if g == 0 else 4) + i)
                    relu_group(g, i)
                    hi_at(NM + 2 * g + (3 if g == 0 else -1), (3 if g == 0 else 4) + i)
            for n in range(2, 16):
                hi_at(NM + n % 4, 7 + n // 4)

        @block.vector
        def _(v):
            V = nc.vector
            links = [0]

            def link(ins):
                links[0] += 1
                ins.then_inc(S("dve_link"), 1)
                v.wait_ge(S("dve_link"), links[0])

            def lo(n):
                v.wait_ge(S("w_hi"), n + 1)
                V.tensor_tensor(lo_of(n), wraw[:, n % 4], hi_of(n).bitcast(F32), ALU.subtract).then_inc(S("w_lo"), 1)

            def acc(n, j, q, dst):
                v.wait_ge(S("chunk_done"), 4 * n + j + 1)
                V.tensor_copy(dst, ps[:, q % 4, 0:dst.shape[-1]]).then_inc(S("acc_read"), 1)

            def rsqrt(name, rows_, dst, inv, k, scale=1.0, sem=None):
                b = 4 + (side(name) - 1) % 4
                v.wait_ge(S("side_done"), side(name))
                r = rsq[0:rows_]
                V.tensor_scalar(r[:, 0], ps[0:rows_, b, 0:T], inv, EPS, ALU.mult, ALU.add).then_inc(S("side_read"), 1)
                v.wait_ge(S("sqrt_done"), k)
                link(V.reciprocal(r[:, 1], r[:, 1]))
                link(V.tensor_tensor(r[:, 2], r[:, 1], r[:, 1], ALU.mult))
                link(V.tensor_tensor(r[:, 2], r[:, 2], r[:, 0], ALU.mult))
                link(V.tensor_scalar(r[:, 2], r[:, 2], -0.5, 1.5, ALU.mult, ALU.add))
                ins = V.scalar_tensor_tensor(dst, r[:, 1], scale, r[:, 2], ALU.mult, ALU.mult)
                if sem:
                    ins.then_inc(S(sem), 1)
                else:
                    link(ins)

            def split(src, h_, l_, sem, count=1):
                link(V.tensor_copy(h_, src))
                V.tensor_tensor(l_, src, h_.bitcast(F32), ALU.subtract).then_inc(S(sem), count)

            v.wait_ge(S("side_done"), side("params"))
            V.tensor_copy(par[:, 0:PR_ALL], ps[:, 4, 0:PR_ALL]).then_inc(S("side_read"), 1)
            for c in range(KC):
                v.wait_ge(S("xT_done"), c + 1)
                V.tensor_copy(xT[:, c, :], ps[:, c % 4, 0:T]).then_inc(S("acc_read"), 1)
            rsqrt("x_sum", P, rsq[:, 1], 1.0 / D, 1)
            for c in range(KC):
                i = V.scalar_tensor_tensor(xn[:, c, :], xT[:, c, :], par[:, PR_MIX + c:PR_MIX + c + 1], rsq[:, 1], ALU.mult, ALU.mult)
            link(i)
            split(xn[:], Ah[:], Al[:], "a_ready")
            lo(0)
            lo(1)
            v.wait_ge(S("side_done"), side("rope_raw"))
            V.tensor_copy(krT[:], ps[:, 4 + (side("rope_raw") - 1) % 4, 0:T]).then_inc(S("side_read"), 1)
            v.wait_ge(S("side_done"), side("decay_raw"))
            V.tensor_copy(decay_raw[:], ps[0:64, 4 + (side("decay_raw") - 1) % 4, 0:T]).then_inc(S("side_read"), 1)
            lo(2)
            for j in range(4):
                acc(1, j, KC + j, kv[:, j, :])
            lo(3)
            rsqrt("kv_sum", P, rsq[:, 1], 1.0 / LAT, 2)
            for c in range(4):
                i = V.scalar_tensor_tensor(kv[:, c, :], kv[:, c, :], par[:, PR_KVA + c:PR_KVA + c + 1], rsq[:, 1], ALU.mult, ALU.mult)
            link(i)
            V.tensor_copy(cnew[:], kv[:, :, TP:T])
            split(kv[:], ch[:], cl[:], "c_ready")
            rsqrt("kr_sum", P, rsq[:, 1], 1.0 / ROPE, 3)
            V.scalar_tensor_tensor(krT[:], krT[:], par[:, PR_KR:PR_KR + 1], rsq[:, 1], ALU.mult, ALU.mult).then_inc(S("kr_scaled"), 1)
            v.wait_ge(S("side_done"), side("kr_rot"))
            v.wait_ge(S("kr_scaled"), 1)
            V.tensor_tensor(rsq[:, 0], ps[:, 4 + (side("kr_rot") - 1) % 4, 0:T], consts[:, C_SIN], ALU.mult).then_inc(S("side_read"), 1)
            link(V.tensor_tensor(krT[:], krT[:], consts[:, C_COS], ALU.mult))
            v.wait_ge(S("side_read"), side("kr_rot"))
            V.tensor_tensor(krT[:], krT[:], rsq[:, 0], ALU.add).then_inc(S("kr_ready"), 1)
            lo(4)
            for j in range(4):
                acc(3, j, KC + 4 + j, qd[:, j, :])
            v.wait_ge(S("kr_ready"), 1)
            rsqrt("qd_sum", P, rsq[:, 1], 1.0 / 512, 4)
            for c in range(4):
                i = V.scalar_tensor_tensor(qd[:, c, :], qd[:, c, :], par[:, PR_QA + c:PR_QA + c + 1], rsq[:, 1], ALU.mult, ALU.mult)
            link(i)
            split(qd[:], qdh[:], qdl[:], "qd_ready")
            lo(5)
            for j in range(4):
                acc(4, j, KC + 8 + j, qn[:, j, :])
            lo(6)
            for j in range(4):
                acc(5, j, KC + 12 + j, qn[:, 4 + j, :])
            lo(7)
            for j in range(4):
                acc(6, j, KC + 16 + j, qr[:, j, :])
            lo(8)
            for j in range(4):
                acc(7, j, KC + 20 + j, kn[:, j, :])
            lo(9)
            for j in range(4):
                acc(8, j, KC + 24 + j, kn[:, 4 + j, :])
            lo(10)
            for j in range(4):
                acc(9 + j // 2, 2 * (j % 2) + 1, KC + 28 + j, vtok[:, j % 2, (j // 2) * 512:(j // 2) * 512 + 512])
            v.wait_ge(S("chunk_done"), 4 * NF)
            for c in range(4):
                i = V.tensor_tensor(ukf[:, c, :], ukh[:, c, :].bitcast(F32), ukl[:, c, :].bitcast(F32), ALU.add)
            i.then_inc(S("ukf_ready"), 1)
            v.wait_ge(S("side_done"), side("rope_rows"))
            rsqrt("nope_rows", 16, nrow[:], 1.0 / 128, 5, consts[0:16, C_RSC], "nope_rstd")
            v.wait_ge(S("nope_rstd"), 1)
            rsqrt("rope_rows", 8, rrow[:], 1.0 / 64, 6, SCALE, "rope_rstd")
            for h in range(16):
                t = (qn if h < 8 else kn)[:, h % 8, :]
                g = PR_QN if h < 8 else PR_KN
                v.wait_ge(S("side_done"), side(f"nope{h}"))
                V.scalar_tensor_tensor(t, t, par[:, g:g + 1], ps[:, 4 + (side(f"nope{h}") - 1) % 4, 0:T], ALU.mult, ALU.mult).then_inc(S("side_read"), 1)
            for n, p in enumerate(range(4)):
                v.wait_ge(S("side_done"), side(f"rope{p}"))
                V.scalar_tensor_tensor(qr[:, p, :], qr[:, p, :], par[:, PR_QR:PR_QR + 1], ps[:, 4 + (side(f"rope{p}") - 1) % 4, 0:T], ALU.mult, ALU.mult).then_inc(S("side_read"), 1)
            for p in range(4):
                v.wait_ge(S("side_done"), side(f"rot{p}"))
                v.wait_ge(S("side_read"), side(f"rot{p}") - 1)
                V.tensor_tensor(rsq[:, p % 3], ps[:, 4 + (side(f"rot{p}") - 1) % 4, 0:T], consts[:, C_SIN], ALU.mult).then_inc(S("side_read"), 1)
                link(V.tensor_tensor(qr[:, p, :], qr[:, p, :], consts[:, C_COS], ALU.mult))
                v.wait_ge(S("side_read"), side(f"rot{p}"))
                i = V.tensor_tensor(qr[:, p, :], qr[:, p, :], rsq[:, p % 3], ALU.add)
                if p < 3:
                    link(i)
            i.then_inc(S("qr_ready"), 1)
            V.tensor_scalar(qg[:], qn[:, :, TP:T], par[:, PR_KN:PR_KN + 1], None, ALU.mult).then_inc(S("qg_ready"), 1)
            V.tensor_tensor(qk[:, 0], qn[:, :, TP:T], kn[:, :, TP:T], ALU.mult)
            v.wait_ge(S("qr_ready"), 1)
            V.memset(qk[:, 1], 0.0).then_inc(S("qk_clear"), 1)
            v.wait_ge(S("qk_clear"), 1)
            for b in range(2):
                r = slice(64 * b, 64 * b + 64)
                i = V.tensor_tensor(qk[r, 1].rearrange("p (a b) s -> p a b s", b=2)[:, :, b, :], qr[r, :, TP:T],
                                krT[r, TP:T].unsqueeze(1).to_broadcast([64, 4, NS]), ALU.mult)
            i.then_inc(S("qk_ready"), 1)

            def probs(h):
                v.wait_ge(S("exp_done"), h + 1)
                link(V.reciprocal(ls[:, h, :], ls[:, h, :]))
                V.tensor_scalar(pr[:, h % 2, 0:128], pr[:, h % 2, 0:128], ls[:, h, 0:1], None, ALU.mult)
                V.tensor_scalar(pr[:, h % 2, 128:384], pr[:, h % 2, 128:384], ls[:, h, 1:2], None, ALU.mult).then_inc(S("p_ready"), 1)

            def out_head(h):
                v.wait_ge(S("pv_done"), h + 1)
                V.tensor_copy(yb[:, h, 0:TP], ps[:, 3, 0:TP]).then_inc(S("yb_read"), 1)

            for h in range(H):
                v.wait_ge(S("sc_done"), h + 1)
                if h >= 2:
                    v.wait_ge(S("exp_done"), h - 1)
                V.tensor_tensor(sc[:, h % 2, :], ps[:, h % 2, 0:384], consts[:, C_NEG], ALU.add).then_inc(S("sc_read"), 1)
                v.wait_ge(S("sc_read"), h + 1)
                V.reduce_max(mx[:, h, 0:1], sc[:, h % 2, 0:128], AX)
                link(V.reduce_max(mx[:, h, 1:2], sc[:, h % 2, 128:384], AX))
                V.tensor_scalar(mx[:, h, :], mx[:, h, :], -1.0, None, ALU.mult).then_inc(S("max_ready"), 1)
                if h >= 1:
                    probs(h - 1)
                if h >= 2:
                    out_head(h - 2)
                if h < 6:
                    t = h // 2
                    rows_, c0, n_ = P if t < 2 else NS, 512 * (h % 2), 512 if h % 2 == 0 else ROPE
                    v.wait_ge(S("side_done"), side(f"row{h}"))
                    V.tensor_copy(ltok[0:rows_, t, c0:c0 + n_], ps[0:rows_, 4 + (side(f"row{h}") - 1) % 4, 0:n_]).then_inc(S("side_read"), 1)
            probs(H - 1)
            out_head(H - 2)
            out_head(H - 1)

            for h in range(H):
                v.wait_ge(S("ukT_done"), h + 1)
                if h >= 2:
                    v.wait_ge(S("qe_done"), h - 1)
                V.tensor_copy(ukT[:, h % 2, :], ps[:, 4 + h % 2, :]).then_inc(S("ukT_read"), 1)
            v.wait_ge(S("qe_done"), H)
            V.tensor_copy(qeff[:, :, 0:4, :], ps[:, 6, 0:256].rearrange("p (c h s) -> p s c h", c=4, h=H)).then_inc(S("qeff_ready"), 1)
            qx = qeff[:, :, 4, :].rearrange("p s (a b) -> p a b s", b=2)
            V.tensor_copy(qx[64:128, :, 1, :], qr[64:128, :, TP:T]).then_inc(S("qeff_ready"), 1)
            v.wait_ge(S("qr64_landed"), 16)
            V.tensor_copy(qx[64:128, :, 0, :], qr64[64:128]).then_inc(S("qeff_ready"), 1)
            v.wait_ge(S("qk_sum"), 1)
            V.tensor_copy(snew[:], ps[:, 7, 0:64]).then_inc(S("snew_ready"), 1)

            v.wait_ge(S("att_clear"), 3)

            def split_lo(i, u):
                n = 8 * i + u
                v.wait_ge(S("ct_hi"), n + 1)
                tok = slice(128 * (u % 4), 128 * (u % 4) + 128)
                V.tensor_tensor(cTl[:, :, tok], trp, cTh[:, :, tok].bitcast(F32), ALU.subtract).then_inc(S("ct_lo"), 1)
                v.wait_ge(S("nat_hi"), n + 1)
                V.tensor_tensor(natl[:, u // 4, u % 4, :], craw[:, u, 0:LAT], nath[:, u // 4, u % 4, :].bitcast(F32), ALU.subtract).then_inc(S("nat_lo"), 1)

            def queries(i, s):
                wait(v, "qk_done", 2 * i)
                V.tensor_copy(qst[:, 0:4, 0:8], qeff[:, s, 0:4, :].rearrange("p o c h -> p (o c) h"))
                V.tensor_copy(qst[:, 4, 32:40], qeff[:, s, 4, :].rearrange("p o h -> p (o h)")).then_inc(S("qst_hi"), 1)
                v.wait_ge(S("qst_hi"), i + 1)
                V.tensor_tensor(qst[:, 0:4, 8:16], qeff[:, s, 0:4, :].rearrange("p o c h -> p (o c) h"), qst[:, 0:4, 0:8].bitcast(F32), ALU.subtract)
                V.tensor_tensor(qst[:, 4, 40:48], qeff[:, s, 4, :].rearrange("p o h -> p (o h)"), qst[:, 4, 32:40].bitcast(F32), ALU.subtract).then_inc(S("qst_ready"), 1)

            def probabilities(gg, y):
                v.wait_ge(S("pex_ready"), gg + 1)
                V.tensor_copy(pst[:, y, :, 0:8], pex[:, y]).then_inc(S("pst_hi"), 1)
                V.tensor_reduce(lall[:, bass.ds(gg, 1), :].rearrange("p o h -> p (o h)"), pex[:, y].rearrange("p t h -> p h t"), AX, ALU.add)
                v.wait_ge(S("pst_hi"), gg + 1)
                V.tensor_tensor(pst[:, y, :, 8:16], pex[:, y], pst[:, y, :, 0:8].bitcast(F32), ALU.subtract).then_inc(S("pst_ready"), 1)

            def maxima(gg, y):
                v.wait_ge(S("smax_ready"), gg + 1)
                m = mall[:, bass.ds(gg, 1), :].rearrange("p o h -> p (o h)")
                V.tensor_reduce(m, smax[:].rearrange("p t h -> p h t"), AX, ALU.max).then_inc(S("mall_ready"), 1)
                v.wait_ge(S("mall_ready"), gg + 1)
                V.tensor_tensor(ssc[:, y], ssc[:, y], mall[:, bass.ds(gg, 1), :].to_broadcast([P, 4, H]), ALU.subtract).then_inc(S("sub_ready"), 1)

            def scaled(gg, y):
                v.wait_ge(S("rk_ready"), gg + 1)
                v.wait_ge(S("st_done"), gg + 1)
                V.tensor_tensor(ssc[:, y], stp[:, :, 0:8], rk[:, y], ALU.mult).then_inc(S("s_half"), 1)
                v.wait_ge(S("s_half"), gg + 1)
                V.tensor_tensor(ssc[:, y], stp[:, :, 8:16], ssc[:, y], ALU.add).then_inc(S("s_ready"), 1)

            def body_dve(i, s, first, last):
                queries(i, s)
                for u in range(8):
                    n, y, t = 8 * i + u, u // 4, u % 4
                    prev = not (first and y == 0)
                    gp = 2 * i + y - 1
                    if u < 7:
                        split_lo(i, u + 1)
                    elif not last:
                        split_lo(i + 1, 0)
                    if t == 1 and prev:
                        maxima(gp, 1 - y)
                    v.wait_ge(S("ksq_ready"), n + 1)
                    V.tensor_reduce(kss[:, y, t, :], ksq[:, n_par(u)].rearrange("p (h d) -> p h d", h=H), AX, ALU.add).then_inc(S("kss_done"), 1)
                    if t == 0 and prev:
                        scaled(gp, 1 - y)
                    if t == 1 and prev:
                        probabilities(gp, 1 - y)
                    if t == 3:
                        v.wait_ge(S("kss_done"), n + 1)
                        V.tensor_scalar(kss[:, y], kss[:, y], 1.0 / 128, EPS, ALU.mult, ALU.add).then_inc(S("ms_ready"), 1)
                    if t == 3 and prev:
                        latent_sum(gp)

            def latent_sum(gg):
                v.wait_ge(S("pvt_done"), gg + 1)
                V.tensor_copy(accT[:, bass.ds(gg, 1), :, :].rearrange("p o c h -> p (o c h)"), pvt).then_inc(S("accT_ready"), 1)

            split_lo(0, 0)
            body_dve(0, bass.ds(0, 1), True, False)
            with v.Fori(1, NG // 2 - 1) as i:
                body_dve(i, bass.ds(i // 2, 1), False, False)
            body_dve(NG // 2 - 1, bass.ds(NS - 1, 1), False, True)
            scaled(NG - 1, 1)
            maxima(NG - 1, 1)
            probabilities(NG - 1, 1)
            latent_sum(NG - 1)
            v.wait_ge(S("accT_ready"), NG)
            v.wait_ge(S("mall_ready"), NG)

            sn = snew[:].rearrange("p (h s) -> p s h", s=NS)
            link(V.tensor_reduce(mfin[:, 0], mall[:].rearrange("p (s g) h -> p s h g", g=4), AX, ALU.max))
            link(V.tensor_tensor(mfin[:, 0], mfin[:, 0], sn, ALU.max))
            V.tensor_tensor(wall[:].rearrange("p (s g) h -> p s g h", g=4), mall[:].rearrange("p (s g) h -> p s g h", g=4),
                            mfin[:, 0].unsqueeze(2).to_broadcast([P, NS, 4, H]), ALU.subtract)
            V.tensor_tensor(mfin[:, 1], sn, mfin[:, 0], ALU.subtract).then_inc(S("mfin_ready"), 1)
            v.wait_ge(S("wall_ready"), 2)
            link(V.tensor_tensor(lall[:], lall[:], wall[:], ALU.mult))
            V.tensor_reduce(lfin[:, 0], lall[:].rearrange("p (s g) h -> p s h g", g=4), AX, ALU.add).then_inc(S("lpart_ready"), 1)
            link(V.tensor_tensor(accT[:], accT[:], wall[:].unsqueeze(2).to_broadcast([P, NG, 4, H]), ALU.mult))
            V.tensor_reduce(olat[:].rearrange("p s c h -> p s (c h)"), accT[:].rearrange("p (s g) c h -> p s (c h) g", g=4), AX, ALU.add)
            link(V.tensor_tensor(onew[:], cnew[:].rearrange("p c s -> p s c").unsqueeze(3).to_broadcast([P, NS, 4, H]),
                                 mfin[:, 2].unsqueeze(2).to_broadcast([P, NS, 4, H]), ALU.mult))
            link(V.tensor_tensor(olat[:], olat[:], onew[:], ALU.add))
            v.wait_ge(S("lsum_done"), 1)
            link(V.tensor_tensor(lfin[:, 1].rearrange("p s h -> p (s h)"), ps[:, 6, 0:64], mfin[:, 2].rearrange("p s h -> p (s h)"), ALU.add))
            link(V.reciprocal(lfin[:, 1], lfin[:, 1]))
            V.tensor_tensor(olat[:], olat[:], lfin[:, 1].unsqueeze(2).to_broadcast([P, NS, 4, H]), ALU.mult).then_inc(S("olat_ready"), 1)
            v.wait_ge(S("yb_sample"), 1)
            V.tensor_copy(yb[:, :, TP:T], ps[:, 7, 0:64].rearrange("p (h s) -> p h s", h=H)).then_inc(S("yb_ready"), 1)

            def lo_at(ns, r):
                v.wait_ge(S("w_hi"), ns + 1 + 4 * r)
                V.tensor_tensor(wl[:, ns % 2], wraw[:, ns % 4], wh[:, ns % 2].bitcast(F32), ALU.subtract).then_inc(S("w_lo"), 1)

            def a_bank(name):
                k = SIDE_A.index(name)
                v.wait_ge(S("a_done"), k + 1)
                return ps[:, 4 + k % 4]

            def group_out(g, i):
                for j in range(4):
                    v.wait_ge(S("chunk_done"), 4 * (NP + 2 * g + 1) + j + 1 + 16 * i)
                    V.tensor_copy(proj[:, bass.ds(8 * i + 4 * g + j, 1), :].rearrange("p o n -> p (o n)"), ps[:, j, 0:T]).then_inc(S("acc_read"), 1)

            lo_at(NP, 0)
            lo_at(NP + 1, 0)
            with v.Fori(0, 5) as i:
                lo_at(NP + 2, i)
                group_out(0, i)
                lo_at(NP + 3, i)
                lo_at(NP, i + 1)
                group_out(1, i)
                lo_at(NP + 1, i + 1)
            lo_at(NP + 2, 5)
            group_out(0, 5)
            lo_at(NP + 3, 5)
            group_out(1, 5)

            r32 = slice(32, 40)
            v.wait_ge(S("ab_landed"), 32)
            link(V.tensor_scalar(gw[r32, 0], decay_raw[r32], ab[r32, 1:2], None, ALU.add))
            link(V.tensor_scalar(gw[r32, 1], gw[r32, 0], -1.0, None, ALU.mult))
            V.tensor_tensor(gw[r32, 2], gw[r32, 0], gw[r32, 1], ALU.min).then_inc(S("nabs_ready"), 1)
            link(V.tensor_scalar(gw[r32, 0], gw[r32, 0], 0.0, None, ALU.max))
            v.wait_ge(S("ln_ready"), 1)
            link(V.tensor_tensor(gw[r32, 0], gw[r32, 0], gw[r32, 4], ALU.add))
            link(V.tensor_scalar(gw[r32, 0], gw[r32, 0], ab[r32, 2:3], -1.0, ALU.mult, ALU.mult))
            v.wait_ge(S("rw_clear"), 1)
            for n in range(2):
                s_ = slice(CH * n, CH * n + CH)
                V.tensor_tensor_scan(rw[r32, s_], consts[r32, C_ONE], gw[r32, 0, s_], 0.0, ALU.mult, ALU.add)
            V.tensor_copy(rw[r32, TP:T], gw[r32, 0, TP:T]).then_inc(S("g_ready"), 1)

            v.wait_ge(S("b_done"), b_count("rw5"))
            for c in range(24):
                if c >= 4:
                    v.wait_ge(S("silu_done"), c - 3)
                y, x = ysc[:, c % 4], proj[:, c]
                w_ = [par[:, PR_CONV + 24 * k + c:PR_CONV + 24 * k + c + 1] for k in range(CONVW)]
                link(V.tensor_scalar(y[:, 0:TP], x[:, 0:TP], w_[3], None, ALU.mult))
                for back in range(1, CONVW):
                    ins = V.scalar_tensor_tensor(y[:, back:TP], x[:, 0:TP - back], w_[3 - back], y[:, back:TP], ALU.mult, ALU.add)
                    if back < CONVW - 1:
                        link(ins)
                ins.then_inc(S("conv_done"), 1)
            v.wait_ge(S("b_read"), b_count("cs5"))
            xs = proj[:, 0:24, TP:T]

            def tap(k):
                return par[:, PR_CONV + 24 * k:PR_CONV + 24 * k + 24].unsqueeze(2).to_broadcast([P, 24, NS])

            ss_ = sconv[:]
            link(V.tensor_tensor(xs, xs, tap(3), ALU.mult))
            for k in range(CONVW - 1):
                link(V.tensor_tensor(ss_, csT[:].rearrange("p c (s w) -> p c s w", w=3)[:, :, :, k], tap(k), ALU.mult))
                ins = V.tensor_tensor(xs, xs, ss_, ALU.add)
                if k < 2:
                    link(ins)
            ins.then_inc(S("sconv_done"), 1)

            for n in range(2):
                b_ = a_bank(f"bg{n}")
                V.tensor_copy(bg[:, n, :], b_[:, 0:64]).then_inc(S("a_read"), 1)
            v.wait_ge(S("qkv_ready"), 1)
            v.wait_ge(S("conv_out"), 48)
            for h in range(H):
                b_ = a_bank(f"br{h}")
                V.tensor_copy(br[:, h, :], b_[:, 0:T]).then_inc(S("a_read"), 1)
            for h in range(H):
                b_ = a_bank(f"gr{h}")
                V.tensor_copy(gr[:, h, :], b_[:, 0:T]).then_inc(S("a_read"), 1)
            v.wait_ge(S("a_read"), a_count("gr7"))
            V.tensor_copy(cols[:, 0], bg[:, :, 32:40]).then_inc(S("gr_ready"), 1)
            V.tensor_tensor(cols[:, 1], gr[:, :, 0:TP].rearrange("p h (n i) -> p n h i", n=2)[:, :, :, CH - 1], bg[:, :, 32:40], ALU.subtract).then_inc(S("kdiff_ready"), 1)
            for h in range(H):
                for n in range(2):
                    i = V.tensor_scalar(dt_[:, 2 * h + n, :], gr[:, h, CH * n:CH * n + CH], bg[:, n, 32 + h:33 + h], 0.0, ALU.subtract, ALU.min)
            i.then_inc(S("dt_ready"), 1)
            b_ = a_bank("l2rows")
            V.tensor_scalar(rsq[0:16, 0], b_[0:16, 0:T], 1.0, EPS, ALU.mult, ALU.add).then_inc(S("a_read"), 1)

            def newton(rows_, dst, k, scale, sem):
                v.wait_ge(S("sqrt_done"), k)
                r = rsq[0:rows_]
                link(V.reciprocal(r[:, 1], r[:, 1]))
                link(V.tensor_tensor(r[:, 2], r[:, 1], r[:, 1], ALU.mult))
                link(V.tensor_tensor(r[:, 2], r[:, 2], r[:, 0], ALU.mult))
                link(V.tensor_scalar(r[:, 2], r[:, 2], -0.5, 1.5, ALU.mult, ALU.add))
                V.scalar_tensor_tensor(dst, r[:, 1], scale, r[:, 2], ALU.mult, ALU.mult).then_inc(S(sem), 1)

            newton(16, lrow[:], 7, consts[0:16, C_RSG], "lrow_ready")
            for c in range(16):
                b_ = a_bank(f"l2b{c}")
                V.tensor_tensor(proj[:, c, :], proj[:, c, :], b_[:, 0:T], ALU.mult).then_inc(S("a_read"), 1)
            v.wait_ge(S("dt_exp"), 1)
            link(V.tensor_tensor(dt_[:], dt_[:], consts[:, C_INCL].unsqueeze(1).to_broadcast([P, 16, CH]), ALU.mult))
            for g in range(4):
                b_ = a_bank(f"qk{g}")
                us = slice(4 * g, 4 * g + 4)
                V.tensor_tensor(aqT[:, us, :], b_.rearrange("p (u n) -> p u n", u=4), dt_[:, us, :], ALU.mult).then_inc(S("a_read"), 1)
            v.wait_ge(S("a_read"), a_count("qk3"))
            link(V.tensor_tensor(dt_[:], dt_[:], consts[:, C_STRICT].unsqueeze(1).to_broadcast([P, 16, CH]), ALU.mult))
            link(V.tensor_tensor(dt_[:].rearrange("p (h n) i -> p h (n i)", n=2), dt_[:].rearrange("p (h n) i -> p h (n i)", n=2), br[:, :, 0:TP], ALU.mult))
            for g in range(4):
                b_ = a_bank(f"kk{g}")
                us = slice(4 * g, 4 * g + 4)
                V.tensor_tensor(lT[:, us, :], b_.rearrange("p (u n) -> p u n", u=4), dt_[:, us, :], ALU.mult).then_inc(S("a_read"), 1)
            v.wait_ge(S("cols_ready"), 1)
            for g in range(4):
                b_ = a_bank(f"kt{g}")
                for w in range(4):
                    u = 4 * g + w
                    i = V.tensor_scalar(kd[:, u, :], b_[:, CH * w:CH * w + CH], cols[:, 1, u % 2, u // 2:u // 2 + 1], None, ALU.mult)
                i.then_inc(S("a_read"), 1)
            def small(k):
                return sm[:, k].rearrange("p (s h) -> p s h", h=H)

            idb = consts[:, C_ID].unsqueeze(1).to_broadcast([P, 16, CH])
            V.tensor_copy(T_[:], idb)
            V.tensor_copy(U_[:], idb).then_inc(S("tu_ready"), 1)
            for s_ in range(LEVELS):
                mask = consts[:, C_LVL[s_]].unsqueeze(1).to_broadcast([P, 4, CH])
                for g in range(4):
                    us = slice(4 * g, 4 * g + 4)
                    b_ = a_bank(f"x{s_}_{g}")
                    V.tensor_tensor(X_[:, us, :], b_.rearrange("p (u n) -> p u n", u=4), mask, ALU.mult).then_inc(S("a_read"), 1)
                for g in range(4):
                    us = slice(4 * g, 4 * g + 4)
                    if s_ < LEVELS - 1:
                        b_ = a_bank(f"t{s_}_{g}")
                        V.tensor_tensor(T_[:, us, :], T_[:, us, :], b_.rearrange("p (u n) -> p u n", u=4), ALU.subtract).then_inc(S("a_read"), 1)
                    b_ = a_bank(f"u{s_}_{g}")
                    V.tensor_tensor(U_[:, us, :], U_[:, us, :], b_.rearrange("p (u n) -> p u n", u=4), ALU.subtract).then_inc(S("a_read"), 1)
            v.wait_ge(S("a_read"), a_count(f"u{LEVELS - 1}_3"))
            v.wait_ge(S("eg_ready"), 1)
            V.tensor_copy(small(7), br[:, :, TP:T].rearrange("p h s -> p s h"))
            V.tensor_tensor(proj[:, 0:8, 0:TP], proj[:, 0:8, 0:TP], eg[:, :, 0:TP], ALU.mult).then_inc(S("inverse_done"), 1)
            v.wait_ge(S("inverse_done"), 1)

            v.wait_ge(S("b_read"), b_count("vt3"))
            for h in range(H):
                i = V.tensor_scalar(rhs_[:, h, :], vt[:, 2 * h, :], bg[:, 0, h:h + 1], None, ALU.mult)
            i.then_inc(S("rhs_ready"), 1)
            for g in range(2):
                b_ = a_bank(f"uu0_{g}")
                V.tensor_copy(uu[:, 4 * g:4 * g + 4, :].rearrange("p u n -> p (u n)"), b_).then_inc(S("a_read"), 1)
            for g in range(2):
                b_ = a_bank(f"o0_{g}")
                V.tensor_copy(oT[:, 4 * g:4 * g + 4, 0:CH], b_.rearrange("p (u n) -> p u n", u=4)).then_inc(S("a_read"), 1)
            for g in range(2):
                b_ = a_bank(f"s0_{g}")
                V.tensor_copy(st[:, 4 * g:4 * g + 4, :].rearrange("p u n -> p (u n)"), b_).then_inc(S("a_read"), 1)
            for g in range(2):
                b_ = a_bank(f"ks_{g}")
                for w in range(4):
                    h = 4 * g + w
                    i = V.tensor_scalar(rhs_[:, h, :], b_[:, CH * w:CH * w + CH], cols[:, 0, 1, h:h + 1], None, ALU.mult)
                i.then_inc(S("a_read"), 1)
            v.wait_ge(S("a_read"), a_count("ks_1"))
            link(V.tensor_tensor(rhs_[:], vt[:].rearrange("p (h n) i -> p h n i", n=2)[:, :, 1, :], rhs_[:], ALU.subtract))
            for h in range(H):
                i = V.tensor_scalar(rhs_[:, h, :], rhs_[:, h, :], bg[:, 1, h:h + 1], None, ALU.mult)
            i.then_inc(S("rhs_ready"), 1)
            for g in range(2):
                b_ = a_bank(f"uu1_{g}")
                V.tensor_copy(uu[:, 4 * g:4 * g + 4, :].rearrange("p u n -> p (u n)"), b_).then_inc(S("a_read"), 1)
            for g in range(2):
                b_ = a_bank(f"o1_{g}")
                V.tensor_copy(oT[:, 4 * g:4 * g + 4, CH:TP], b_.rearrange("p (u n) -> p u n", u=4)).then_inc(S("a_read"), 1)
            for h in range(H):
                i = V.tensor_scalar(st[:, h, :], st[:, h, :], eg[:, h, TP - 1:TP], None, ALU.mult)
            link(i)
            for g in range(2):
                b_ = a_bank(f"s1_{g}")
                V.tensor_tensor(st[:, 4 * g:4 * g + 4, :], st[:, 4 * g:4 * g + 4, :], b_.rearrange("p (u n) -> p u n", u=4), ALU.add).then_inc(S("a_read"), 1)

            def sample_of(c0):
                return proj[:, c0:c0 + 8, TP:T].rearrange("p h s -> p s h")

            egs = eg[:, :, TP:T].rearrange("p h s -> p s h")
            brs = small(7)
            V.tensor_copy(small(1), sample_of(8)).then_inc(S("ksmall_ready"), 1)
            V.tensor_tensor(small(2), sample_of(0), sample_of(8), ALU.mult).then_inc(S("ksmall_ready"), 1)
            b_ = a_bank("kqs")
            kq = b_[:, 0:128].rearrange("p (s h t) -> p s h t", s=NS, t=2)
            V.tensor_tensor(small(3), kq[:, :, :, 1], egs, ALU.mult)
            V.tensor_tensor(small(4), kq[:, :, :, 0], egs, ALU.mult).then_inc(S("a_read"), 1)
            v.wait_ge(S("a_read"), a_count("kqs"))
            link(V.tensor_tensor(small(3), sample_of(16), small(3), ALU.subtract))
            V.tensor_tensor(small(5), small(3), brs, ALU.mult).then_inc(S("u_ready"), 1)
            b_ = a_bank("qks")
            v.wait_ge(S("u_ready"), 1)
            V.tensor_tensor(small(6), b_[:, 0:64].rearrange("p (s h) -> p s h", h=H), small(5), ALU.mult).then_inc(S("a_read"), 1)
            v.wait_ge(S("a_read"), a_count("qks"))
            V.tensor_tensor(oT[:, :, TP:T].rearrange("p h s -> p s h"), small(6), small(4), ALU.add).then_inc(S("oT_ready"), 3)
            for k, name in enumerate(("krow", "urow")):
                b_ = a_bank(name)
                V.tensor_copy(urow[:, k, :], b_[0:64, 0:128]).then_inc(S("a_read"), 1)
            v.wait_ge(S("a_read"), a_count("urow"))
            v.wait_ge(S("sst_landed"), 16 * NS)
            for b in range(NS):
                if b >= 1:
                    v.wait_ge(S("a_done"), a_count(f"out{b - 1}_1"))
                V.tensor_tensor(umask[:], urow[:, 1, :].unsqueeze(1).to_broadcast([64, H, P]),
                                consts[0:64, C_ID.start + 8 * b:C_ID.start + 8 * b + 8].unsqueeze(2).to_broadcast([64, H, P]), ALU.mult).then_inc(S("umask_ready"), 1)
                link(V.tensor_tensor(sst[:, b], sst[:, b], egs[:, b, :].unsqueeze(2).to_broadcast([P, H, P]), ALU.mult))
                for g in range(2):
                    b_ = a_bank(f"out{b}_{g}")
                    V.tensor_tensor(sst[:, b, 4 * g:4 * g + 4, :], sst[:, b, 4 * g:4 * g + 4, :], b_.rearrange("p (u n) -> p u n", u=4), ALU.add).then_inc(S("a_read"), 1)

            b_ = a_bank("orows")
            V.tensor_scalar(rsq[0:8, 0], b_[0:8, 0:T], 1.0 / P, EPS, ALU.mult, ALU.add).then_inc(S("a_read"), 1)
            newton(8, orow[:], 8, 1.0, "orow_ready")
            v.wait_ge(S("z_ready"), 1)
            for h in range(H):
                b_ = a_bank(f"ob{h}")
                link(V.scalar_tensor_tensor(oT[:, h, :], oT[:, h, :], par[:, PR_GDN:PR_GDN + 1], b_[:, 0:T], ALU.mult, ALU.mult))
                V.tensor_tensor(oT[:, h, :], oT[:, h, :], proj[:, 24 + h, :], ALU.mult).then_inc(S("a_read"), 1)
            v.wait_ge(S("a_read"), a_count("ob7"))
            split(oT[:], Ah[:], Al[:], "ya_ready")
            split(yb[:], Bh[:], Bl[:], "yb_split")

            lo_at(NM, 0)
            lo_at(NM + 1, 0)
            v.wait_ge(S("gates_ready"), 1)
            v.wait_ge(S("ya_ready"), 1)

            def merged(r, g, out):
                for j in range(4):
                    v.wait_ge(S("chunk_done"), 4 * (NM + 4 * r + 2 * g + 1) + j + 1)
                    out(4 * g + j, ps[:, j, 0:T])

            def gated_a(c, b_):
                V.tensor_tensor(mT[:, c, :], b_, proj[:, 32 + c, :], ALU.mult).then_inc(S("acc_read"), 1)

            def gated_b(c, b_):
                V.tensor_tensor(mtmp[:, c % 4, :], b_, proj[:, 40 + c, :], ALU.mult).then_inc(S("acc_read"), 1)
                v.wait_ge(S("acc_read"), QM + 8 + c + 1)
                V.tensor_tensor(mT[:, c, :], mT[:, c, :], mtmp[:, c % 4, :], ALU.add).then_inc(S("m_part"), 1)

            def residual(c, b_):
                V.tensor_tensor(xT[:, c, :], xT[:, c, :], b_, ALU.add).then_inc(S("acc_read"), 1)

            for r, out in enumerate((gated_a, gated_b, residual)):
                lo_at(NM + 2, r)
                merged(r, 0, out)
                lo_at(NM + 3, r)
                lo_at(NM, r + 1)
                merged(r, 1, out)
                lo_at(NM + 1, r + 1)
                if r == 1:
                    v.wait_ge(S("m_part"), KC)
                    split(mT[:], Ah[:], Al[:], "m_ready")
            v.wait_ge(S("acc_read"), QM + 24)
            b_ = a_bank("x2_sum")
            V.tensor_scalar(rsq[:, 0], b_[:, 0:T], 1.0 / D, EPS, ALU.mult, ALU.add).then_inc(S("a_read"), 1)
            newton(P, rsq[:, 1], 9, 1.0, "x2_rstd")
            v.wait_ge(S("x2_rstd"), 1)
            for c in range(KC):
                i = V.scalar_tensor_tensor(x2n[:, c, :], xT[:, c, :], par[:, PR_MLP + c:PR_MLP + c + 1], rsq[:, 1], ALU.mult, ALU.mult)
            link(i)
            split(x2n[:], Ah[:], Al[:], "h_split", 2)


            def hidden(g, i):
                gg = 2 * i + g
                v.wait_ge(S("acc_read"), QM + 24 + 4 * g + 4 + 8 * i)
                V.tensor_tensor(hsq[:], rel[:, g], rel[:, g], ALU.mult).then_inc(S("hsq_ready"), 1)
                v.wait_ge(S("hsq_ready"), gg + 1)
                hs = bass.ds(4 * gg, 4)
                V.tensor_copy(Hh[:, hs, :], hsq[:]).then_inc(S("h_hi"), 1)
                v.wait_ge(S("h_hi"), gg + 1)
                V.tensor_tensor(Hl[:, hs, :], hsq[:], Hh[:, hs, :].bitcast(F32), ALU.subtract).then_inc(S("h_split"), 1)

            with v.Fori(0, 4) as i:
                lo_at(NM + 2, 3 + i)
                hidden(0, i)
                lo_at(NM + 3, 3 + i)
                lo_at(NM, 4 + i)
                hidden(1, i)
                lo_at(NM + 1, 4 + i)
            for g in range(2):
                for u in range(8):
                    n = 8 * g + u + 2
                    if n < 16:
                        lo_at(NM + n % 4, 7 + n // 4)
                for j in range(4):
                    v.wait_ge(S("chunk_done"), 4 * (NM + 28 + 8 * g + 7) + j + 1)
                    V.tensor_tensor(xT[:, 4 * g + j, :], xT[:, 4 * g + j, :], ps[:, j, 0:T], ALU.add).then_inc(S("acc_read"), 1)
            for k in range(6):
                b_ = a_bank(f"y{k}")
                t = k // 2
                rows_ = P if t < 2 else NS
                V.tensor_copy(ytok[0:rows_, t, 512 * (k % 2):512 * (k % 2) + 512], b_[0:rows_]).then_inc(S("a_read"), 1)

        @block.tensor
        def _(pe):
            mm = nc.tensor.matmul
            ident = consts[:, C_ID]
            ones = consts[:, C_ONE]

            def begin(name):
                k = side(name) - 1
                if k >= 4:
                    pe.wait_ge(S("side_read"), k - 3)
                return ps[:, 4 + k % 4]

            def bank(q):
                if q >= 4:
                    pe.wait_ge(S("acc_read"), q - 3)
                return ps[:, q % 4]

            def unit(n, q0, mh, ml, first, last):
                pe.wait_ge(S("w_lo"), n + 1)
                for j in range(4):
                    if first:
                        bank(q0 + j)
                    out = ps[:, (q0 + j) % 4, 0:T]
                    for kc in range(4):
                        wh_ = hi_of(n)[:, kc, 128 * j:128 * j + 128]
                        wl_ = lo_of(n)[:, kc, 128 * j:128 * j + 128]
                        mm(out, wh_, mh[:, kc, :], start=first and kc == 0, stop=False)
                        mm(out, wh_, ml[:, kc, :], start=False, stop=False)
                        i = mm(out, wl_, mh[:, kc, :], start=False, stop=last and kc == 3)
                    i.then_inc(S("chunk_done"), 1)

            pe.wait_ge(S("consts_landed"), 16)
            pe.wait_ge(S("params_landed"), 16 * 12)
            nc.tensor.transpose(begin("params")[:, 0:PR_ALL], prow[0:PR_ALL, :], ident[0:PR_ALL, 0:PR_ALL]).then_inc(S("side_done"), 1)
            pe.wait_ge(S("x_landed"), 32)
            for c in range(KC):
                b = bank(c)
                for t in range(2):
                    nc.tensor.transpose(b[:, 128 * t:128 * t + 128], xtok[:, t, 128 * c:128 * c + 128], ident)
                nc.tensor.transpose(b[:, TP:T], xtok[0:NS, 2, 128 * c:128 * c + 128], ident[0:NS, 0:NS]).then_inc(S("xT_done"), 1)
            pe.wait_ge(S("sq_ready"), 1)
            b = begin("x_sum")
            for c in range(KC):
                i = mm(b[:, 0:T], ones, sq[:, c, :], start=c == 0, stop=c == KC - 1)
            i.then_inc(S("side_done"), 1)
            pe.wait_ge(S("a_ready"), 1)
            pe.wait_ge(S("wmisc_landed"), 64)
            b = begin("rope_raw")
            for c in range(KC):
                i = mm(b[:, 0:T], wmisc[:, c, 0:128], xn[:, c, :], start=c == 0, stop=c == KC - 1)
            i.then_inc(S("side_done"), 1)
            b = begin("decay_raw")
            for c in range(KC):
                i = mm(b[0:64, 0:T], wmisc[:, c, 128:192], xn[:, c, :], start=c == 0, stop=c == KC - 1)
            i.then_inc(S("side_done"), 1)
            unit(0, KC, Ah[:, 0:4], Al[:, 0:4], True, False)
            unit(1, KC, Ah[:, 4:8], Al[:, 4:8], False, True)
            unit(2, KC + 4, Ah[:, 0:4], Al[:, 0:4], True, False)
            unit(3, KC + 4, Ah[:, 4:8], Al[:, 4:8], False, True)
            pe.wait_ge(S("sq_ready"), 2)
            b = begin("kv_sum")
            for c in range(4):
                i = mm(b[:, 0:T], ones, sq[:, c, :], start=c == 0, stop=c == 3)
            i.then_inc(S("side_done"), 1)
            pe.wait_ge(S("sq_ready"), 3)
            mm(begin("kr_sum")[:, 0:T], consts[:, C_BD], sq[:, 8, :], start=True, stop=True).then_inc(S("side_done"), 1)
            pe.wait_ge(S("kr_scaled"), 1)
            mm(begin("kr_rot")[:, 0:T], consts[:, C_ROT], krT[:], start=True, stop=True).then_inc(S("side_done"), 1)
            pe.wait_ge(S("sq_ready"), 4)
            b = begin("qd_sum")
            for c in range(4):
                i = mm(b[:, 0:T], ones, sq[:, 4 + c, :], start=c == 0, stop=c == 3)
            i.then_inc(S("side_done"), 1)
            pe.wait_ge(S("qd_ready"), 1)
            for g in range(3):
                unit(4 + g, KC + 8 + 4 * g, qdh[:], qdl[:], True, True)
            pe.wait_ge(S("c_ready"), 1)
            for g in range(2):
                unit(UK + g, KC + 20 + 4 * g, ch[:], cl[:], True, True)
            for n in (9, 10):
                pe.wait_ge(S("w_lo"), n + 1)
                for t in range(2):
                    out = bank(KC + 28 + 2 * (n - 9) + t)
                    tok = slice(128 * t, 128 * t + 128)
                    for kc in range(4):
                        mm(out, ch[:, kc, tok], hi_of(n)[:, kc, :], start=kc == 0, stop=False)
                        mm(out, ch[:, kc, tok], lo_of(n)[:, kc, :], start=False, stop=False)
                        i = mm(out, cl[:, kc, tok], hi_of(n)[:, kc, :], start=False, stop=kc == 3)
                    i.then_inc(S("chunk_done"), 2)
            pe.wait_ge(S("sq_ready"), 5)
            b = begin("nope_rows")

            def window(r, n):
                return consts[:, C_ZW.start + 15 - r:C_ZW.start + 15 - r + n]

            for h in range(H):
                i = mm(b[0:16, 0:T], window(h, 16), sq[:, h, :], start=h == 0, stop=False)
            i.then_inc(S("nope_used"), 1)
            pe.wait_ge(S("sq_ready"), 6)
            for h in range(H):
                i = mm(b[0:16, 0:T], window(8 + h, 16), sq[:, h, :], start=False, stop=h == H - 1)
            i.then_inc(S("side_done"), 1)
            pe.wait_ge(S("sq_ready"), 7)
            b = begin("rope_rows")
            for p in range(4):
                i = mm(b[0:8, 0:T], consts[:, C_ZP.start + 6 - 2 * p:C_ZP.start + 14 - 2 * p], sq[:, p, :], start=p == 0, stop=p == 3)
            i.then_inc(S("side_done"), 1)
            pe.wait_ge(S("nope_rstd"), 1)
            for h in range(16):
                mm(begin(f"nope{h}")[:, 0:T], consts[0:16, C_ID.start + h:C_ID.start + h + 1].to_broadcast([16, P]), nrow[:],
                   start=True, stop=True).then_inc(S("side_done"), 1)
            pe.wait_ge(S("rope_rstd"), 1)
            for p in range(4):
                b = begin(f"rope{p}")
                for half in range(2):
                    col = C_ID.start + 2 * p + half
                    i = mm(b[64 * half:64 * half + 64, 0:T], consts[0:8, col:col + 1].to_broadcast([8, 64]), rrow[:], start=True, stop=True)
                i.then_inc(S("side_done"), 1)
            for p in range(4):
                pe.wait_ge(S("side_read"), side(f"rope{p}"))
                mm(begin(f"rot{p}")[:, 0:T], consts[:, C_ROT], qr[:, p, :], start=True, stop=True).then_inc(S("side_done"), 1)

            def scores(h):
                if h >= 2:
                    pe.wait_ge(S("sc_read"), h - 1)
                b = ps[:, h % 2]
                r = slice(64 * (h % 2), 64 * (h % 2) + 64)
                mm(b[:, 0:128], qn[:, h, 0:128], kn[:, h, 0:128], start=True, stop=False)
                mm(b[:, 0:128], qr[r, h // 2, 0:128], krT[r, 0:128], start=False, stop=True)
                mm(b[:, 128:384], qn[:, h, 128:256], kn[:, h, 0:256], start=True, stop=False)
                mm(b[:, 128:384], qr[r, h // 2, 128:256], krT[r, 0:256], start=False, stop=True).then_inc(S("sc_done"), 1)

            def transposed(h):
                pe.wait_ge(S("p_ready"), h + 1)
                if h >= 1:
                    pe.wait_ge(S("pt_read"), h)
                for j in range(3):
                    i = nc.tensor.transpose(ps[:, 2, 128 * j:128 * j + 128], pr[:, h % 2, 128 * j:128 * j + 128], ident)
                i.then_inc(S("pt_done"), 1)

            def weighed(h):
                pe.wait_ge(S("pt_read"), h + 1)
                if h >= 1:
                    pe.wait_ge(S("yb_read"), h)
                b, hd = ps[:, 3], slice(128 * h, 128 * h + 128)
                mm(b[:, 0:128], vtok[:, 0, hd], pT[:, h % 2, 0:128], start=True, stop=True)
                mm(b[:, 128:256], vtok[:, 0, hd], pT[:, h % 2, 128:256], start=True, stop=False)
                mm(b[:, 128:256], vtok[:, 1, hd], pT[:, h % 2, 256:384], start=False, stop=True).then_inc(S("pv_done"), 1)

            pe.wait_ge(S("qr_ready"), 1)
            pe.wait_ge(S("acc_read"), KC + 32)
            for h in range(H):
                scores(h)
                if h >= 1:
                    transposed(h - 1)
                if h >= 2:
                    weighed(h - 2)
                if h < 6:
                    b = begin(f"row{h}")
                    t0, n_ = CH * (h // 2), CH if h < 4 else NS
                    if h % 2 == 0:
                        for c in range(4):
                            i = nc.tensor.transpose(b[0:n_, 128 * c:128 * c + 128], kv[:, c, t0:t0 + n_], ident)
                    else:
                        i = nc.tensor.transpose(b[0:n_, 0:ROPE], krT[0:ROPE, t0:t0 + n_], ident[0:ROPE, 0:ROPE])
                    i.then_inc(S("side_done"), 1)
            transposed(H - 1)
            weighed(H - 2)
            weighed(H - 1)

            pe.wait_ge(S("ukf_ready"), 1)
            pe.wait_ge(S("side_read"), len(SIDE))
            pe.wait_ge(S("qg_ready"), 1)

            def turned(h):
                if h >= 2:
                    pe.wait_ge(S("ukT_read"), h - 1)
                for c in range(4):
                    i = nc.tensor.transpose(ps[:, 4 + h % 2, 128 * c:128 * c + 128], ukf[:, c, 128 * h:128 * h + 128], ident)
                i.then_inc(S("ukT_done"), 1)

            turned(0)
            for h in range(H):
                if h + 1 < H:
                    turned(h + 1)
                pe.wait_ge(S("ukT_read"), h + 1)
                for c in range(4):
                    i = mm(ps[:, 6, (c * H + h) * NS:(c * H + h + 1) * NS], ukT[:, h % 2, 128 * c:128 * c + 128], qg[:, h, :], start=True, stop=True)
                i.then_inc(S("qe_done"), 1)
            pe.wait_ge(S("qk_ready"), 1)
            mm(ps[:, 7, 0:64], ones, qk[:, 0], start=True, stop=False)
            mm(ps[:, 7, 0:64], ones, qk[:, 1], start=False, stop=True).then_inc(S("qk_sum"), 1)

            for w, val in FRONT_DONE:
                pe.wait_ge(S(w), val)

            def transposes(i, u):
                n = 8 * i + u
                pe.wait_ge(S(f"page_landed{u}"), 16 * i + 16)
                wait(pe, "ct_lo", n)
                for c in range(4):
                    nc.tensor.transpose(ps[:, 4, 128 * c:128 * c + 128], craw[:, u, 128 * c:128 * c + 128], ident)
                nc.tensor.transpose(ps[:, 5, 0:128], craw[:, u, LW - 128:LW], ident).then_inc(S("tr_done"), 1)

            def keys(i, u):
                n = 8 * i + u
                tok = slice(128 * (u % 4), 128 * (u % 4) + 128)
                pe.wait_ge(S("ct_lo"), n + 1)
                wait(pe, "ksq_ready", n - 1)
                for half_ in range(2):
                    out, cols = kps(u)[:, half_], slice(512 * half_, 512 * half_ + 512)
                    for c in range(4):
                        mm(out, cTh[:, c, tok], ukh[:, c, cols], start=c == 0, stop=False)
                        mm(out, cTh[:, c, tok], ukl[:, c, cols], start=False, stop=False)
                        k = mm(out, cTl[:, c, tok], ukh[:, c, cols], start=False, stop=c == 3)
                k.then_inc(S("k_done"), 1)

            def query_products(gg, i):
                pe.wait_ge(S("qst_ready"), i + 1)
                wait(pe, "s_ready", gg)
                for c in range(5):
                    mm(ps[:, 6, :], qst[:, c, :], cTh[:, c, :], start=c == 0, stop=False)
                    k = mm(ps[:, 6, :], qst[:, c, :], cTl[:, c, :], start=False, stop=c == 4)
                k.then_inc(S("qk_done"), 1)

            def score_columns(gg):
                pe.wait_ge(S("ssb_ready"), gg + 1)
                for t in range(4):
                    k = mm(stp[:, t, :], ssb[:, 128 * t:128 * t + 128], consts[0:48, C_II], start=True, stop=True)
                k.then_inc(S("st_done"), 1)

            def weigh(gg, y):
                pe.wait_ge(S("pst_ready"), gg + 1)
                wait(pe, "accT_ready", gg)
                for t in range(4):
                    mm(ps[:, 7, :], pst[:, y, t, :], nath[:, y, t, :], start=t == 0, stop=False)
                    k = mm(ps[:, 7, :], pst[:, y, t, :], natl[:, y, t, :], start=False, stop=t == 3)
                k.then_inc(S("pv_used"), 1)

            def latent_columns(gg):
                pe.wait_ge(S("pvs_ready"), gg + 1)
                for c in range(4):
                    k = mm(pvt[:, c * H:(c + 1) * H], pvs[:, 128 * c:128 * c + 128], consts[0:16, C_II.start:C_II.start + 8], start=True, stop=True)
                k.then_inc(S("pvt_done"), 1)

            def body_pe(i, first, last):
                for u in range(8):
                    n, y, t = 8 * i + u, u // 4, u % 4
                    prev = not (first and y == 0)
                    if t == 3:
                        pe.wait_ge(S("ct_lo"), n + 1)
                        query_products(2 * i + y, i)
                    if u < 7:
                        transposes(i, u + 1)
                    elif not last:
                        transposes(i + 1, 0)
                    if t == 2 and prev:
                        weigh(2 * i + y - 1, 1 - y)
                    keys(i, u)
                    if t == 3:
                        score_columns(2 * i + y)
                    if t == 3 and prev:
                        latent_columns(2 * i + y - 1)

            transposes(0, 0)
            body_pe(0, True, False)
            with pe.Fori(1, NG // 2 - 1) as i:
                body_pe(i, False, False)
            body_pe(NG // 2 - 1, False, True)
            weigh(NG - 1, 1)
            latent_columns(NG - 1)
            pe.wait_ge(S("lpart_ready"), 1)
            mm(ps[:, 6, 0:64], ones, lfin[:, 0].rearrange("p s h -> p (s h)"), start=True, stop=True).then_inc(S("lsum_done"), 1)
            pe.wait_ge(S("olat_ready"), 1)
            pe.wait_ge(S("wuvf_landed"), 16)
            for h in range(H):
                for c in range(4):
                    k = mm(ps[:, 7, NS * h:NS * h + NS], wuvf[:, c, 128 * h:128 * h + 128], olat[:, :, c, h], start=c == 0, stop=c == 3)
            k.then_inc(S("yb_sample"), 1)

            def unit_at(ns, r, mh, ml, first, last, drained=None):
                pe.wait_ge(S("w_lo"), ns + 1 + 4 * r)
                for j in range(4):
                    if first and drained is not None:
                        pe.wait_ge(S("acc_read"), drained + j)
                    out = ps[:, j, 0:T]
                    for kc in range(4):
                        w_hi, w_lo = wh[:, ns % 2, kc, 128 * j:128 * j + 128], wl[:, ns % 2, kc, 128 * j:128 * j + 128]
                        mm(out, w_hi, mh[:, kc, :], start=first and kc == 0, stop=False)
                        mm(out, w_hi, ml[:, kc, :], start=False, stop=False)
                        k = mm(out, w_lo, mh[:, kc, :], start=False, stop=last and kc == 3)
                    k.then_inc(S("chunk_done"), 1)

            def body(ns, r, q0, mh, ml):
                for g in range(2):
                    unit_at(ns + 2 * g, r, mh[:, 0:4], ml[:, 0:4], True, False, q0 + 4 * g - 3)
                    unit_at(ns + 2 * g + 1, r, mh[:, 4:8], ml[:, 4:8], False, True)

            pe.wait_ge(S("yb_ready"), 1)
            with pe.Fori(0, 6) as i:
                body(NP, i, QP + 8 * i, Ah, Al)

            def begin_a(name):
                k = SIDE_A.index(name)
                if k >= 4:
                    pe.wait_ge(S("a_read"), k - 3)
                return ps[:, 4 + k % 4]

            def begin_b(name):
                k = SIDE_B.index(name)
                if k >= 4:
                    pe.wait_ge(S("b_read"), k - 3)
                return ps[:, k % 4]

            def a_done(k):
                k.then_inc(S("a_done"), 1)

            def b_done(k):
                k.then_inc(S("b_done"), 1)

            pe.wait_ge(S("acc_read"), QP + 48)
            pe.wait_ge(S("scrow_landed"), 16)
            for g in range(6):
                b = begin_b(f"cs{g}")
                for c in range(4):
                    k = nc.tensor.transpose(b[:, 24 * c:24 * c + 24], scrow[:, 128 * (4 * g + c):128 * (4 * g + c) + 128], ident[0:24, 0:24])
                b_done(k)
            for g in range(6):
                b = begin_b(f"rw{g}")
                for c in range(4):
                    k = nc.tensor.transpose(b[0:11, 128 * c:128 * c + 128], proj[:, 4 * g + c, TP - 3:T], ident)
                b_done(k)
            pe.wait_ge(S("g_ready"), 1)
            pe.wait_ge(S("beta_ready"), 1)
            for n in range(2):
                a_done(nc.tensor.transpose(begin_a(f"bg{n}")[:, 0:64], rw[:, CH * n:CH * n + CH], ident[0:64, 0:64]))
            for name, r0 in (("br", 0), ("gr", 32)):
                for h in range(H):
                    col = C_ID.start + r0 + h
                    a_done(mm(begin_a(f"{name}{h}")[:, 0:T], consts[0:64, col:col + 1].to_broadcast([64, P]), rw[:], start=True, stop=True))
            pe.wait_ge(S("gsq_ready"), 1)
            b = begin_a("l2rows")
            for c in range(16):
                k = mm(b[0:16, 0:T], window(c, 16), gsq[:, c, :], start=c == 0, stop=c == 15)
            a_done(k)
            pe.wait_ge(S("qkv_ready"), 1)
            for g in range(4):
                b = begin_b(f"vt{g}")
                for w in range(4):
                    h, n = (4 * g + w) // 2, w % 2
                    k = nc.tensor.transpose(b[:, CH * w:CH * w + CH], proj[:, 16 + h, CH * n:CH * n + CH], ident)
                b_done(k)
            pe.wait_ge(S("lrow_ready"), 1)
            for c in range(16):
                col = C_ID.start + c
                a_done(mm(begin_a(f"l2b{c}")[:, 0:T], consts[0:16, col:col + 1].to_broadcast([16, P]), lrow[:], start=True, stop=True))

            def four(name, g, product):
                b = begin_a(name)
                for w in range(4):
                    k = product(b[:, CH * w:CH * w + CH], 4 * g + w)
                a_done(k)

            def chunk(c0, u):
                return proj[:, c0 + u // 2, CH * (u % 2):CH * (u % 2) + CH]

            pe.wait_ge(S("a_read"), a_count("l2b15"))
            for g in range(4):
                four(f"qk{g}", g, lambda out, u: mm(out, chunk(8, u), chunk(0, u), start=True, stop=True))
            for g in range(4):
                four(f"kk{g}", g, lambda out, u: mm(out, chunk(8, u), chunk(8, u), start=True, stop=True))
            for g in range(4):
                four(f"kt{g}", g, lambda out, u: nc.tensor.transpose(out, chunk(8, u), ident))
            pe.wait_ge(S("tu_ready"), 1)
            for s_ in range(LEVELS):
                for g in range(4):
                    if s_ >= 1:
                        pe.wait_ge(S("a_read"), a_count(f"t{s_ - 1}_{g}"))
                    four(f"x{s_}_{g}", g, lambda out, u: mm(out, lT[:, u, :], T_[:, u, :], start=True, stop=True))
                for g in range(4):
                    pe.wait_ge(S("a_read"), a_count(f"x{s_}_{g}"))
                    if s_ >= 1:
                        pe.wait_ge(S("a_read"), a_count(f"u{s_ - 1}_{g}"))
                    if s_ < LEVELS - 1:
                        four(f"t{s_}_{g}", g, lambda out, u: mm(out, U_[:, u, :], X_[:, u, :], start=True, stop=True))
                    four(f"u{s_}_{g}", g, lambda out, u: mm(out, X_[:, u, :], U_[:, u, :], start=True, stop=True))
            pe.wait_ge(S("a_read"), a_count(f"u{LEVELS - 1}_3"))
            pe.wait_ge(S("rhs_ready"), 1)
            for g in range(2):
                four(f"uu0_{g}", g, lambda out, h: mm(out, U_[:, 2 * h, :], rhs_[:, h, :], start=True, stop=True))
            for g in range(2):
                pe.wait_ge(S("a_read"), a_count(f"uu0_{g}"))
                four(f"o0_{g}", g, lambda out, h: mm(out, uu[:, h, :], aqT[:, 2 * h, :], start=True, stop=True))
            for g in range(2):
                four(f"s0_{g}", g, lambda out, h: mm(out, kd[:, 2 * h, :], uu[:, h, :], start=True, stop=True))
            for g in range(2):
                pe.wait_ge(S("a_read"), a_count(f"s0_{g}"))
                four(f"ks_{g}", g, lambda out, h: mm(out, chunk(8, 2 * h + 1), st[:, h, :], start=True, stop=True))
            pe.wait_ge(S("rhs_ready"), 2)
            for g in range(2):
                four(f"uu1_{g}", g, lambda out, h: mm(out, U_[:, 2 * h + 1, :], rhs_[:, h, :], start=True, stop=True))

            def second_output(out, h):
                mm(out, st[:, h, :], chunk(0, 2 * h + 1), start=True, stop=False)
                return mm(out, uu[:, h, :], aqT[:, 2 * h + 1, :], start=False, stop=True)

            for g in range(2):
                pe.wait_ge(S("a_read"), a_count(f"uu1_{g}"))
                four(f"o1_{g}", g, second_output)
            for g in range(2):
                four(f"s1_{g}", g, lambda out, h: mm(out, kd[:, 2 * h + 1, :], uu[:, h, :], start=True, stop=True))
            pe.wait_ge(S("sst_landed"), 16 * NS)
            qks = proj[:, 0:16, :].rearrange("p (t h) n -> p h n t", t=2)
            b = begin_a("kqs")
            for s_ in range(NS):
                for h in range(H):
                    at = 2 * (H * s_ + h)
                    k = mm(b[:, at:at + 2], sst[:, s_, h, :], qks[:, h, TP + s_, :], start=True, stop=True)
            a_done(k)
            pe.wait_ge(S("ksmall_ready"), 2)
            a_done(mm(begin_a("qks")[:, 0:64], ones, sm[:, 2], start=True, stop=True))
            a_done(nc.tensor.transpose(begin_a("krow")[0:64, 0:128], sm[:, 1], ident))
            pe.wait_ge(S("u_ready"), 1)
            a_done(nc.tensor.transpose(begin_a("urow")[0:64, 0:128], sm[:, 5], ident))
            pe.wait_ge(S("a_read"), a_count("urow"))
            for s_ in range(NS):
                pe.wait_ge(S("umask_ready"), s_ + 1)
                for g in range(2):
                    a_done(mm(begin_a(f"out{s_}_{g}"), urow[:, 0, :], umask[:, 4 * g:4 * g + 4, :].rearrange("p h n -> p (h n)"), start=True, stop=True))
            pe.wait_ge(S("osq_ready"), 1)
            b = begin_a("orows")
            for h in range(H):
                k = mm(b[0:8, 0:T], window(h, 8), osq[:, h, :], start=h == 0, stop=h == H - 1)
            a_done(k)
            pe.wait_ge(S("orow_ready"), 1)
            for h in range(H):
                col = C_ID.start + h
                a_done(mm(begin_a(f"ob{h}")[:, 0:T], consts[0:8, col:col + 1].to_broadcast([8, P]), orow[:], start=True, stop=True))

            pe.wait_ge(S("b_read"), len(SIDE_B))
            pe.wait_ge(S("ya_ready"), 1)
            body(NM, 0, QM, Ah, Al)
            pe.wait_ge(S("yb_split"), 1)
            body(NM, 1, QM + 8, Bh, Bl)
            pe.wait_ge(S("m_ready"), 1)
            body(NM, 2, QM + 16, Ah, Al)
            pe.wait_ge(S("xsq_ready"), 1)
            b = begin_a("x2_sum")
            for c in range(KC):
                k = mm(b[:, 0:T], ones, xsq[:, c, :], start=c == 0, stop=c == KC - 1)
            a_done(k)
            pe.wait_ge(S("h_split"), 2)
            with pe.Fori(0, 4) as i:
                body(NM, 3 + i, QM + 24 + 8 * i, Ah, Al)
            for g in range(2):
                for u in range(8):
                    if g == 0:
                        pe.wait_ge(S("h_split"), 2 + u + 1)
                    unit_at(NM + u % 4, 7 + 2 * g + u // 4, Hh[:, 4 * u:4 * u + 4], Hl[:, 4 * u:4 * u + 4], u == 0, u == 7, QM + 56 + 4 * g - 3)
            pe.wait_ge(S("acc_read"), QM + 64)
            for k6 in range(6):
                b, t = begin_a(f"y{k6}"), k6 // 2
                n_ = P if t < 2 else NS
                for c in range(4):
                    k = nc.tensor.transpose(b[0:n_, 128 * c:128 * c + 128], xT[:, 4 * (k6 % 2) + c, CH * t:CH * t + n_], ident)
                a_done(k)


INPUTS = ["x_prompt", "x_sample", "cache_mla", "state_gdn", "state_conv", "page_table", "norm_mix", "w_in", "conv_w", "a_log",
          "dt_bias", "gdn_norm", "q_a_norm", "w_uq", "kv_a_norm", "w_uk", "w_uv", "q_norm_nope", "q_norm_rope", "k_norm_nope",
          "k_norm_rope", "w_ya", "w_yb", "w_o", "norm_mlp", "w_up", "w_down"]

OUTPUTS = [("y_prompt", (1, TP, D)), ("y_sample", (NS, 1, D)), ("rows_prompt", (1, 1, TP, LW)), ("gdn_prompt", (1, 1, H, P, P)),
           ("conv_prompt", (1, 1, CONVW - 1, 3 * D)), ("rows_sample", (1, NS, 1, LW)), ("gdn_sample", (1, NS, H, P, P)),
           ("conv_sample", (1, NS, CONVW - 1, 3 * D))]


def kernel(**inputs):
    import concourse.bacc as bacc
    from concourse.bass_utils import run_bass_kernel_spmd

    nc = bacc.Bacc("TRN2", target_bir_lowering=False, num_devices=1)
    arrays = {n: np.ascontiguousarray(inputs[n]) for n in INPUTS}
    arrays["consts"] = constants()
    I = {n: nc.dram_tensor(n, a.shape, mybir.dt.from_np(a.dtype), kind="ExternalInput").ap() for n, a in arrays.items()}
    O = {n: nc.dram_tensor(n, shape, F32, kind="ExternalOutput").ap() for n, shape in OUTPUTS}
    build(nc, I, O)
    r = run_bass_kernel_spmd(nc, [arrays], core_ids=[0])
    return tuple(r.results[0][n] for n, _ in OUTPUTS)
```

```python
from contextlib import ExitStack

import numpy as np
import concourse.bass as bass
from concourse import mybir

F32 = mybir.dt.float32
F32R = mybir.dt.float32r
I32 = mybir.dt.int32
ALU = mybir.AluOpType
ACT = mybir.ActivationFunctionType
AX = mybir.AxisListType.X
RMAX = bass.bass_isa.ReduceOp.max

P = 128
D = 1024
TP = 256
NS = 8
T = TP + NS
KC = D // P
H = 8
EPS = 1e-6
SCALE = (128 + 64) ** -0.5
LAT = 512
ROPE = 64
LW = LAT + ROPE
PAST = 2048
PAGE = 128
PAGES = PAST // PAGE
NT = NS * PAGES
NG = NT // 4
OFF_BETA = 4096
OFF_QDOWN = OFF_BETA + 16
OFF_KV = OFF_QDOWN + 512
OFF_ROPE = OFF_KV + LAT
OFF_GATES = OFF_KV + LW
CONVW = 4
FF = 4 * D
CH = 128
LEVELS = 7

_at = 0


def _col(n):
    global _at
    a = _at
    _at += n
    return slice(a, _at)


C_ID, C_BD, C_ROT, C_ONE = _col(P), _col(P), _col(P), _col(P)
C_COS, C_SIN = _col(T), _col(T)
C_INCL, C_STRICT = _col(P), _col(P)
C_LVL = [_col(P) for _ in range(LEVELS)]
C_NEG = _col(3 * P)
C_II = _col(16)
C_ZW = _col(32)
C_ZP = _col(16)
C_RSC = _col(1)
C_RSG = _col(1)
C_ALL = _at


def constants():
    c = np.zeros((P, C_ALL), np.float32)
    k, m = np.arange(P)[:, None], np.arange(P)[None, :]
    c[:, C_ID] = k == m
    c[:, C_BD] = k // 64 == m // 64
    c[:, C_ROT] = np.where((k == m + 32) & (m % 64 < 32), -1.0, 0) + ((k == m - 32) & (m % 64 >= 32))
    c[:, C_ONE] = 1.0
    inv = np.power(np.float32(10000.0), -np.arange(0, ROPE, 2, dtype=np.float32) / np.float32(ROPE)).astype(np.float32)
    pos = np.concatenate([np.arange(TP), np.full(NS, PAST)]).astype(np.float32)
    ang = (pos[:, None] * inv[None, :]).astype(np.float32)
    c[:, C_COS] = np.tile(np.cos(ang).T, (4, 1))
    c[:, C_SIN] = np.tile(np.sin(ang).T, (4, 1))
    c[:, C_INCL] = k <= m
    c[:, C_STRICT] = k < m
    for s, at in enumerate(C_LVL):
        b = 1 << s
        c[:, at] = (k // (2 * b) == m // (2 * b)) & (k % (2 * b) >= b) & (m % (2 * b) < b)
    neg = np.where(m > k, np.float32(-1e30), np.float32(0.0))
    c[:, C_NEG] = np.concatenate([neg, np.zeros((P, P)), neg], 1)
    for r in range(8):
        c[r, C_II.start + r] = c[8 + r, C_II.start + r] = 1
        c[32 + r, C_II.start + 8 + r] = c[40 + r, C_II.start + 8 + r] = 1
    c[:, C_ZW.start + 15] = 1
    c[0:64, C_ZP.start + 6] = c[64:128, C_ZP.start + 7] = 1
    c[0:8, C_RSC] = SCALE
    c[8:16, C_RSC] = 1
    c[0:8, C_RSG] = 128 ** -0.5
    c[8:16, C_RSG] = 1
    return c


PR_CONV, PR_MIX, PR_QA, PR_KVA, PR_MLP, PR_GDN, PR_QN, PR_KN, PR_QR, PR_KR, PR_ALL = 0, 96, 104, 108, 112, 120, 121, 122, 123, 124, 125

SIDE = (["params", "x_sum", "rope_raw", "decay_raw", "kv_sum", "kr_sum", "qd_sum", "kr_rot", "nope_rows", "rope_rows"]
        + [f"nope{h}" for h in range(16)] + [f"rope{p}" for p in range(4)] + [f"rot{p}" for p in range(4)]
        + [f"row{k}" for k in range(6)])

SIDE_A = (["bg0", "bg1"] + [f"br{h}" for h in range(H)] + [f"gr{h}" for h in range(H)] + ["l2rows"] + [f"l2b{c}" for c in range(16)]
          + [f"qk{g}" for g in range(4)] + [f"kk{g}" for g in range(4)] + [f"kt{g}" for g in range(4)])
for _s in range(LEVELS):
    SIDE_A += [f"x{_s}_{g}" for g in range(4)]
    for _g in range(4):
        SIDE_A += ([f"t{_s}_{_g}"] if _s < LEVELS - 1 else []) + [f"u{_s}_{_g}"]
for _n in ("uu0", "o0", "s0", "ks", "uu1", "o1", "s1"):
    SIDE_A += [f"{_n}_0", f"{_n}_1"]
SIDE_A += ["kqs", "qks", "krow", "urow"] + [f"out{b}_{g}" for b in range(NS) for g in range(2)] + ["orows"]
SIDE_A += [f"ob{h}" for h in range(H)] + ["x2_sum"] + [f"y{k}" for k in range(6)]
SIDE_B = [f"rw{g}" for g in range(6)] + [f"cs{g}" for g in range(6)] + [f"vt{g}" for g in range(4)]


def a_count(name):
    return SIDE_A.index(name) + 1


def b_count(name):
    return SIDE_B.index(name) + 1


def side(name):
    return SIDE.index(name) + 1


FRONT_DONE = [("qeff_ready", 3), ("snew_ready", 1), ("yb_read", H), ("rows_out", 32)]


def build(nc, I, O):
    C_in, ctx = I["consts"], ExitStack()
    with ctx:
        sems = {}

        def S(name):
            if name not in sems:
                sems[name] = ctx.enter_context(nc.semaphore(name))
            return sems[name]

        taken = {}
        tens, f32r = {}, set()

        def place(name, shape, dt, off):
            off = (off + 31) // 32 * 32
            n = int(np.prod(shape[1:])) * 4
            taken[name] = (off, off + n)
            with ExitStack() as scope:
                if off:
                    scope.enter_context(nc.sbuf_tensor(f"below_{name}", [P, off // 4], F32))
                tens[name] = scope.enter_context(nc.sbuf_tensor(name, shape, dt))
            if dt == F32R:
                f32r.add(name)
            return tens[name], off + n

        o = 0
        consts, o = place("consts_sb", [P, C_ALL], F32, o)
        par, o = place("par", [P, P], F32, o)
        xT, o = place("xT", [P, KC, T], F32, o)
        Ah, o = place("Ah", [P, KC, T], F32R, o)
        Al, o = place("Al", [P, KC, T], F32R, o)
        krT, o = place("krT", [P, T], F32, o)
        decay_raw, o = place("decay_raw", [64, T], F32, o)
        qeff, o = place("qeff", [P, NS, 5, H], F32, o)
        cnew, o = place("cnew", [P, 4, NS], F32, o)
        snew, o = place("snew", [P, 64], F32, o)
        ab, o = place("ab", [64, 4], F32, o)
        ptab, o = place("ptab", [1, NS * PAGES], I32, o)
        rsq, o = place("rsq", [P, 3, T], F32, o)
        rx, o = place("rx", [P, T], F32, o)
        yb, o = place("yb", [P, KC, T], F32, o)
        PERSIST = o
        ukh, o = place("ukh", [P, 4, D], F32R, o)
        ukl, o = place("ukl", [P, 4, D], F32R, o)
        ATT = o
        wraw, o = place("wraw", [P, 4, 4, 512], F32, o)
        wh, o = place("wh", [P, 2, 4, 512], F32R, o)
        wl, o = place("wl", [P, 2, 4, 512], F32R, o)
        kv, o = place("kv", [P, 4, T], F32, o)
        ch, o = place("ch", [P, 4, T], F32R, o)
        cl, o = place("cl", [P, 4, T], F32R, o)
        qd, o = place("qd", [P, 4, T], F32, o)
        QH = o
        qdh, o = place("qdh", [P, 4, T], F32R, o)
        qdl, o = place("qdl", [P, 4, T], F32R, o)
        vtok, _ = place("vtok", [P, 2, D], F32, QH)
        sq, o = place("sq", [P, 9, T], F32, o)
        XN = o
        xn, _ = place("xn", [P, KC, T], F32, o)
        qn, o = place("qn", [P, KC, T], F32, o)
        kn, o = place("kn", [P, KC, T], F32, o)
        qr, o = place("qr", [P, 4, T], F32, o)
        wmisc, _ = place("wmisc", [P, KC, 192], F32, taken["kn"][0])
        xtok, _ = place("xtok", [P, 3, D], F32, taken["ukh"][0])
        prow, _ = place("prow", [P, P], F32, taken["ukl"][0])
        assert o <= 212800, o
        o = ATT
        ukf, o = place("ukf", [P, 4, D], F32, o)
        ukT, o = place("ukT", [P, 2, 512], F32, o)
        sc, o = place("sc", [P, 2, 384], F32, o)
        pr, o = place("pr", [P, 3, 384], F32, o)
        pT, o = place("pT", [P, 2, 384], F32, o)
        mx, o = place("mx", [P, H, 2], F32, o)
        ls, o = place("ls", [P, H, 2], F32, o)
        qg, o = place("qg", [P, H, NS], F32, o)
        qk, o = place("qk", [P, 2, H, NS], F32, o)
        qr64, o = place("qr64", [P, 4, NS], F32, o)
        assert o <= taken["kv"][0]
        ltok, e = place("ltok", [P, 3, LW], F32, taken["ch"][0])
        assert e <= taken["qd"][0]
        nrow, e = place("nrow", [16, T], F32, taken["sq"][0] + 4 * T * 4)
        rrow, e = place("rrow", [8, T], F32, e)

        o = PERSIST
        scrow, o = place("scrow", [24, 3 * D], F32, o)
        crow, o = place("crow", [11, 3 * D], F32, o)
        csT, o = place("csT", [P, 24, 24], F32, o)
        ysc, o = place("ysc", [P, 4, T], F32, o)
        assert o <= ATT
        o = PERSIST
        gr, o = place("gr", [P, H, T], F32, o)
        br, o = place("br", [P, H, T], F32, o)
        eg, o = place("eg", [P, H, T], F32, o)
        sm, o = place("sm", [P, 16, 64], F32, o)
        assert o <= ATT
        rhs_, _ = place("rhs_", [P, H, CH], F32, taken["gr"][0])
        uu, _ = place("uu", [P, H, CH], F32, taken["gr"][0] + 4096)
        st, _ = place("st", [P, H, P], F32, taken["br"][0])
        urow, _ = place("urow", [64, 2, P], F32, taken["uu"][0])
        umask = [place("umask0", [64, H, P], F32, taken["rhs_"][0])[0], place("umask1", [64, H, P], F32, taken["br"][0] + 4096)[0]]
        assert taken["umask1"][1] <= taken["br"][1]
        o = ATT
        U_, o = place("U_", [P, 16, CH], F32, o)
        aqT, o = place("aqT", [P, 16, CH], F32, o)
        vt, o = place("vt", [P, 16, CH], F32, o)
        kd, o = place("kd", [P, 16, CH], F32, o)
        LT = o
        lT, o = place("lT", [P, 16, CH], F32, o)
        T_, o = place("T_", [P, 16, CH], F32, o)
        X_, o = place("X_", [P, 16, CH], F32, o)
        dt_, o = place("dt_", [P, 16, CH], F32, o)
        assert o == taken["wl"][1]
        sst, _ = place("sst", [P, NS, H, P], F32, LT)
        PROJ = o
        proj, o = place("proj", [P, 48, T], F32, o)
        oT, o = place("oT", [P, H, T], F32, o)
        rw, o = place("rw", [64, T], F32, o)
        bg, o = place("bg", [P, 2, 64], F32, o)
        cols, o = place("cols", [P, 4, 2, H], F32, o)
        assert o <= 212800, o
        gw, _ = place("gw", [64, 5, T], F32, taken["oT"][0])
        gsq, _ = place("gsq", [P, 4, T], F32, taken["oT"][0])
        lrow, e = place("lrow", [16, T], F32, taken["gw"][1])
        sconv, e = place("sconv", [P, 24, NS], F32, e)
        assert e <= taken["oT"][1]
        osq, _ = place("osq", [P, H, T], F32, PROJ + 16 * T * 4)
        orow, _ = place("orow", [8, T], F32, taken["rw"][0])
        Bh, o = place("Bh", [P, KC, T], F32R, PROJ)
        Bl, o = place("Bl", [P, KC, T], F32R, o)
        mT, o = place("mT", [P, KC, T], F32, o)
        mtmp, _ = place("mtmp", [P, 4, T], F32, taken["oT"][0])
        Hh, o = place("Hh", [P, 32, T], F32R, PROJ)
        xsq, _ = place("xsq", [P, KC, T], F32, PROJ)
        x2n, _ = place("x2n", [P, KC, T], F32, taken["mT"][0])
        rel, o = place("rel", [P, 2, 4, T], F32, o)
        hsq, o = place("hsq", [P, 4, T], F32, o)
        ytok, o = place("ytok", [P, 3, D], F32, o)
        assert o <= 212800, o
        Hl, o = place("Hl", [P, 32, T], F32R, taken["yb"][0])
        assert o <= ATT

        o = ATT
        craw, o = place("craw", [P, 8, LW], F32, o)
        cTh, o = place("cTh", [P, 5, 512], F32R, o)
        cTl, o = place("cTl", [P, 5, 512], F32R, o)
        nath, o = place("nath", [P, 2, 4, 512], F32R, o)
        natl, o = place("natl", [P, 2, 4, 512], F32R, o)
        ksq, o = place("ksq", [P, 2, D], F32, o)
        qst, o = place("qst", [P, 5, P], F32R, o)
        pst, o = place("pst", [P, 2, 4, P], F32R, o)
        kss, o = place("kss", [P, 2, 4, H], F32, o)
        rk, o = place("rk", [P, 2, 4, H], F32, o)
        ssc, o = place("ssc", [P, 2, 4, H], F32, o)
        smax, o = place("smax", [P, 4, H], F32, o)
        pex, o = place("pex", [P, 2, 4, H], F32, o)
        mhalf, o = place("mhalf", [P, 4, H], F32, o)
        ssb, o = place("ssb", [48, 512], F32, o)
        pvs, o = place("pvs", [16, 512], F32, o)
        mall, o = place("mall", [P, NG, H], F32, o)
        lall, o = place("lall", [P, NG, H], F32, o)
        accT, o = place("accT", [P, NG, 4, H], F32, o)
        wall, o = place("wall", [P, NG, H], F32, o)
        mfin, o = place("mfin", [P, 3, NS, H], F32, o)
        lfin, o = place("lfin", [P, 2, NS, H], F32, o)
        gate, o = place("gate", [1, 1], F32, o)
        olat, o = place("olat", [P, NS, 4, H], F32, o)
        onew, o = place("onew", [P, NS, 4, H], F32, o)
        wuvf, o = place("wuvf", [P, 4, D], F32, o)
        assert o <= 212800, o

        ps = ctx.enter_context(nc.psum_tensor("ps", [P, 8, 512], F32))

        win = I["w_in"][0].rearrange("(c p) n -> p c n", p=P)
        wuq = I["w_uq"][0].rearrange("(c p) (h e) -> p c h e", p=P, e=192)
        wuk = I["w_uk"][0].rearrange("(c p) n -> p c n", p=P)
        wuv = I["w_uv"][0].rearrange("(c p) n -> p c n", p=P)

        front = []
        for half in range(2):
            front.append([(slice(0, 4), win[:, 4 * half:4 * half + 4, OFF_KV:OFF_KV + 512])])
        for half in range(2):
            front.append([(slice(0, 4), win[:, 4 * half:4 * half + 4, OFF_QDOWN:OFF_QDOWN + 512])])
        for g in range(2):
            front.append([(slice(0, 4), wuk[:, :, 512 * g:512 * g + 512])])
        for g in range(2):
            front.append([(c, wuq[:, c, 4 * g:4 * g + 4, 0:128]) for c in range(4)])
        front.append([(c, wuq[:, c, :, 128:192]) for c in range(4)])
        for g in range(2):
            front.append([(slice(0, 4), wuv[:, :, 512 * g:512 * g + 512])])
        NF = len(front)
        NP = NF
        NM = NP + 24
        QP = KC + 32
        QM = QP + 48
        wya, wyb, wo, wup, wdn = (I[n][0].rearrange("(c p) n -> p c n", p=P) for n in ("w_ya", "w_yb", "w_o", "w_up", "w_down"))
        UK = 4
        landed = []
        tot = [0] * 4
        for n, parts in enumerate(front):
            tot[n % 4] += 16 * len(parts)
            landed.append(tot[n % 4])
        landed_end = list(tot)

        def landed_later(ns, r):
            return landed_end[ns % 4] + 16 * ((ns - NF) // 4 + 1) + 16 * r

        def hi_of(n):
            return ukh[:, :, (n - UK) * 512:(n - UK + 1) * 512] if n in (UK, UK + 1) else wh[:, n % 2]

        def lo_of(n):
            return ukl[:, :, (n - UK) * 512:(n - UK + 1) * 512] if n in (UK, UK + 1) else wl[:, n % 2]

        trp = ps[:, 4:6, :].rearrange("p b n -> p (b n)")[:, 0:640].rearrange("p (c n) -> p c n", c=5)
        stp = ps[:, 6, 0:64].rearrange("p (t n) -> p t n", t=4)
        pvt = ps[:, 7, 0:32]

        def n_par(u):
            return u % 2

        def kps(u):
            return ps[:, 2 * (u % 2):2 * (u % 2) + 2, :]

        def b_bank(k):
            return ps[:, 4 + k % 4] if k < 12 else ps[:, k % 4]

        SPREAD = [SIDE_A[4 * k:min(4 * k + 4, SIDE_A.index("l2rows"))] for k in range(5)]

        def wait(eng, name, value):
            if not isinstance(value, int) or value > 0:
                eng.wait_ge(S(name), value)

        block = ctx.enter_context(nc.Block())

        @block.sync
        def _(sp):
            sp.dma_start(xtok[:, 0:2, :], I["x_prompt"][0].rearrange("(t p) n -> p t n", p=P)).then_inc(S("x_landed"), 16)
            sp.dma_start(xtok[0:NS, 2, :], I["x_sample"].rearrange("b s n -> (b s) n")).then_inc(S("x_landed"), 16)
            rows = [(PR_MIX, 8, I["norm_mix"].rearrange("l (c p) -> (l c) p", p=P)),
                    (PR_QA, 4, I["q_a_norm"].rearrange("l (c p) -> (l c) p", p=P)),
                    (PR_KVA, 4, I["kv_a_norm"].rearrange("l (c p) -> (l c) p", p=P)),
                    (PR_MLP, 8, I["norm_mlp"].rearrange("l (c p) -> (l c) p", p=P)),
                    (PR_GDN, 1, I["gdn_norm"]), (PR_QN, 1, I["q_norm_nope"]), (PR_KN, 1, I["k_norm_nope"])]
            for r, n, src in rows:
                sp.dma_start(prow[r:r + n, :], src).then_inc(S("params_landed"), 16)
            for n, parts in enumerate(front):
                if n >= 4:
                    sp.wait_ge(S("w_hi"), n - 3)
                    sp.wait_ge(S("w_lo"), n - 3)
                for at, src in parts:
                    dst = wraw[:, n % 4, at]
                    if isinstance(at, int):
                        dst = dst.rearrange("p (h e) -> p h e", h=src.shape[1])
                    sp.dma_start(dst, src).then_inc(S(f"w_landed{n % 4}"), 16)
            sp.wait_ge(S("qr_ready"), 1)
            sp.dma_start(qr64[64:128, :, :], qr[0:64, :, TP:T]).then_inc(S("qr64_landed"), 16)
            for w, val in FRONT_DONE + [("ptab_landed", 16)]:
                sp.wait_ge(S(w), val)

            def page(u, n):
                pg = sp.value_load(ptab[0:1, bass.ds(n, 1)] if not isinstance(n, int) else ptab[0:1, n:n + 1], min_val=0, max_val=I["cache_mla"].shape[1] - 1)
                sp.dma_start(craw[:, u, :], I["cache_mla"][0][bass.ds(pg, 1), :, :].rearrange("o p n -> p (o n)")).then_inc(S(f"page_landed{u}"), 16)

            for u in range(8):
                page(u, u)
            sp.dma_start(wuvf[:], wuv).then_inc(S("wuvf_landed"), 16)
            with sp.Fori(0, NT // 8 - 1) as i:
                for u in range(8):
                    sp.wait_ge(S("tr_done"), 8 * i + u + 1)
                    sp.wait_ge(S("nat_hi"), 8 * i + u + 1)
                    sp.wait_ge(S("nat_lo"), 8 * i + u + 1)
                    page(u, 8 * i + (u + 8))
            sp.wait_ge(S("k_done"), NT)
            sp.wait_ge(S("qk_done"), NG)
            sp.wait_ge(S("nat_hi"), NT)
            sp.wait_ge(S("nat_lo"), NT)
            sp.dma_start(scrow[:], I["state_conv"][0].rearrange("b w n -> (b w) n")).then_inc(S("scrow_landed"), 16)

            def load(ns, r, src):
                sp.wait_ge(S("w_hi"), ns - 3 + 4 * r)
                sp.wait_ge(S("w_lo"), ns - 3 + 4 * r)
                sp.dma_start(wraw[:, ns % 4], src).then_inc(S(f"w_landed{ns % 4}"), 16)

            def load_body(ns, r, w, col):
                for u in range(4):
                    load(ns + u, r, w[:, 4 * (u % 2):4 * (u % 2) + 4, bass.ds(col + 512 * (u // 2), 512)])

            sp.dma_start(O["conv_sample"][0, :, 0:CONVW - 2, :], I["state_conv"][0, :, 1:CONVW - 1, :]).then_inc(S("conv_out"), 16)
            with sp.Fori(0, 4) as i:
                load_body(NP, i, win, 1024 * i)
            for i in range(2):
                load_body(NP, 4 + i, win, OFF_GATES + 1024 * i)
            sp.wait_ge(S("inverse_done"), 1)
            for b in range(NS):
                sp.dma_start(sst[:, b], I["state_gdn"][0, b].rearrange("h k v -> k h v")).then_inc(S("sst_landed"), 16)
            sp.wait_ge(S("a_read"), a_count("s1_1"))
            sp.dma_start(O["gdn_prompt"][0, 0].rearrange("h k v -> k h v"), st[:]).then_inc(S("gdn_out"), 16)
            load_body(NM, 0, wyb, 0)
            for b in range(NS):
                sp.wait_ge(S("a_read"), a_count(f"out{b}_1"))
                sp.dma_start(O["gdn_sample"][0, b].rearrange("h k v -> k h v"), sst[:, b]).then_inc(S("gdn_out"), 16)
            load_body(NM, 1, wya, 0)
            load_body(NM, 2, wo, 0)
            with sp.Fori(0, 4) as i:
                load_body(NM, 3 + i, wup, 1024 * i)
            for g in range(2):
                for u in range(8):
                    load(NM + u % 4, 7 + 2 * g + u // 4, wdn[:, 4 * u:4 * u + 4, 512 * g:512 * g + 512])
            sp.wait_ge(S("a_read"), len(SIDE_A))
            sp.dma_start(O["y_prompt"][0].rearrange("(t p) n -> p t n", p=P), ytok[:, 0:2, :]).then_inc(S("y_out"), 16)
            sp.dma_start(O["y_sample"].rearrange("b s n -> (b s) n"), ytok[0:NS, 2, :]).then_inc(S("y_out"), 16)
            sp.wait_ge(S("y_out"), 32)
            sp.wait_ge(S("conv_out"), 48)
            sp.wait_ge(S("rows_out"), 32)
            sp.wait_ge(S("ab_landed"), 32)

        @block.gpsimd
        def _(g):
            nc.gpsimd.memset(wmisc[:], 0.0).then_inc(S("wmisc_clear"), 1)
            nc.gpsimd.memset(qeff[0:64, :, 4, :], 0.0).then_inc(S("qeff_clear"), 1)
            g.wait_ge(S("chunk_done"), 4 * NF)
            for c in range(4):
                i = nc.gpsimd.tensor_tensor(ukf[:, c, :], ukh[:, c, :].bitcast(F32), ukl[:, c, :].bitcast(F32), ALU.add)
            i.then_inc(S("ukf_ready"), 1)
            g.wait_ge(S("side_read"), len(SIDE))
            g.dma_start(O["rows_prompt"][0, 0].rearrange("(t p) n -> p t n", p=P), ltok[:, 0:2, :]).then_inc(S("rows_out"), 16)
            g.dma_start(O["rows_sample"][0, :, 0, :], ltok[0:NS, 2, :]).then_inc(S("rows_out"), 16)
            for w, val in FRONT_DONE:
                g.wait_ge(S(w), val)
            nc.gpsimd.memset(qst[:].bitcast(F32), 0.0).then_inc(S("att_clear"), 1)
            nc.gpsimd.memset(pst[:].bitcast(F32), 0.0).then_inc(S("att_clear"), 1)
            nc.gpsimd.memset(mhalf[:], -0.5).then_inc(S("att_clear"), 1)
            g.wait_ge(S("att_clear"), 3)

            def group(gg, y):
                g.wait_ge(S("ms_ready"), gg + 1)
                nc.gpsimd.tensor_tensor(rk[:, y], kss[:, y], mhalf[:], ALU.pow).then_inc(S("rk_ready"), 1)
                g.wait_ge(S("s_ready"), gg + 1)
                nc.gpsimd.tensor_tensor(gate[:], mhalf[0:1, 0, 0:1], mhalf[0:1, 0, 0:1], ALU.add)
                nc.gpsimd.partition_all_reduce(smax[:].rearrange("p t h -> p (t h)"), ssc[:, y].rearrange("p t h -> p (t h)"), P, RMAX).then_inc(S("smax_ready"), 1)

            with g.Fori(0, NG // 2) as i:
                for y in range(2):
                    group(2 * i + y, y)
            g.wait_ge(S("yb_ready"), 1)
            nc.gpsimd.memset(rw[:], 0.0).then_inc(S("rw_clear"), 1)
            def low_part(ns, r):
                g.wait_ge(S("w_hi"), ns + 1 + 4 * r)
                nc.gpsimd.tensor_tensor(wl[:, ns % 2], wraw[:, ns % 4], wh[:, ns % 2].bitcast(F32), ALU.subtract).then_inc(S("w_lo"), 1)

            g.wait_ge(S("w_lo"), NP + 12)
            for k in range(12):
                low_part(NP + k % 4, 3 + k // 4)
            g.wait_ge(S("a_read"), a_count("urow"))
            for b in range(NS):
                if b >= 2:
                    g.wait_ge(S("a_done"), a_count(f"out{b - 2}_1"))
                nc.gpsimd.tensor_tensor(umask[b % 2][:], urow[:, 1, :].unsqueeze(1).to_broadcast([64, H, P]),
                                        consts[0:64, C_ID.start + 8 * b:C_ID.start + 8 * b + 8].unsqueeze(2).to_broadcast([64, H, P]), ALU.mult).then_inc(S("umask_ready"), 1)
            nc.gpsimd.tensor_copy(Bh[:], yb[:]).then_inc(S("yb_hi"), 1)
            g.wait_ge(S("yb_hi"), 1)
            nc.gpsimd.tensor_tensor(Bl[:], yb[:], Bh[:].bitcast(F32), ALU.subtract).then_inc(S("yb_split"), 1)
            for k in range(4):
                low_part(NM + k, 0)

        @block.scalar
        def _(act):
            act.dma_start(consts[:, 0:C_COS.start], C_in[:, 0:C_COS.start]).then_inc(S("consts_landed"), 16)
            rows = [(PR_CONV, 96, I["conv_w"][0].rearrange("w (c p) -> (w c) p", p=P))]
            for r, n, src in rows:
                act.dma_start(prow[r:r + n, :], src).then_inc(S("params_landed"), 16)
            for r, name in ((PR_QR, "q_norm_rope"), (PR_KR, "k_norm_rope")):
                for half in range(2):
                    act.dma_start(prow[r:r + 1, 64 * half:64 * half + 64], I[name]).then_inc(S("params_landed"), 16)
            act.wait_ge(S("wmisc_clear"), 1)
            for c0, src in ((0, win[:, :, OFF_ROPE:OFF_ROPE + 64]), (64, win[:, :, OFF_ROPE:OFF_ROPE + 64]),
                            (128, win[:, :, OFF_BETA:OFF_BETA + 8]), (160, win[:, :, OFF_BETA + 8:OFF_BETA + 16])):
                act.dma_start(wmisc[:, :, c0:c0 + src.shape[2]], src).then_inc(S("wmisc_landed"), 16)
            act.dma_start(consts[:, C_COS.start:], C_in[:, C_COS.start:]).then_inc(S("tables_landed"), 16)
            act.dma_start(ab[32:40, 0:1], I["a_log"].rearrange("l h -> h l")).then_inc(S("ab_landed"), 16)
            act.dma_start(ab[32:40, 1:2], I["dt_bias"].rearrange("l h -> h l")).then_inc(S("ab_landed"), 16)
            act.dma_start(ptab[:], I["page_table"].rearrange("b g -> (b g)").rearrange("(o n) -> o n", o=1)).then_inc(S("ptab_landed"), 16)

            def hi(n):
                act.wait_ge(S(f"w_landed{n % 4}"), landed[n])
                before = {0: 0, 1: 0, UK: 1, UK + 1: 1, UK + 2: UK - 1, UK + 3: UK}.get(n, n - 1)
                if before:
                    act.wait_ge(S("chunk_done"), 4 * before)
                nc.scalar.activation(hi_of(n), wraw[:, n % 4], ACT.Copy).then_inc(S("w_hi"), 1)

            def square(out, src, sem):
                nc.scalar.activation(out, src, ACT.Square).then_inc(S(sem), 1)

            def sqrt(rows_, w):
                act.wait_ge(S("side_read"), w)
                nc.scalar.activation(rsq[0:rows_, 1], rsq[0:rows_, 0], ACT.Sqrt).then_inc(S("sqrt_done"), 1)

            act.wait_ge(S("acc_read"), KC)
            square(sq[:, 0:8, :], xT[:], "sq_ready")
            hi(0)
            sqrt(P, side("x_sum"))
            hi(1)
            hi(2)
            act.wait_ge(S("acc_read"), KC + 4)
            act.wait_ge(S("side_done"), side("x_sum"))
            square(sq[:, 0:4, :], kv[:], "sq_ready")
            hi(3)
            act.wait_ge(S("side_read"), side("decay_raw"))
            square(sq[:, 8, :], krT[:], "sq_ready")
            hi(4)
            hi(5)
            sqrt(P, side("kv_sum"))
            hi(6)
            act.wait_ge(S("acc_read"), KC + 8)
            square(sq[:, 4:8, :], qd[:], "sq_ready")
            sqrt(P, side("kr_sum"))
            hi(7)
            sqrt(P, side("qd_sum"))
            act.wait_ge(S("acc_read"), KC + 16)
            act.wait_ge(S("side_done"), side("qd_sum"))
            square(sq[:, 0:8, :], kn[:], "sq_ready")
            hi(8)
            hi(9)
            act.wait_ge(S("acc_read"), KC + 24)
            act.wait_ge(S("nope_used"), 1)
            square(sq[:, 0:8, :], qn[:], "sq_ready")
            hi(10)
            act.wait_ge(S("acc_read"), KC + 28)
            act.wait_ge(S("side_done"), side("nope_rows"))
            square(sq[:, 0:4, :], qr[:], "sq_ready")
            sqrt(16, side("nope_rows"))
            sqrt(8, side("rope_rows"))

            def turned_out(h):
                act.wait_ge(S("pt_done"), h + 1)
                if h >= 2:
                    act.wait_ge(S("pv_done"), h - 1)
                nc.scalar.activation(pT[:, h % 2, :], ps[:, 2, 0:384], ACT.Copy).then_inc(S("pt_read"), 1)

            for h in range(H):
                act.wait_ge(S("max_ready"), h + 1)
                if h >= 3:
                    act.wait_ge(S("pt_done"), h - 2)
                nc.scalar.activation(pr[:, h % 3, 0:128], sc[:, h % 2, 0:128], ACT.Exp, bias=mx[:, h, 0:1], accum_out=ls[:, h, 0:1])
                nc.scalar.activation(pr[:, h % 3, 128:384], sc[:, h % 2, 128:384], ACT.Exp, bias=mx[:, h, 1:2], accum_out=ls[:, h, 1:2]).then_inc(S("exp_done"), 1)
                if h >= 2:
                    turned_out(h - 2)
            turned_out(H - 2)
            turned_out(H - 1)

            for w, val in FRONT_DONE:
                act.wait_ge(S(w), val)

            def split_hi(i, u):
                n = 8 * i + u
                act.wait_ge(S("tr_done"), n + 1)
                nc.scalar.activation(cTh[:, :, 128 * (u % 4):128 * (u % 4) + 128], trp, ACT.Copy).then_inc(S("ct_hi"), 1)
                act.wait_ge(S(f"page_landed{u}"), 16 * i + 16)
                if u % 4 == 0:
                    wait(act, "pv_used", 2 * i + u // 4 - 1)
                nc.scalar.activation(nath[:, u // 4, u % 4, :], craw[:, u, 0:LAT], ACT.Copy).then_inc(S("nat_hi"), 1)

            def body_act(i, first, last):
                for u in range(8):
                    n, y, t = 8 * i + u, u // 4, u % 4
                    prev = not (first and y == 0)
                    if u < 7:
                        split_hi(i, u + 1)
                    elif not last:
                        split_hi(i + 1, 0)
                    if t == 1 and prev:
                        act.wait_ge(S("sub_ready"), 2 * i + y)
                        nc.scalar.activation(pex[:, 1 - y], ssc[:, 1 - y], ACT.Exp).then_inc(S("pex_ready"), 1)
                    if t == 3:
                        act.wait_ge(S("qk_done"), 2 * i + y + 1)
                        nc.scalar.activation(ssb[:], ps[0:48, 6, :], ACT.Copy).then_inc(S("ssb_ready"), 1)
                    act.wait_ge(S("k_done"), n + 1)
                    wait(act, "kss_done", n - 1)
                    nc.scalar.activation(ksq[:, n_par(u)], kps(u), ACT.Square).then_inc(S("ksq_ready"), 1)
                    if t == 2 and prev:
                        act.wait_ge(S("pv_used"), 2 * i + y)
                        wait(act, "pvt_done", 2 * i + y - 1)
                        nc.scalar.activation(pvs[:], ps[0:16, 7, :], ACT.Copy).then_inc(S("pvs_ready"), 1)

            split_hi(0, 0)
            body_act(0, True, False)
            with act.Fori(1, NG // 2 - 1) as i:
                body_act(i, False, False)
            body_act(NG // 2 - 1, False, True)
            act.wait_ge(S("sub_ready"), NG)
            nc.scalar.activation(pex[:, 1], ssc[:, 1], ACT.Exp).then_inc(S("pex_ready"), 1)
            act.wait_ge(S("pv_used"), NG)
            nc.scalar.activation(pvs[:], ps[0:16, 7, :], ACT.Copy).then_inc(S("pvs_ready"), 1)
            act.wait_ge(S("mfin_ready"), 1)
            nc.scalar.activation(wall[:], wall[:], ACT.Exp).then_inc(S("wall_ready"), 1)
            nc.scalar.activation(mfin[:, 2], mfin[:, 1], ACT.Exp).then_inc(S("wall_ready"), 1)

            def hi_at(ns, r):
                act.wait_ge(S(f"w_landed{ns % 4}"), landed_later(ns, r))
                act.wait_ge(S("chunk_done"), 4 * (ns - 1) + 16 * r)
                nc.scalar.activation(wh[:, ns % 2], wraw[:, ns % 4], ACT.Copy).then_inc(S("w_hi"), 1)

            def copy_b(name, dst, src):
                k = SIDE_B.index(name)
                act.wait_ge(S("b_done"), k + 1)
                nc.scalar.activation(dst, src(b_bank(k)), ACT.Copy).then_inc(S("b_read"), 1)

            act.wait_ge(S("pv_used"), NG)
            hi_at(NP, 0)
            hi_at(NP + 1, 0)
            act.wait_ge(S("ab_landed"), 32)
            nc.scalar.activation(ab[32:40, 2:3], ab[32:40, 0:1], ACT.Exp).then_inc(S("ea_ready"), 1)
            act.wait_ge(S("nabs_ready"), 1)
            nc.scalar.activation(gw[32:40, 3], gw[32:40, 2], ACT.Exp).then_inc(S("ea_ready"), 1)
            act.wait_ge(S("ea_ready"), 2)
            nc.scalar.activation(gw[32:40, 4], gw[32:40, 3], ACT.Ln, bias=1.0).then_inc(S("ln_ready"), 1)
            act.wait_ge(S("rw_clear"), 1)
            nc.scalar.activation(rw[0:8, :], decay_raw[0:8, :], ACT.Sigmoid).then_inc(S("beta_ready"), 1)
            with act.Fori(0, 2) as i:
                for u in range(4):
                    hi_at(NP + (u + 2) % 4, i + (u + 2) // 4)
            hi_at(NP + 2, 2)
            hi_at(NP + 3, 2)

            def silu(c):
                act.wait_ge(S("conv_done"), c + 1)
                nc.scalar.activation(proj[:, c, 0:TP], ysc[:, c % 4, 0:TP], ACT.Silu).then_inc(S("silu_done"), 1)

            hi_at(NP, 3)
            for k in range(12):
                if k < 11:
                    hi_at(NP + (k + 1) % 4, 3 + (k + 1) // 4)
                if k < 2:
                    for g in range(3 * k, 3 * k + 3):
                        copy_b(f"rw{g}", crow[:, 512 * g:512 * g + 512], lambda b: b[0:11])
                elif k < 4:
                    for g in range(3 * k - 6, 3 * k - 3):
                        copy_b(f"cs{g}", csT[:, 4 * g:4 * g + 4, :].rearrange("p c n -> p (c n)"), lambda b: b[:, 0:96])
                if k == 2:
                    act.wait_ge(S("b_read"), b_count("rw5"))
                    act.dma_start(O["conv_prompt"][0, 0], crow[0:3, :]).then_inc(S("conv_out"), 16)
                    act.dma_start(O["conv_sample"][0, :, CONVW - 2, :], crow[3:11, :]).then_inc(S("conv_out"), 16)
                    silu(0)
                    silu(1)
                if k >= 2:
                    silu(2 * k - 2)
                    silu(2 * k - 1)
                if k == 5:
                    act.wait_ge(S("sconv_done"), 1)
                    nc.scalar.activation(proj[:, 0:24, TP:T], proj[:, 0:24, TP:T], ACT.Silu).then_inc(S("qkv_ready"), 1)
                if k >= 8:
                    if k == 8:
                        act.wait_ge(S("silu_done"), 16)
                        act.wait_ge(S("qkv_ready"), 1)
                        act.wait_ge(S("g_ready"), 1)
                    for c in range(4 * (k - 8), 4 * (k - 8) + 4):
                        if c >= 4:
                            act.wait_ge(S("l2_used"), c - 3)
                        nc.scalar.activation(gsq[:, c % 4], proj[:, c, :], ACT.Square).then_inc(S("gsq_ready"), 1)
            silu(22)
            silu(23)
            act.wait_ge(S("a_read"), a_count("l2rows"))
            nc.scalar.activation(rsq[0:16, 1], rsq[0:16, 0], ACT.Sqrt).then_inc(S("sqrt_done"), 1)
            act.wait_ge(S("gr_ready"), 1)
            nc.scalar.activation(eg[:], gr[:], ACT.Exp).then_inc(S("eg_ready"), 1)
            act.wait_ge(S("kdiff_ready"), 1)
            nc.scalar.activation(cols[:, 0:2], cols[:, 0:2], ACT.Exp).then_inc(S("cols_ready"), 1)
            act.wait_ge(S("dt_ready"), 1)
            nc.scalar.activation(dt_[:], dt_[:], ACT.Exp).then_inc(S("dt_exp"), 1)
            for g in range(4):
                copy_b(f"vt{g}", vt[:, 4 * g:4 * g + 4, :].rearrange("p u n -> p (u n)"), lambda b: b)
            nc.scalar.activation(proj[:, 24:32, :], proj[:, 24:32, :], ACT.Silu).then_inc(S("z_ready"), 1)
            nc.scalar.activation(proj[:, 32:48, :], proj[:, 32:48, :], ACT.Sigmoid).then_inc(S("gates_ready"), 1)
            act.wait_ge(S("oT_ready"), 3)
            nc.scalar.activation(osq[:], oT[:], ACT.Square).then_inc(S("osq_ready"), 1)
            act.wait_ge(S("a_read"), a_count("orows"))
            nc.scalar.activation(rsq[0:8, 1], rsq[0:8, 0], ACT.Sqrt).then_inc(S("sqrt_done"), 1)

            act.wait_ge(S("gdn_out"), 16 * (1 + NS))
            for u in range(2):
                hi_at(NM + u, 0)

            def body_hi(r):
                for u in range(4):
                    hi_at(NM + (u + 2) % 4, r + (u + 2) // 4)

            body_hi(0)
            body_hi(1)
            body_hi(2)
            act.wait_ge(S("acc_read"), QM + 24)
            nc.scalar.activation(xsq[:], xT[:], ACT.Square).then_inc(S("xsq_ready"), 1)
            act.wait_ge(S("a_read"), a_count("x2_sum"))
            nc.scalar.activation(rsq[:, 1], rsq[:, 0], ACT.Sqrt).then_inc(S("sqrt_done"), 1)

            def relu_group(g, i):
                for j in range(4):
                    act.wait_ge(S("chunk_done"), 4 * (NM + 12 + 2 * g + 1) + j + 1 + 16 * i)
                    if j == 0:
                        act.wait_ge(S("h_split"), 2 * i + g + 1)
                    nc.scalar.activation(rel[:, g, j, :], ps[:, j, 0:T], ACT.Relu).then_inc(S("acc_read"), 1)

            with act.Fori(0, 4) as i:
                for g in range(2):
                    hi_at(NM + 2 * g + (2 if g == 0 else -2), (3 if g == 0 else 4) + i)
                    relu_group(g, i)
                    hi_at(NM + 2 * g + (3 if g == 0 else -1), (3 if g == 0 else 4) + i)
            for n in range(2, 16):
                hi_at(NM + n % 4, 7 + n // 4)

        @block.vector
        def _(v):
            V = nc.vector
            links = [0]

            def link(ins):
                links[0] += 1
                ins.then_inc(S("dve_link"), 1)
                v.wait_ge(S("dve_link"), links[0])

            def lo(n):
                v.wait_ge(S("w_hi"), n + 1)
                V.tensor_tensor(lo_of(n), wraw[:, n % 4], hi_of(n).bitcast(F32), ALU.subtract).then_inc(S("w_lo"), 1)

            def acc(n, j, q, dst, norm=None):
                v.wait_ge(S("chunk_done"), 4 * n + j + 1)
                if norm is None:
                    V.tensor_copy(dst, ps[:, q % 4, 0:dst.shape[-1]]).then_inc(S("acc_read"), 1)
                else:
                    V.tensor_tensor(dst, ps[:, q % 4, 0:dst.shape[-1]], norm, ALU.mult).then_inc(S("acc_read"), 1)

            def rsqrt(name, rows_, dst, inv, k, scale=1.0, sem=None):
                b = 4 + (side(name) - 1) % 4
                v.wait_ge(S("side_done"), side(name))
                r = rsq[0:rows_]
                V.tensor_scalar(r[:, 0], ps[0:rows_, b, 0:T], inv, EPS, ALU.mult, ALU.add).then_inc(S("side_read"), 1)
                v.wait_ge(S("sqrt_done"), k)
                link(V.reciprocal(r[:, 1], r[:, 1]))
                link(V.tensor_tensor(r[:, 2], r[:, 1], r[:, 1], ALU.mult))
                link(V.tensor_tensor(r[:, 2], r[:, 2], r[:, 0], ALU.mult))
                link(V.tensor_scalar(r[:, 2], r[:, 2], -0.5, 1.5, ALU.mult, ALU.add))
                ins = V.scalar_tensor_tensor(dst, r[:, 1], scale, r[:, 2], ALU.mult, ALU.mult)
                if sem:
                    ins.then_inc(S(sem), 1)
                else:
                    link(ins)

            def split(src, h_, l_, sem, count=1):
                link(V.tensor_copy(h_, src))
                V.tensor_tensor(l_, src, h_.bitcast(F32), ALU.subtract).then_inc(S(sem), count)

            for c in range(KC):
                v.wait_ge(S("xT_done"), c + 1)
                V.tensor_copy(xT[:, c, :], ps[:, c % 4, 0:T]).then_inc(S("acc_read"), 1)
            v.wait_ge(S("side_done"), side("params"))
            V.tensor_copy(par[:, 0:PR_ALL], ps[:, 4, 0:PR_ALL]).then_inc(S("side_read"), 1)
            v.wait_ge(S("side_read"), 1)
            v.wait_ge(S("acc_read"), KC)
            link(V.tensor_tensor(xn[:], xT[:], par[:, PR_MIX:PR_MIX + KC].unsqueeze(2).to_broadcast([P, KC, T]), ALU.mult))
            split(xn[:], Ah[:], Al[:], "a_ready")
            lo(0)
            rsqrt("x_sum", P, rx[:], 1.0 / D, 1)
            lo(1)
            lo(2)
            for j in range(4):
                acc(1, j, KC + j, kv[:, j, :], rx[:])
            lo(3)
            v.wait_ge(S("side_done"), side("rope_raw"))
            V.tensor_tensor(krT[:], ps[:, 4 + (side("rope_raw") - 1) % 4, 0:T], rx[:], ALU.mult).then_inc(S("side_read"), 1)
            v.wait_ge(S("side_done"), side("decay_raw"))
            V.tensor_tensor(decay_raw[:], ps[0:64, 4 + (side("decay_raw") - 1) % 4, 0:T], rx[0:64], ALU.mult).then_inc(S("side_read"), 1)
            lo(4)
            lo(5)
            rsqrt("kv_sum", P, rsq[:, 1], 1.0 / LAT, 2)
            for c in range(4):
                i = V.scalar_tensor_tensor(kv[:, c, :], kv[:, c, :], par[:, PR_KVA + c:PR_KVA + c + 1], rsq[:, 1], ALU.mult, ALU.mult)
            link(i)
            V.tensor_copy(cnew[:], kv[:, :, TP:T])
            split(kv[:], ch[:], cl[:], "c_ready")
            lo(6)
            for j in range(4):
                acc(3, j, KC + 4 + j, qd[:, j, :], rx[:])
            rsqrt("kr_sum", P, rsq[:, 1], 1.0 / ROPE, 3)
            V.scalar_tensor_tensor(krT[:], krT[:], par[:, PR_KR:PR_KR + 1], rsq[:, 1], ALU.mult, ALU.mult).then_inc(S("kr_scaled"), 1)
            for j in range(4):
                acc(4, j, KC + 8 + j, kn[:, j, :])
            v.wait_ge(S("kr_scaled"), 1)
            rsqrt("qd_sum", P, rsq[:, 1], 1.0 / 512, 4)
            for c in range(4):
                i = V.scalar_tensor_tensor(qd[:, c, :], qd[:, c, :], par[:, PR_QA + c:PR_QA + c + 1], rsq[:, 1], ALU.mult, ALU.mult)
            link(i)
            split(qd[:], qdh[:], qdl[:], "qd_ready")
            for j in range(4):
                acc(5, j, KC + 12 + j, kn[:, 4 + j, :])
            lo(7)
            v.wait_ge(S("side_done"), side("kr_rot"))
            v.wait_ge(S("tables_landed"), 16)
            V.tensor_tensor(rsq[:, 0], ps[:, 4 + (side("kr_rot") - 1) % 4, 0:T], consts[:, C_SIN], ALU.mult).then_inc(S("side_read"), 1)
            link(V.tensor_tensor(krT[:], krT[:], consts[:, C_COS], ALU.mult))
            v.wait_ge(S("side_read"), side("kr_rot"))
            V.tensor_tensor(krT[:], krT[:], rsq[:, 0], ALU.add).then_inc(S("kr_ready"), 1)
            for j in range(4):
                acc(6, j, KC + 16 + j, qn[:, j, :])
            lo(8)
            for j in range(4):
                acc(7, j, KC + 20 + j, qn[:, 4 + j, :])
            lo(9)
            for j in range(4):
                acc(8, j, KC + 24 + j, qr[:, j, :])
            lo(10)
            for j in range(2):
                acc(9, 2 * j + 1, KC + 28 + j, vtok[:, j, 0:512])
            v.wait_ge(S("kr_ready"), 1)
            rsqrt("nope_rows", 16, nrow[:], 1.0 / 128, 5, consts[0:16, C_RSC], "nope_rstd")
            for j in range(2):
                acc(10, 2 * j + 1, KC + 30 + j, vtok[:, j, 512:1024])
            v.wait_ge(S("nope_rstd"), 1)
            rsqrt("rope_rows", 8, rrow[:], 1.0 / 64, 6, SCALE, "rope_rstd")
            for h in range(16):
                t = (qn if h < 8 else kn)[:, h % 8, :]
                g = PR_QN if h < 8 else PR_KN
                v.wait_ge(S("side_done"), side(f"nope{h}"))
                V.scalar_tensor_tensor(t, t, par[:, g:g + 1], ps[:, 4 + (side(f"nope{h}") - 1) % 4, 0:T], ALU.mult, ALU.mult).then_inc(S("side_read"), 1)
            for n, p in enumerate(range(4)):
                v.wait_ge(S("side_done"), side(f"rope{p}"))
                V.scalar_tensor_tensor(qr[:, p, :], qr[:, p, :], par[:, PR_QR:PR_QR + 1], ps[:, 4 + (side(f"rope{p}") - 1) % 4, 0:T], ALU.mult, ALU.mult).then_inc(S("side_read"), 1)
            for p in range(4):
                v.wait_ge(S("side_done"), side(f"rot{p}"))
                v.wait_ge(S("side_read"), side(f"rot{p}") - 1)
                V.tensor_tensor(rsq[:, p % 3], ps[:, 4 + (side(f"rot{p}") - 1) % 4, 0:T], consts[:, C_SIN], ALU.mult).then_inc(S("side_read"), 1)
                link(V.tensor_tensor(qr[:, p, :], qr[:, p, :], consts[:, C_COS], ALU.mult))
                v.wait_ge(S("side_read"), side(f"rot{p}"))
                i = V.tensor_tensor(qr[:, p, :], qr[:, p, :], rsq[:, p % 3], ALU.add)
                if p < 3:
                    link(i)
            i.then_inc(S("qr_ready"), 1)
            V.tensor_scalar(qg[:], qn[:, :, TP:T], par[:, PR_KN:PR_KN + 1], None, ALU.mult).then_inc(S("qg_ready"), 1)
            V.tensor_tensor(qk[:, 0], qn[:, :, TP:T], kn[:, :, TP:T], ALU.mult)
            v.wait_ge(S("qr_ready"), 1)
            V.memset(qk[:, 1], 0.0).then_inc(S("qk_clear"), 1)
            v.wait_ge(S("qk_clear"), 1)
            for b in range(2):
                r = slice(64 * b, 64 * b + 64)
                i = V.tensor_tensor(qk[r, 1].rearrange("p (a b) s -> p a b s", b=2)[:, :, b, :], qr[r, :, TP:T],
                                krT[r, TP:T].unsqueeze(1).to_broadcast([64, 4, NS]), ALU.mult)
            i.then_inc(S("qk_ready"), 1)

            def probs(h):
                v.wait_ge(S("exp_done"), h + 1)
                link(V.reciprocal(ls[:, h, :], ls[:, h, :]))
                V.tensor_scalar(pr[:, h % 3, 0:128], pr[:, h % 3, 0:128], ls[:, h, 0:1], None, ALU.mult)
                V.tensor_scalar(pr[:, h % 3, 128:384], pr[:, h % 3, 128:384], ls[:, h, 1:2], None, ALU.mult).then_inc(S("p_ready"), 1)

            def out_head(h):
                v.wait_ge(S("pv_done"), h + 1)
                V.tensor_copy(yb[:, h, 0:TP], ps[:, 3, 0:TP]).then_inc(S("yb_read"), 1)

            for h in range(H):
                v.wait_ge(S("sc_done"), h + 1)
                if h >= 2:
                    v.wait_ge(S("exp_done"), h - 1)
                V.tensor_tensor(sc[:, h % 2, :], ps[:, h % 2, 0:384], consts[:, C_NEG], ALU.add).then_inc(S("sc_read"), 1)
                v.wait_ge(S("sc_read"), h + 1)
                V.reduce_max(mx[:, h, 0:1], sc[:, h % 2, 0:128], AX)
                link(V.reduce_max(mx[:, h, 1:2], sc[:, h % 2, 128:384], AX))
                V.tensor_scalar(mx[:, h, :], mx[:, h, :], -1.0, None, ALU.mult).then_inc(S("max_ready"), 1)
                if h >= 1:
                    probs(h - 1)
                if h >= 3:
                    out_head(h - 3)
                if h < 6:
                    t = h // 2
                    rows_, c0, n_ = P if t < 2 else NS, 512 * (h % 2), 512 if h % 2 == 0 else ROPE
                    v.wait_ge(S("side_done"), side(f"row{h}"))
                    V.tensor_copy(ltok[0:rows_, t, c0:c0 + n_], ps[0:rows_, 4 + (side(f"row{h}") - 1) % 4, 0:n_]).then_inc(S("side_read"), 1)
            probs(H - 1)
            out_head(H - 3)
            out_head(H - 2)
            out_head(H - 1)

            for h in range(H):
                v.wait_ge(S("ukT_done"), h + 1)
                if h >= 2:
                    v.wait_ge(S("qe_done"), h - 1)
                V.tensor_copy(ukT[:, h % 2, :], ps[:, 4 + h % 2, :]).then_inc(S("ukT_read"), 1)
            v.wait_ge(S("qe_done"), H)
            V.tensor_copy(qeff[:, :, 0:4, :], ps[:, 6, 0:256].rearrange("p (c h s) -> p s c h", c=4, h=H)).then_inc(S("qeff_ready"), 1)
            qx = qeff[:, :, 4, :].rearrange("p s (a b) -> p a b s", b=2)
            V.tensor_copy(qx[64:128, :, 1, :], qr[64:128, :, TP:T]).then_inc(S("qeff_ready"), 1)
            v.wait_ge(S("qr64_landed"), 16)
            V.tensor_copy(qx[64:128, :, 0, :], qr64[64:128]).then_inc(S("qeff_ready"), 1)
            v.wait_ge(S("qk_sum"), 1)
            V.tensor_copy(snew[:], ps[:, 7, 0:64]).then_inc(S("snew_ready"), 1)

            v.wait_ge(S("att_clear"), 3)

            def split_lo(i, u):
                n = 8 * i + u
                v.wait_ge(S("ct_hi"), n + 1)
                tok = slice(128 * (u % 4), 128 * (u % 4) + 128)
                V.tensor_tensor(cTl[:, :, tok], trp, cTh[:, :, tok].bitcast(F32), ALU.subtract).then_inc(S("ct_lo"), 1)
                v.wait_ge(S("nat_hi"), n + 1)
                V.tensor_tensor(natl[:, u // 4, u % 4, :], craw[:, u, 0:LAT], nath[:, u // 4, u % 4, :].bitcast(F32), ALU.subtract).then_inc(S("nat_lo"), 1)

            def queries(i, s):
                wait(v, "qk_done", 2 * i)
                V.tensor_copy(qst[:, 0:4, 0:8], qeff[:, s, 0:4, :].rearrange("p o c h -> p (o c) h"))
                V.tensor_copy(qst[:, 4, 32:40], qeff[:, s, 4, :].rearrange("p o h -> p (o h)")).then_inc(S("qst_hi"), 1)
                v.wait_ge(S("qst_hi"), i + 1)
                V.tensor_tensor(qst[:, 0:4, 8:16], qeff[:, s, 0:4, :].rearrange("p o c h -> p (o c) h"), qst[:, 0:4, 0:8].bitcast(F32), ALU.subtract)
                V.tensor_tensor(qst[:, 4, 40:48], qeff[:, s, 4, :].rearrange("p o h -> p (o h)"), qst[:, 4, 32:40].bitcast(F32), ALU.subtract).then_inc(S("qst_ready"), 1)

            def probabilities(gg, y):
                v.wait_ge(S("pex_ready"), gg + 1)
                V.tensor_copy(pst[:, y, :, 0:8], pex[:, y]).then_inc(S("pst_hi"), 1)
                V.tensor_reduce(lall[:, bass.ds(gg, 1), :].rearrange("p o h -> p (o h)"), pex[:, y].rearrange("p t h -> p h t"), AX, ALU.add)
                v.wait_ge(S("pst_hi"), gg + 1)
                V.tensor_tensor(pst[:, y, :, 8:16], pex[:, y], pst[:, y, :, 0:8].bitcast(F32), ALU.subtract).then_inc(S("pst_ready"), 1)

            def maxima(gg, y):
                v.wait_ge(S("smax_ready"), gg + 1)
                m = mall[:, bass.ds(gg, 1), :].rearrange("p o h -> p (o h)")
                V.tensor_reduce(m, smax[:].rearrange("p t h -> p h t"), AX, ALU.max).then_inc(S("mall_ready"), 1)
                v.wait_ge(S("mall_ready"), gg + 1)
                V.tensor_tensor(ssc[:, y], ssc[:, y], mall[:, bass.ds(gg, 1), :].to_broadcast([P, 4, H]), ALU.subtract).then_inc(S("sub_ready"), 1)

            def scaled(gg, y):
                v.wait_ge(S("rk_ready"), gg + 1)
                v.wait_ge(S("st_done"), gg + 1)
                V.tensor_tensor(ssc[:, y], stp[:, :, 0:8], rk[:, y], ALU.mult).then_inc(S("s_half"), 1)
                v.wait_ge(S("s_half"), gg + 1)
                V.tensor_tensor(ssc[:, y], stp[:, :, 8:16], ssc[:, y], ALU.add).then_inc(S("s_ready"), 1)

            def body_dve(i, s, first, last):
                queries(i, s)
                for u in range(8):
                    n, y, t = 8 * i + u, u // 4, u % 4
                    prev = not (first and y == 0)
                    gp = 2 * i + y - 1
                    if u < 7:
                        split_lo(i, u + 1)
                    elif not last:
                        split_lo(i + 1, 0)
                    if t == 1 and prev:
                        maxima(gp, 1 - y)
                    v.wait_ge(S("ksq_ready"), n + 1)
                    V.tensor_reduce(kss[:, y, t, :], ksq[:, n_par(u)].rearrange("p (h d) -> p h d", h=H), AX, ALU.add).then_inc(S("kss_done"), 1)
                    if t == 0 and prev:
                        scaled(gp, 1 - y)
                    if t == 1 and prev:
                        probabilities(gp, 1 - y)
                    if t == 3:
                        v.wait_ge(S("kss_done"), n + 1)
                        V.tensor_scalar(kss[:, y], kss[:, y], 1.0 / 128, EPS, ALU.mult, ALU.add).then_inc(S("ms_ready"), 1)
                    if t == 3 and prev:
                        latent_sum(gp)

            def latent_sum(gg):
                v.wait_ge(S("pvt_done"), gg + 1)
                V.tensor_copy(accT[:, bass.ds(gg, 1), :, :].rearrange("p o c h -> p (o c h)"), pvt).then_inc(S("accT_ready"), 1)

            split_lo(0, 0)
            body_dve(0, bass.ds(0, 1), True, False)
            with v.Fori(1, NG // 2 - 1) as i:
                body_dve(i, bass.ds(i // 2, 1), False, False)
            body_dve(NG // 2 - 1, bass.ds(NS - 1, 1), False, True)
            scaled(NG - 1, 1)
            maxima(NG - 1, 1)
            probabilities(NG - 1, 1)
            latent_sum(NG - 1)
            v.wait_ge(S("accT_ready"), NG)
            v.wait_ge(S("mall_ready"), NG)

            sn = snew[:].rearrange("p (h s) -> p s h", s=NS)
            link(V.tensor_reduce(mfin[:, 0], mall[:].rearrange("p (s g) h -> p s h g", g=4), AX, ALU.max))
            link(V.tensor_tensor(mfin[:, 0], mfin[:, 0], sn, ALU.max))
            V.tensor_tensor(wall[:].rearrange("p (s g) h -> p s g h", g=4), mall[:].rearrange("p (s g) h -> p s g h", g=4),
                            mfin[:, 0].unsqueeze(2).to_broadcast([P, NS, 4, H]), ALU.subtract)
            V.tensor_tensor(mfin[:, 1], sn, mfin[:, 0], ALU.subtract).then_inc(S("mfin_ready"), 1)
            v.wait_ge(S("wall_ready"), 2)
            link(V.tensor_tensor(lall[:], lall[:], wall[:], ALU.mult))
            V.tensor_reduce(lfin[:, 0], lall[:].rearrange("p (s g) h -> p s h g", g=4), AX, ALU.add).then_inc(S("lpart_ready"), 1)
            link(V.tensor_tensor(accT[:], accT[:], wall[:].unsqueeze(2).to_broadcast([P, NG, 4, H]), ALU.mult))
            V.tensor_reduce(olat[:].rearrange("p s c h -> p s (c h)"), accT[:].rearrange("p (s g) c h -> p s (c h) g", g=4), AX, ALU.add)
            link(V.tensor_tensor(onew[:], cnew[:].rearrange("p c s -> p s c").unsqueeze(3).to_broadcast([P, NS, 4, H]),
                                 mfin[:, 2].unsqueeze(2).to_broadcast([P, NS, 4, H]), ALU.mult))
            link(V.tensor_tensor(olat[:], olat[:], onew[:], ALU.add))
            v.wait_ge(S("lsum_done"), 1)
            link(V.tensor_tensor(lfin[:, 1].rearrange("p s h -> p (s h)"), ps[:, 6, 0:64], mfin[:, 2].rearrange("p s h -> p (s h)"), ALU.add))
            link(V.reciprocal(lfin[:, 1], lfin[:, 1]))
            V.tensor_tensor(olat[:], olat[:], lfin[:, 1].unsqueeze(2).to_broadcast([P, NS, 4, H]), ALU.mult).then_inc(S("olat_ready"), 1)
            def lo_at(ns, r):
                v.wait_ge(S("w_hi"), ns + 1 + 4 * r)
                V.tensor_tensor(wl[:, ns % 2], wraw[:, ns % 4], wh[:, ns % 2].bitcast(F32), ALU.subtract).then_inc(S("w_lo"), 1)

            lo_at(NP, 0)
            lo_at(NP + 1, 0)
            v.wait_ge(S("yb_sample"), 1)
            V.tensor_copy(yb[:, :, TP:T], ps[:, 7, 0:64].rearrange("p (h s) -> p h s", h=H)).then_inc(S("yb_ready"), 1)

            def a_bank(name):
                k = SIDE_A.index(name)
                v.wait_ge(S("a_done"), k + 1)
                return ps[:, 4 + k % 4]

            def group_out(g, i):
                for j in range(4):
                    v.wait_ge(S("chunk_done"), 4 * (NP + 2 * g + 1) + j + 1 + 16 * i)
                    V.tensor_tensor(proj[:, bass.ds(8 * i + 4 * g + j, 1), :].rearrange("p o n -> p (o n)"), ps[:, j, 0:T], rx[:], ALU.mult).then_inc(S("acc_read"), 1)

            r32 = slice(32, 40)
            v.wait_ge(S("ab_landed"), 32)
            link(V.tensor_scalar(gw[r32, 0], decay_raw[r32], ab[r32, 1:2], None, ALU.add))
            link(V.tensor_scalar(gw[r32, 1], gw[r32, 0], -1.0, None, ALU.mult))
            V.tensor_tensor(gw[r32, 2], gw[r32, 0], gw[r32, 1], ALU.min).then_inc(S("nabs_ready"), 1)
            link(V.tensor_scalar(gw[r32, 0], gw[r32, 0], 0.0, None, ALU.max))
            v.wait_ge(S("ln_ready"), 1)
            link(V.tensor_tensor(gw[r32, 0], gw[r32, 0], gw[r32, 4], ALU.add))
            link(V.tensor_scalar(gw[r32, 0], gw[r32, 0], ab[r32, 2:3], -1.0, ALU.mult, ALU.mult))
            v.wait_ge(S("rw_clear"), 1)
            for n in range(2):
                s_ = slice(CH * n, CH * n + CH)
                V.tensor_tensor_scan(rw[r32, s_], consts[r32, C_ONE], gw[r32, 0, s_], 0.0, ALU.mult, ALU.add)
            V.tensor_copy(rw[r32, TP:T], gw[r32, 0, TP:T]).then_inc(S("g_ready"), 1)

            with v.Fori(0, 2) as i:
                lo_at(NP + 2, i)
                group_out(0, i)
                lo_at(NP + 3, i)
                lo_at(NP, i + 1)
                group_out(1, i)
                lo_at(NP + 1, i + 1)
            lo_at(NP + 2, 2)
            group_out(0, 2)
            lo_at(NP + 3, 2)
            group_out(1, 2)

            def conv(c):
                if c >= 4:
                    v.wait_ge(S("silu_done"), c - 3)
                y, x = ysc[:, c % 4], proj[:, c]
                w_ = [par[:, PR_CONV + 24 * k + c:PR_CONV + 24 * k + c + 1] for k in range(CONVW)]
                link(V.tensor_scalar(y[:, 0:TP], x[:, 0:TP], w_[3], None, ALU.mult))
                for back in range(1, CONVW):
                    ins = V.scalar_tensor_tensor(y[:, back:TP], x[:, 0:TP - back], w_[3 - back], y[:, back:TP], ALU.mult, ALU.add)
                    if back < CONVW - 1:
                        link(ins)
                ins.then_inc(S("conv_done"), 1)

            def tap(k):
                return par[:, PR_CONV + 24 * k:PR_CONV + 24 * k + 24].unsqueeze(2).to_broadcast([P, 24, NS])

            def sample_conv():
                v.wait_ge(S("b_read"), b_count("cs5"))
                xs = proj[:, 0:24, TP:T]
                link(V.tensor_tensor(xs, xs, tap(3), ALU.mult))
                for k in range(CONVW - 1):
                    link(V.tensor_tensor(sconv[:], csT[:].rearrange("p c (s w) -> p c s w", w=3)[:, :, :, k], tap(k), ALU.mult))
                    ins = V.tensor_tensor(xs, xs, sconv[:], ALU.add)
                    if k < 2:
                        link(ins)
                ins.then_inc(S("sconv_done"), 1)

            def spread_out(name):
                b_, n = a_bank(name), int(name[2:])
                if name.startswith("bg"):
                    V.tensor_copy(bg[:, n, :], b_[:, 0:64]).then_inc(S("a_read"), 1)
                else:
                    V.tensor_copy((br if name.startswith("br") else gr)[:, n, :], b_[:, 0:T]).then_inc(S("a_read"), 1)

            v.wait_ge(S("acc_read"), QP + 24)
            for k in range(12):
                if 5 <= k < 10:
                    if k == 5:
                        v.wait_ge(S("conv_out"), 48)
                    for name in SPREAD[k - 5]:
                        spread_out(name)
                if k == 4:
                    sample_conv()
                conv(2 * k)
                conv(2 * k + 1)
                if k % 2 == 1:
                    group_out((k % 4) // 2, 3 + k // 4)
            v.wait_ge(S("a_read"), a_count("gr7"))
            V.tensor_copy(cols[:, 0], bg[:, :, 32:40]).then_inc(S("gr_ready"), 1)
            V.tensor_tensor(cols[:, 1], gr[:, :, 0:TP].rearrange("p h (n i) -> p n h i", n=2)[:, :, :, CH - 1], bg[:, :, 32:40], ALU.subtract).then_inc(S("kdiff_ready"), 1)
            for h in range(H):
                for n in range(2):
                    i = V.tensor_scalar(dt_[:, 2 * h + n, :], gr[:, h, CH * n:CH * n + CH], bg[:, n, 32 + h:33 + h], 0.0, ALU.subtract, ALU.min)
            i.then_inc(S("dt_ready"), 1)
            b_ = a_bank("l2rows")
            V.tensor_scalar(rsq[0:16, 0], b_[0:16, 0:T], 1.0, EPS, ALU.mult, ALU.add).then_inc(S("a_read"), 1)

            def newton(rows_, dst, k, scale, sem):
                v.wait_ge(S("sqrt_done"), k)
                r = rsq[0:rows_]
                link(V.reciprocal(r[:, 1], r[:, 1]))
                link(V.tensor_tensor(r[:, 2], r[:, 1], r[:, 1], ALU.mult))
                link(V.tensor_tensor(r[:, 2], r[:, 2], r[:, 0], ALU.mult))
                link(V.tensor_scalar(r[:, 2], r[:, 2], -0.5, 1.5, ALU.mult, ALU.add))
                V.scalar_tensor_tensor(dst, r[:, 1], scale, r[:, 2], ALU.mult, ALU.mult).then_inc(S(sem), 1)

            newton(16, lrow[:], 7, consts[0:16, C_RSG], "lrow_ready")
            for c in range(16):
                b_ = a_bank(f"l2b{c}")
                V.tensor_tensor(proj[:, c, :], proj[:, c, :], b_[:, 0:T], ALU.mult).then_inc(S("a_read"), 1)
            v.wait_ge(S("dt_exp"), 1)
            link(V.tensor_tensor(dt_[:], dt_[:], consts[:, C_INCL].unsqueeze(1).to_broadcast([P, 16, CH]), ALU.mult))
            for g in range(4):
                b_ = a_bank(f"qk{g}")
                us = slice(4 * g, 4 * g + 4)
                V.tensor_tensor(aqT[:, us, :], b_.rearrange("p (u n) -> p u n", u=4), dt_[:, us, :], ALU.mult).then_inc(S("a_read"), 1)
            v.wait_ge(S("a_read"), a_count("qk3"))
            link(V.tensor_tensor(dt_[:], dt_[:], consts[:, C_STRICT].unsqueeze(1).to_broadcast([P, 16, CH]), ALU.mult))
            link(V.tensor_tensor(dt_[:].rearrange("p (h n) i -> p h (n i)", n=2), dt_[:].rearrange("p (h n) i -> p h (n i)", n=2), br[:, :, 0:TP], ALU.mult))
            for g in range(4):
                b_ = a_bank(f"kk{g}")
                us = slice(4 * g, 4 * g + 4)
                V.tensor_tensor(lT[:, us, :], b_.rearrange("p (u n) -> p u n", u=4), dt_[:, us, :], ALU.mult).then_inc(S("a_read"), 1)
            v.wait_ge(S("cols_ready"), 1)
            for g in range(4):
                b_ = a_bank(f"kt{g}")
                for w in range(4):
                    u = 4 * g + w
                    i = V.tensor_scalar(kd[:, u, :], b_[:, CH * w:CH * w + CH], cols[:, 1, u % 2, u // 2:u // 2 + 1], None, ALU.mult)
                i.then_inc(S("a_read"), 1)
            def small(k):
                return sm[:, k].rearrange("p (s h) -> p s h", h=H)

            idb = consts[:, C_ID].unsqueeze(1).to_broadcast([P, 16, CH])
            V.tensor_copy(T_[:], idb)
            V.tensor_copy(U_[:], idb).then_inc(S("tu_ready"), 1)
            for s_ in range(LEVELS):
                mask = consts[:, C_LVL[s_]].unsqueeze(1).to_broadcast([P, 4, CH])
                for g in range(4):
                    us = slice(4 * g, 4 * g + 4)
                    b_ = a_bank(f"x{s_}_{g}")
                    V.tensor_tensor(X_[:, us, :], b_.rearrange("p (u n) -> p u n", u=4), mask, ALU.mult).then_inc(S("a_read"), 1)
                for g in range(4):
                    us = slice(4 * g, 4 * g + 4)
                    if s_ < LEVELS - 1:
                        b_ = a_bank(f"t{s_}_{g}")
                        V.tensor_tensor(T_[:, us, :], T_[:, us, :], b_.rearrange("p (u n) -> p u n", u=4), ALU.subtract).then_inc(S("a_read"), 1)
                    b_ = a_bank(f"u{s_}_{g}")
                    V.tensor_tensor(U_[:, us, :], U_[:, us, :], b_.rearrange("p (u n) -> p u n", u=4), ALU.subtract).then_inc(S("a_read"), 1)
            v.wait_ge(S("a_read"), a_count(f"u{LEVELS - 1}_3"))
            v.wait_ge(S("eg_ready"), 1)
            V.tensor_copy(small(7), br[:, :, TP:T].rearrange("p h s -> p s h"))
            V.tensor_tensor(proj[:, 0:8, 0:TP], proj[:, 0:8, 0:TP], eg[:, :, 0:TP], ALU.mult).then_inc(S("inverse_done"), 1)
            v.wait_ge(S("inverse_done"), 1)

            v.wait_ge(S("b_read"), b_count("vt3"))
            for h in range(H):
                i = V.tensor_scalar(rhs_[:, h, :], vt[:, 2 * h, :], bg[:, 0, h:h + 1], None, ALU.mult)
            i.then_inc(S("rhs_ready"), 1)
            for g in range(2):
                b_ = a_bank(f"uu0_{g}")
                V.tensor_copy(uu[:, 4 * g:4 * g + 4, :].rearrange("p u n -> p (u n)"), b_).then_inc(S("a_read"), 1)
            for g in range(2):
                b_ = a_bank(f"o0_{g}")
                V.tensor_copy(oT[:, 4 * g:4 * g + 4, 0:CH], b_.rearrange("p (u n) -> p u n", u=4)).then_inc(S("a_read"), 1)
            for g in range(2):
                b_ = a_bank(f"s0_{g}")
                V.tensor_copy(st[:, 4 * g:4 * g + 4, :].rearrange("p u n -> p (u n)"), b_).then_inc(S("a_read"), 1)
            for g in range(2):
                b_ = a_bank(f"ks_{g}")
                for w in range(4):
                    h = 4 * g + w
                    i = V.tensor_scalar(rhs_[:, h, :], b_[:, CH * w:CH * w + CH], cols[:, 0, 1, h:h + 1], None, ALU.mult)
                i.then_inc(S("a_read"), 1)
            v.wait_ge(S("a_read"), a_count("ks_1"))
            link(V.tensor_tensor(rhs_[:], vt[:].rearrange("p (h n) i -> p h n i", n=2)[:, :, 1, :], rhs_[:], ALU.subtract))
            for h in range(H):
                i = V.tensor_scalar(rhs_[:, h, :], rhs_[:, h, :], bg[:, 1, h:h + 1], None, ALU.mult)
            i.then_inc(S("rhs_ready"), 1)
            for g in range(2):
                b_ = a_bank(f"uu1_{g}")
                V.tensor_copy(uu[:, 4 * g:4 * g + 4, :].rearrange("p u n -> p (u n)"), b_).then_inc(S("a_read"), 1)
            for g in range(2):
                b_ = a_bank(f"o1_{g}")
                V.tensor_copy(oT[:, 4 * g:4 * g + 4, CH:TP], b_.rearrange("p (u n) -> p u n", u=4)).then_inc(S("a_read"), 1)
            for h in range(H):
                i = V.tensor_scalar(st[:, h, :], st[:, h, :], eg[:, h, TP - 1:TP], None, ALU.mult)
            link(i)
            for g in range(2):
                b_ = a_bank(f"s1_{g}")
                V.tensor_tensor(st[:, 4 * g:4 * g + 4, :], st[:, 4 * g:4 * g + 4, :], b_.rearrange("p (u n) -> p u n", u=4), ALU.add).then_inc(S("a_read"), 1)

            def sample_of(c0):
                return proj[:, c0:c0 + 8, TP:T].rearrange("p h s -> p s h")

            egs = eg[:, :, TP:T].rearrange("p h s -> p s h")
            brs = small(7)
            V.tensor_copy(small(1), sample_of(8)).then_inc(S("ksmall_ready"), 1)
            V.tensor_tensor(small(2), sample_of(0), sample_of(8), ALU.mult).then_inc(S("ksmall_ready"), 1)
            b_ = a_bank("kqs")
            kq = b_[:, 0:128].rearrange("p (s h t) -> p s h t", s=NS, t=2)
            V.tensor_tensor(small(3), kq[:, :, :, 1], egs, ALU.mult)
            V.tensor_tensor(small(4), kq[:, :, :, 0], egs, ALU.mult).then_inc(S("a_read"), 1)
            v.wait_ge(S("a_read"), a_count("kqs"))
            link(V.tensor_tensor(small(3), sample_of(16), small(3), ALU.subtract))
            V.tensor_tensor(small(5), small(3), brs, ALU.mult).then_inc(S("u_ready"), 1)
            b_ = a_bank("qks")
            v.wait_ge(S("u_ready"), 1)
            V.tensor_tensor(small(6), b_[:, 0:64].rearrange("p (s h) -> p s h", h=H), small(5), ALU.mult).then_inc(S("a_read"), 1)
            v.wait_ge(S("a_read"), a_count("qks"))
            V.tensor_tensor(oT[:, :, TP:T].rearrange("p h s -> p s h"), small(6), small(4), ALU.add).then_inc(S("oT_ready"), 3)
            for k, name in enumerate(("krow", "urow")):
                b_ = a_bank(name)
                V.tensor_copy(urow[:, k, :], b_[0:64, 0:128]).then_inc(S("a_read"), 1)
            v.wait_ge(S("a_read"), a_count("urow"))
            v.wait_ge(S("sst_landed"), 16 * NS)
            for b in range(NS):
                for g in range(2):
                    b_ = a_bank(f"out{b}_{g}")
                    for w in range(4):
                        h = 4 * g + w
                        i = V.scalar_tensor_tensor(sst[:, b, h, :], sst[:, b, h, :], eg[:, h, TP + b:TP + b + 1], b_[:, CH * w:CH * w + CH], ALU.mult, ALU.add)
                    i.then_inc(S("a_read"), 1)

            b_ = a_bank("orows")
            V.tensor_scalar(rsq[0:8, 0], b_[0:8, 0:T], 1.0 / P, EPS, ALU.mult, ALU.add).then_inc(S("a_read"), 1)
            newton(8, orow[:], 8, 1.0, "orow_ready")
            v.wait_ge(S("z_ready"), 1)
            for h in range(H):
                b_ = a_bank(f"ob{h}")
                link(V.scalar_tensor_tensor(oT[:, h, :], oT[:, h, :], par[:, PR_GDN:PR_GDN + 1], b_[:, 0:T], ALU.mult, ALU.mult))
                V.tensor_tensor(oT[:, h, :], oT[:, h, :], proj[:, 24 + h, :], ALU.mult).then_inc(S("a_read"), 1)
            v.wait_ge(S("a_read"), a_count("ob7"))
            split(oT[:], Ah[:], Al[:], "ya_ready")

            v.wait_ge(S("gates_ready"), 1)

            def merged(r, g, out):
                for j in range(4):
                    v.wait_ge(S("chunk_done"), 4 * (NM + 4 * r + 2 * g + 1) + j + 1)
                    out(4 * g + j, ps[:, j, 0:T])

            def gated_b(c, b_):
                V.tensor_tensor(mT[:, c, :], b_, proj[:, 40 + c, :], ALU.mult).then_inc(S("acc_read"), 1)

            def gated_a(c, b_):
                V.tensor_tensor(mtmp[:, c % 4, :], b_, proj[:, 32 + c, :], ALU.mult).then_inc(S("acc_read"), 1)
                v.wait_ge(S("acc_read"), QM + 8 + c + 1)
                V.tensor_tensor(mT[:, c, :], mT[:, c, :], mtmp[:, c % 4, :], ALU.add).then_inc(S("m_part"), 1)

            def residual(c, b_):
                V.tensor_tensor(xT[:, c, :], xT[:, c, :], b_, ALU.add).then_inc(S("acc_read"), 1)

            def split_m(g):
                v.wait_ge(S("m_part"), 4 * g + 4)
                cs = slice(4 * g, 4 * g + 4)
                split(mT[:, cs, :], Bh[:, cs, :], Bl[:, cs, :], "m_ready")

            def split_x2(g):
                v.wait_ge(S("acc_read"), QM + 16 + 4 * g + 4)
                cs = slice(4 * g, 4 * g + 4)
                link(V.tensor_tensor(x2n[:, cs, :], xT[:, cs, :], par[:, PR_MLP + 4 * g:PR_MLP + 4 * g + 4].unsqueeze(2).to_broadcast([P, 4, T]), ALU.mult))
                split(x2n[:, cs, :], Ah[:, cs, :], Al[:, cs, :], "h_split")

            merged(0, 0, gated_b)
            v.wait_ge(S("w_lo"), NM + 4)
            lo_at(NM, 1)
            merged(0, 1, gated_b)
            lo_at(NM + 1, 1)
            lo_at(NM + 2, 1)
            merged(1, 0, gated_a)
            lo_at(NM + 3, 1)
            split_m(0)
            lo_at(NM, 2)
            merged(1, 1, gated_a)
            split_m(1)
            lo_at(NM + 1, 2)
            lo_at(NM + 2, 2)
            merged(2, 0, residual)
            lo_at(NM + 3, 2)
            split_x2(0)
            lo_at(NM, 3)
            merged(2, 1, residual)
            split_x2(1)
            lo_at(NM + 1, 3)
            b_ = a_bank("x2_sum")
            V.tensor_scalar(rsq[:, 0], b_[:, 0:T], 1.0 / D, EPS, ALU.mult, ALU.add).then_inc(S("a_read"), 1)
            newton(P, rx[:], 9, 1.0, "x2_rstd")
            v.wait_ge(S("x2_rstd"), 1)


            def hidden(g, i, ns, r):
                gg = 2 * i + g
                v.wait_ge(S("h_split"), gg + 2)
                v.wait_ge(S("acc_read"), QM + 24 + 4 * g + 4 + 8 * i)
                V.tensor_tensor(hsq[:], rel[:, g], rx[:].unsqueeze(1).to_broadcast([P, 4, T]), ALU.mult).then_inc(S("h_scaled"), 1)
                lo_at(ns, r)
                v.wait_ge(S("h_scaled"), gg + 1)
                V.tensor_tensor(hsq[:], hsq[:], hsq[:], ALU.mult).then_inc(S("hsq_ready"), 1)
                v.wait_ge(S("hsq_ready"), gg + 1)
                hs = bass.ds(4 * gg, 4)
                V.tensor_copy(Hh[:, hs, :], hsq[:]).then_inc(S("h_hi"), 1)
                v.wait_ge(S("h_hi"), gg + 1)
                V.tensor_tensor(Hl[:, hs, :], hsq[:], Hh[:, hs, :].bitcast(F32), ALU.subtract).then_inc(S("h_split"), 1)

            with v.Fori(0, 4) as i:
                lo_at(NM + 2, 3 + i)
                hidden(0, i, NM + 3, 3 + i)
                lo_at(NM, 4 + i)
                hidden(1, i, NM + 1, 4 + i)
            for g in range(2):
                for u in range(8):
                    n = 8 * g + u + 2
                    if n < 16:
                        lo_at(NM + n % 4, 7 + n // 4)
                for j in range(4):
                    v.wait_ge(S("chunk_done"), 4 * (NM + 28 + 8 * g + 7) + j + 1)
                    V.tensor_tensor(xT[:, 4 * g + j, :], xT[:, 4 * g + j, :], ps[:, 4 * g + j, 0:T], ALU.add).then_inc(S("acc_read"), 1)
            for k in range(6):
                b_ = a_bank(f"y{k}")
                t = k // 2
                rows_ = P if t < 2 else NS
                V.tensor_copy(ytok[0:rows_, t, 512 * (k % 2):512 * (k % 2) + 512], b_[0:rows_]).then_inc(S("a_read"), 1)

        @block.tensor
        def _(pe):
            mm = nc.tensor.matmul
            ident = consts[:, C_ID]
            ones = consts[:, C_ONE]

            def begin(name):
                k = side(name) - 1
                if k >= 4:
                    pe.wait_ge(S("side_read"), k - 3)
                return ps[:, 4 + k % 4]

            def bank(q):
                if q >= 4:
                    pe.wait_ge(S("acc_read"), q - 3)
                return ps[:, q % 4]

            def unit(n, q0, mh, ml, first, last):
                pe.wait_ge(S("w_lo"), n + 1)
                for j in range(4):
                    if first:
                        bank(q0 + j)
                    out = ps[:, (q0 + j) % 4, 0:T]
                    for kc in range(4):
                        wh_ = hi_of(n)[:, kc, 128 * j:128 * j + 128]
                        wl_ = lo_of(n)[:, kc, 128 * j:128 * j + 128]
                        mm(out, wh_, mh[:, kc, :], start=first and kc == 0, stop=False)
                        mm(out, wh_, ml[:, kc, :], start=False, stop=False)
                        i = mm(out, wl_, mh[:, kc, :], start=False, stop=last and kc == 3)
                    i.then_inc(S("chunk_done"), 1)

            pe.wait_ge(S("consts_landed"), 16)
            pe.wait_ge(S("x_landed"), 32)
            for c in range(KC):
                b = bank(c)
                for t in range(2):
                    nc.tensor.transpose(b[:, 128 * t:128 * t + 128], xtok[:, t, 128 * c:128 * c + 128], ident)
                nc.tensor.transpose(b[:, TP:T], xtok[0:NS, 2, 128 * c:128 * c + 128], ident[0:NS, 0:NS]).then_inc(S("xT_done"), 1)
            pe.wait_ge(S("params_landed"), 16 * 12)
            nc.tensor.transpose(begin("params")[:, 0:PR_ALL], prow[0:PR_ALL, :], ident[0:PR_ALL, 0:PR_ALL]).then_inc(S("side_done"), 1)

            def sum_of(name, c0, n, last=True):
                b = begin(name)
                for c in range(n):
                    i = mm(b[:, 0:T], ones, sq[:, c0 + c, :], start=c == 0, stop=c == n - 1)
                i.then_inc(S("side_done"), 1)

            def window(r, n):
                return consts[:, C_ZW.start + 15 - r:C_ZW.start + 15 - r + n]

            def head_sums(b, r0):
                for h in range(H):
                    i = mm(b[0:16, 0:T], window(r0 + h, 16), sq[:, h, :], start=r0 == 8 and h == 0, stop=r0 == 0 and h == H - 1)
                return i

            pe.wait_ge(S("sq_ready"), 1)
            sum_of("x_sum", 0, KC)
            pe.wait_ge(S("a_ready"), 1)
            unit(0, KC, Ah[:, 0:4], Al[:, 0:4], True, False)
            unit(1, KC, Ah[:, 4:8], Al[:, 4:8], False, True)
            pe.wait_ge(S("wmisc_landed"), 64)
            b = begin("rope_raw")
            for c in range(KC):
                i = mm(b[:, 0:T], wmisc[:, c, 0:128], xn[:, c, :], start=c == 0, stop=c == KC - 1)
            i.then_inc(S("side_done"), 1)
            b = begin("decay_raw")
            for c in range(KC):
                i = mm(b[0:64, 0:T], wmisc[:, c, 128:192], xn[:, c, :], start=c == 0, stop=c == KC - 1)
            i.then_inc(S("side_done"), 1)
            unit(2, KC + 4, Ah[:, 0:4], Al[:, 0:4], True, False)
            pe.wait_ge(S("sq_ready"), 2)
            sum_of("kv_sum", 0, 4)
            pe.wait_ge(S("sq_ready"), 3)
            mm(begin("kr_sum")[:, 0:T], consts[:, C_BD], sq[:, 8, :], start=True, stop=True).then_inc(S("side_done"), 1)
            unit(3, KC + 4, Ah[:, 4:8], Al[:, 4:8], False, True)
            pe.wait_ge(S("c_ready"), 1)
            unit(UK, KC + 8, ch[:], cl[:], True, True)
            pe.wait_ge(S("sq_ready"), 4)
            sum_of("qd_sum", 4, 4)
            unit(UK + 1, KC + 12, ch[:], cl[:], True, True)
            pe.wait_ge(S("kr_scaled"), 1)
            mm(begin("kr_rot")[:, 0:T], consts[:, C_ROT], krT[:], start=True, stop=True).then_inc(S("side_done"), 1)
            pe.wait_ge(S("qd_ready"), 1)
            unit(6, KC + 16, qdh[:], qdl[:], True, True)
            pe.wait_ge(S("tables_landed"), 16)
            pe.wait_ge(S("sq_ready"), 5)
            rows_b = begin("nope_rows")
            head_sums(rows_b, 8).then_inc(S("nope_used"), 1)
            unit(7, KC + 20, qdh[:], qdl[:], True, True)
            unit(8, KC + 24, qdh[:], qdl[:], True, True)
            for n in (9, 10):
                pe.wait_ge(S("w_lo"), n + 1)
                for t in range(2):
                    out = bank(KC + 28 + 2 * (n - 9) + t)
                    tok = slice(128 * t, 128 * t + 128)
                    for kc in range(4):
                        mm(out, ch[:, kc, tok], hi_of(n)[:, kc, :], start=kc == 0, stop=False)
                        mm(out, ch[:, kc, tok], lo_of(n)[:, kc, :], start=False, stop=False)
                        i = mm(out, cl[:, kc, tok], hi_of(n)[:, kc, :], start=False, stop=kc == 3)
                    i.then_inc(S("chunk_done"), 2)
                if n == 9:
                    pe.wait_ge(S("sq_ready"), 6)
                    head_sums(rows_b, 0).then_inc(S("side_done"), 1)
            pe.wait_ge(S("sq_ready"), 7)
            b = begin("rope_rows")
            for p in range(4):
                i = mm(b[0:8, 0:T], consts[:, C_ZP.start + 6 - 2 * p:C_ZP.start + 14 - 2 * p], sq[:, p, :], start=p == 0, stop=p == 3)
            i.then_inc(S("side_done"), 1)
            pe.wait_ge(S("nope_rstd"), 1)
            for h in range(16):
                mm(begin(f"nope{h}")[:, 0:T], consts[0:16, C_ID.start + h:C_ID.start + h + 1].to_broadcast([16, P]), nrow[:],
                   start=True, stop=True).then_inc(S("side_done"), 1)
            pe.wait_ge(S("rope_rstd"), 1)
            for p in range(4):
                b = begin(f"rope{p}")
                for half in range(2):
                    col = C_ID.start + 2 * p + half
                    i = mm(b[64 * half:64 * half + 64, 0:T], consts[0:8, col:col + 1].to_broadcast([8, 64]), rrow[:], start=True, stop=True)
                i.then_inc(S("side_done"), 1)
            for p in range(4):
                pe.wait_ge(S("side_read"), side(f"rope{p}"))
                mm(begin(f"rot{p}")[:, 0:T], consts[:, C_ROT], qr[:, p, :], start=True, stop=True).then_inc(S("side_done"), 1)

            def scores(h):
                if h >= 2:
                    pe.wait_ge(S("sc_read"), h - 1)
                b = ps[:, h % 2]
                r = slice(64 * (h % 2), 64 * (h % 2) + 64)
                mm(b[:, 0:128], qn[:, h, 0:128], kn[:, h, 0:128], start=True, stop=False)
                mm(b[:, 0:128], qr[r, h // 2, 0:128], krT[r, 0:128], start=False, stop=True)
                mm(b[:, 128:384], qn[:, h, 128:256], kn[:, h, 0:256], start=True, stop=False)
                mm(b[:, 128:384], qr[r, h // 2, 128:256], krT[r, 0:256], start=False, stop=True).then_inc(S("sc_done"), 1)

            def transposed(h):
                pe.wait_ge(S("p_ready"), h + 1)
                if h >= 1:
                    pe.wait_ge(S("pt_read"), h)
                for j in range(3):
                    i = nc.tensor.transpose(ps[:, 2, 128 * j:128 * j + 128], pr[:, h % 3, 128 * j:128 * j + 128], ident)
                i.then_inc(S("pt_done"), 1)

            def weighed(h):
                pe.wait_ge(S("pt_read"), h + 1)
                if h >= 1:
                    pe.wait_ge(S("yb_read"), h)
                b, hd = ps[:, 3], slice(128 * h, 128 * h + 128)
                mm(b[:, 0:128], vtok[:, 0, hd], pT[:, h % 2, 0:128], start=True, stop=True)
                mm(b[:, 128:256], vtok[:, 0, hd], pT[:, h % 2, 128:256], start=True, stop=False)
                mm(b[:, 128:256], vtok[:, 1, hd], pT[:, h % 2, 256:384], start=False, stop=True).then_inc(S("pv_done"), 1)

            pe.wait_ge(S("qr_ready"), 1)
            pe.wait_ge(S("acc_read"), KC + 32)
            for h in range(H):
                scores(h)
                if h >= 2:
                    transposed(h - 2)
                if h >= 3:
                    weighed(h - 3)
                if h < 6:
                    b = begin(f"row{h}")
                    t0, n_ = CH * (h // 2), CH if h < 4 else NS
                    if h % 2 == 0:
                        for c in range(4):
                            i = nc.tensor.transpose(b[0:n_, 128 * c:128 * c + 128], kv[:, c, t0:t0 + n_], ident)
                    else:
                        i = nc.tensor.transpose(b[0:n_, 0:ROPE], krT[0:ROPE, t0:t0 + n_], ident[0:ROPE, 0:ROPE])
                    i.then_inc(S("side_done"), 1)
            transposed(H - 2)
            weighed(H - 3)
            transposed(H - 1)
            weighed(H - 2)
            weighed(H - 1)

            pe.wait_ge(S("ukf_ready"), 1)
            pe.wait_ge(S("side_read"), len(SIDE))
            pe.wait_ge(S("qg_ready"), 1)

            def turned(h):
                if h >= 2:
                    pe.wait_ge(S("ukT_read"), h - 1)
                for c in range(4):
                    i = nc.tensor.transpose(ps[:, 4 + h % 2, 128 * c:128 * c + 128], ukf[:, c, 128 * h:128 * h + 128], ident)
                i.then_inc(S("ukT_done"), 1)

            turned(0)
            for h in range(H):
                if h + 1 < H:
                    turned(h + 1)
                pe.wait_ge(S("ukT_read"), h + 1)
                for c in range(4):
                    i = mm(ps[:, 6, (c * H + h) * NS:(c * H + h + 1) * NS], ukT[:, h % 2, 128 * c:128 * c + 128], qg[:, h, :], start=True, stop=True)
                i.then_inc(S("qe_done"), 1)
            pe.wait_ge(S("qk_ready"), 1)
            mm(ps[:, 7, 0:64], ones, qk[:, 0], start=True, stop=False)
            mm(ps[:, 7, 0:64], ones, qk[:, 1], start=False, stop=True).then_inc(S("qk_sum"), 1)

            for w, val in FRONT_DONE:
                pe.wait_ge(S(w), val)

            def transposes(i, u):
                n = 8 * i + u
                pe.wait_ge(S(f"page_landed{u}"), 16 * i + 16)
                wait(pe, "ct_lo", n)
                for c in range(4):
                    nc.tensor.transpose(ps[:, 4, 128 * c:128 * c + 128], craw[:, u, 128 * c:128 * c + 128], ident)
                nc.tensor.transpose(ps[:, 5, 0:128], craw[:, u, LW - 128:LW], ident).then_inc(S("tr_done"), 1)

            def keys(i, u):
                n = 8 * i + u
                tok = slice(128 * (u % 4), 128 * (u % 4) + 128)
                pe.wait_ge(S("ct_lo"), n + 1)
                wait(pe, "ksq_ready", n - 1)
                for half_ in range(2):
                    out, cols = kps(u)[:, half_], slice(512 * half_, 512 * half_ + 512)
                    for c in range(4):
                        mm(out, cTh[:, c, tok], ukh[:, c, cols], start=c == 0, stop=False)
                        mm(out, cTh[:, c, tok], ukl[:, c, cols], start=False, stop=False)
                        k = mm(out, cTl[:, c, tok], ukh[:, c, cols], start=False, stop=c == 3)
                k.then_inc(S("k_done"), 1)

            def query_products(gg, i):
                pe.wait_ge(S("qst_ready"), i + 1)
                wait(pe, "s_ready", gg)
                for c in range(5):
                    mm(ps[:, 6, :], qst[:, c, :], cTh[:, c, :], start=c == 0, stop=False)
                    k = mm(ps[:, 6, :], qst[:, c, :], cTl[:, c, :], start=False, stop=c == 4)
                k.then_inc(S("qk_done"), 1)

            def score_columns(gg):
                pe.wait_ge(S("ssb_ready"), gg + 1)
                for t in range(4):
                    k = mm(stp[:, t, :], ssb[:, 128 * t:128 * t + 128], consts[0:48, C_II], start=True, stop=True)
                k.then_inc(S("st_done"), 1)

            def weigh(gg, y):
                pe.wait_ge(S("pst_ready"), gg + 1)
                wait(pe, "accT_ready", gg)
                for t in range(4):
                    mm(ps[:, 7, :], pst[:, y, t, :], nath[:, y, t, :], start=t == 0, stop=False)
                    k = mm(ps[:, 7, :], pst[:, y, t, :], natl[:, y, t, :], start=False, stop=t == 3)
                k.then_inc(S("pv_used"), 1)

            def latent_columns(gg):
                pe.wait_ge(S("pvs_ready"), gg + 1)
                for c in range(4):
                    k = mm(pvt[:, c * H:(c + 1) * H], pvs[:, 128 * c:128 * c + 128], consts[0:16, C_II.start:C_II.start + 8], start=True, stop=True)
                k.then_inc(S("pvt_done"), 1)

            def body_pe(i, first, last):
                for u in range(8):
                    n, y, t = 8 * i + u, u // 4, u % 4
                    prev = not (first and y == 0)
                    if t == 3:
                        pe.wait_ge(S("ct_lo"), n + 1)
                        query_products(2 * i + y, i)
                    if u < 7:
                        transposes(i, u + 1)
                    elif not last:
                        transposes(i + 1, 0)
                    keys(i, u)
                    if t == 2 and prev:
                        weigh(2 * i + y - 1, 1 - y)
                    if t == 3:
                        score_columns(2 * i + y)
                    if t == 3 and prev:
                        latent_columns(2 * i + y - 1)

            transposes(0, 0)
            body_pe(0, True, False)
            with pe.Fori(1, NG // 2 - 1) as i:
                body_pe(i, False, False)
            body_pe(NG // 2 - 1, False, True)
            weigh(NG - 1, 1)
            latent_columns(NG - 1)
            pe.wait_ge(S("lpart_ready"), 1)
            mm(ps[:, 6, 0:64], ones, lfin[:, 0].rearrange("p s h -> p (s h)"), start=True, stop=True).then_inc(S("lsum_done"), 1)
            pe.wait_ge(S("olat_ready"), 1)
            pe.wait_ge(S("wuvf_landed"), 16)
            for h in range(H):
                for c in range(4):
                    k = mm(ps[:, 7, NS * h:NS * h + NS], wuvf[:, c, 128 * h:128 * h + 128], olat[:, :, c, h], start=c == 0, stop=c == 3)
            k.then_inc(S("yb_sample"), 1)

            def unit_at(ns, r, mh, ml, first, last, drained=None, bank0=0):
                pe.wait_ge(S("w_lo"), ns + 1 + 4 * r)
                for j in range(4):
                    if first and drained is not None:
                        pe.wait_ge(S("acc_read"), drained + j)
                    out = ps[:, bank0 + j, 0:T]
                    for kc in range(4):
                        w_hi, w_lo = wh[:, ns % 2, kc, 128 * j:128 * j + 128], wl[:, ns % 2, kc, 128 * j:128 * j + 128]
                        mm(out, w_hi, mh[:, kc, :], start=first and kc == 0, stop=False)
                        mm(out, w_hi, ml[:, kc, :], start=False, stop=False)
                        k = mm(out, w_lo, mh[:, kc, :], start=False, stop=last and kc == 3)
                    k.then_inc(S("chunk_done"), 1)

            def body(ns, r, q0, mh, ml, beside=None):
                for u in range(4):
                    ks = slice(4 * (u % 2), 4 * (u % 2) + 4)
                    unit_at(ns + u, r, mh[:, ks], ml[:, ks], u % 2 == 0, u % 2 == 1, q0 + 2 * u - 3)
                    if beside:
                        beside(u)

            pe.wait_ge(S("ksq_ready"), NT)
            with pe.Fori(0, 3) as i:
                body(NP, i, QP + 8 * i, Ah, Al)

            def begin_a(name):
                k = SIDE_A.index(name)
                if k >= 4:
                    pe.wait_ge(S("a_read"), k - 3)
                else:
                    pe.wait_ge(S("b_read"), b_count("cs5"))
                return ps[:, 4 + k % 4]

            def begin_b(name):
                k = SIDE_B.index(name)
                if k >= 4:
                    pe.wait_ge(S("b_read"), k - 3)
                return b_bank(k)

            def a_done(k):
                k.then_inc(S("a_done"), 1)

            def b_done(k):
                k.then_inc(S("b_done"), 1)

            def rows_of_state(g):
                b = begin_b(f"rw{g}")
                for c in range(4):
                    k = nc.tensor.transpose(b[0:11, 128 * c:128 * c + 128], proj[:, 4 * g + c, TP - 3:T], ident)
                b_done(k)

            def columns_of_state(g):
                b = begin_b(f"cs{g}")
                for c in range(4):
                    k = nc.tensor.transpose(b[:, 24 * c:24 * c + 24], scrow[:, 128 * (4 * g + c):128 * (4 * g + c) + 128], ident[0:24, 0:24])
                b_done(k)

            def spread(name):
                n = int(name[2:])
                if name.startswith("bg"):
                    a_done(nc.tensor.transpose(begin_a(name)[:, 0:64], rw[:, CH * n:CH * n + CH], ident[0:64, 0:64]))
                else:
                    col = C_ID.start + n + (32 if name.startswith("gr") else 0)
                    a_done(mm(begin_a(name)[:, 0:T], consts[0:64, col:col + 1].to_broadcast([64, P]), rw[:], start=True, stop=True))

            def beside(k):
                if k == 0:
                    pe.wait_ge(S("acc_read"), QP + 24)
                if k == 2:
                    pe.wait_ge(S("scrow_landed"), 16)
                if k < 4:
                    for g in range(3 * (k % 2), 3 * (k % 2) + 3):
                        (rows_of_state if k < 2 else columns_of_state)(g)
                if k == 4:
                    pe.wait_ge(S("g_ready"), 1)
                    pe.wait_ge(S("beta_ready"), 1)
                if 4 <= k < 9:
                    for name in SPREAD[k - 4]:
                        spread(name)
                if k >= 8:
                    b = begin_a("l2rows")
                    for c in range(4 * (k - 8), 4 * (k - 8) + 4):
                        pe.wait_ge(S("gsq_ready"), c + 1)
                        m = mm(b[0:16, 0:T], window(c, 16), gsq[:, c % 4, :], start=c == 0, stop=c == 15)
                        if c < 15:
                            m.then_inc(S("l2_used"), 1)
                    if k == 11:
                        a_done(m)

            for i in range(3, 6):
                body(NP, i, QP + 8 * i, Ah, Al, lambda u: beside(4 * (i - 3) + u))
            pe.wait_ge(S("acc_read"), QP + 48)
            pe.wait_ge(S("silu_done"), 24)
            for g in range(4):
                b = begin_b(f"vt{g}")
                for w in range(4):
                    h, n = (4 * g + w) // 2, w % 2
                    k = nc.tensor.transpose(b[:, CH * w:CH * w + CH], proj[:, 16 + h, CH * n:CH * n + CH], ident)
                b_done(k)
            pe.wait_ge(S("lrow_ready"), 1)
            for c in range(16):
                col = C_ID.start + c
                a_done(mm(begin_a(f"l2b{c}")[:, 0:T], consts[0:16, col:col + 1].to_broadcast([16, P]), lrow[:], start=True, stop=True))

            def four(name, g, product):
                b = begin_a(name)
                for w in range(4):
                    k = product(b[:, CH * w:CH * w + CH], 4 * g + w)
                a_done(k)

            def chunk(c0, u):
                return proj[:, c0 + u // 2, CH * (u % 2):CH * (u % 2) + CH]

            pe.wait_ge(S("a_read"), a_count("l2b15"))
            for g in range(4):
                four(f"qk{g}", g, lambda out, u: mm(out, chunk(8, u), chunk(0, u), start=True, stop=True))
            for g in range(4):
                four(f"kk{g}", g, lambda out, u: mm(out, chunk(8, u), chunk(8, u), start=True, stop=True))
            for g in range(4):
                four(f"kt{g}", g, lambda out, u: nc.tensor.transpose(out, chunk(8, u), ident))
            pe.wait_ge(S("tu_ready"), 1)
            for s_ in range(LEVELS):
                for g in range(4):
                    if s_ >= 1:
                        pe.wait_ge(S("a_read"), a_count(f"t{s_ - 1}_{g}"))
                    four(f"x{s_}_{g}", g, lambda out, u: mm(out, lT[:, u, :], T_[:, u, :], start=True, stop=True))
                for g in range(4):
                    pe.wait_ge(S("a_read"), a_count(f"x{s_}_{g}"))
                    if s_ >= 1:
                        pe.wait_ge(S("a_read"), a_count(f"u{s_ - 1}_{g}"))
                    if s_ < LEVELS - 1:
                        four(f"t{s_}_{g}", g, lambda out, u: mm(out, U_[:, u, :], X_[:, u, :], start=True, stop=True))
                    four(f"u{s_}_{g}", g, lambda out, u: mm(out, X_[:, u, :], U_[:, u, :], start=True, stop=True))
            pe.wait_ge(S("a_read"), a_count(f"u{LEVELS - 1}_3"))
            pe.wait_ge(S("rhs_ready"), 1)
            for g in range(2):
                four(f"uu0_{g}", g, lambda out, h: mm(out, U_[:, 2 * h, :], rhs_[:, h, :], start=True, stop=True))
            for g in range(2):
                pe.wait_ge(S("a_read"), a_count(f"uu0_{g}"))
                four(f"o0_{g}", g, lambda out, h: mm(out, uu[:, h, :], aqT[:, 2 * h, :], start=True, stop=True))
            for g in range(2):
                four(f"s0_{g}", g, lambda out, h: mm(out, kd[:, 2 * h, :], uu[:, h, :], start=True, stop=True))
            for g in range(2):
                pe.wait_ge(S("a_read"), a_count(f"s0_{g}"))
                four(f"ks_{g}", g, lambda out, h: mm(out, chunk(8, 2 * h + 1), st[:, h, :], start=True, stop=True))
            pe.wait_ge(S("rhs_ready"), 2)
            for g in range(2):
                four(f"uu1_{g}", g, lambda out, h: mm(out, U_[:, 2 * h + 1, :], rhs_[:, h, :], start=True, stop=True))

            def second_output(out, h):
                mm(out, st[:, h, :], chunk(0, 2 * h + 1), start=True, stop=False)
                return mm(out, uu[:, h, :], aqT[:, 2 * h + 1, :], start=False, stop=True)

            for g in range(2):
                pe.wait_ge(S("a_read"), a_count(f"uu1_{g}"))
                four(f"o1_{g}", g, second_output)
            for g in range(2):
                four(f"s1_{g}", g, lambda out, h: mm(out, kd[:, 2 * h + 1, :], uu[:, h, :], start=True, stop=True))
            pe.wait_ge(S("sst_landed"), 16 * NS)
            qks = proj[:, 0:16, :].rearrange("p (t h) n -> p h n t", t=2)
            b = begin_a("kqs")
            for s_ in range(NS):
                for h in range(H):
                    at = 2 * (H * s_ + h)
                    k = mm(b[:, at:at + 2], sst[:, s_, h, :], qks[:, h, TP + s_, :], start=True, stop=True)
            a_done(k)
            pe.wait_ge(S("ksmall_ready"), 2)
            a_done(mm(begin_a("qks")[:, 0:64], ones, sm[:, 2], start=True, stop=True))
            a_done(nc.tensor.transpose(begin_a("krow")[0:64, 0:128], sm[:, 1], ident))
            pe.wait_ge(S("u_ready"), 1)
            a_done(nc.tensor.transpose(begin_a("urow")[0:64, 0:128], sm[:, 5], ident))
            pe.wait_ge(S("a_read"), a_count("urow"))
            for s_ in range(NS):
                pe.wait_ge(S("umask_ready"), s_ + 1)
                for g in range(2):
                    a_done(mm(begin_a(f"out{s_}_{g}"), urow[:, 0, :], umask[s_ % 2][:, 4 * g:4 * g + 4, :].rearrange("p h n -> p (h n)"), start=True, stop=True))
            pe.wait_ge(S("osq_ready"), 1)
            b = begin_a("orows")
            for h in range(H):
                k = mm(b[0:8, 0:T], window(h, 8), osq[:, h, :], start=h == 0, stop=h == H - 1)
            a_done(k)
            pe.wait_ge(S("orow_ready"), 1)
            for h in range(H):
                col = C_ID.start + h
                a_done(mm(begin_a(f"ob{h}")[:, 0:T], consts[0:8, col:col + 1].to_broadcast([8, P]), orow[:], start=True, stop=True))

            pe.wait_ge(S("b_read"), len(SIDE_B))
            pe.wait_ge(S("yb_split"), 1)
            body(NM, 0, QM, Bh, Bl)
            pe.wait_ge(S("ya_ready"), 1)
            body(NM, 1, QM + 8, Ah, Al)
            pe.wait_ge(S("m_ready"), 1)
            body(NM, 2, QM + 16, Bh, Bl, lambda u: pe.wait_ge(S("m_ready"), 2) if u == 0 else None)

            def first_up(u):
                if u == 0:
                    pe.wait_ge(S("xsq_ready"), 1)
                    b = begin_a("x2_sum")
                    for c in range(KC):
                        k = mm(b[:, 0:T], ones, xsq[:, c, :], start=c == 0, stop=c == KC - 1)
                    a_done(k)
                    pe.wait_ge(S("h_split"), 2)

            pe.wait_ge(S("h_split"), 1)
            body(NM, 3, QM + 24, Ah, Al, first_up)
            with pe.Fori(1, 4) as i:
                body(NM, 3 + i, QM + 24 + 8 * i, Ah, Al)
            for g in range(2):
                for u in range(8):
                    if g == 0:
                        pe.wait_ge(S("h_split"), 2 + u + 1)
                    unit_at(NM + u % 4, 7 + 2 * g + u // 4, Hh[:, 4 * u:4 * u + 4], Hl[:, 4 * u:4 * u + 4], u == 0, u == 7,
                            QM + 56 - 3 if g == 0 else None, 4 * g)
            pe.wait_ge(S("acc_read"), QM + 64)
            for k6 in range(6):
                b, t = begin_a(f"y{k6}"), k6 // 2
                n_ = P if t < 2 else NS
                for c in range(4):
                    k = nc.tensor.transpose(b[0:n_, 128 * c:128 * c + 128], xT[:, 4 * (k6 % 2) + c, CH * t:CH * t + n_], ident)
                a_done(k)


INPUTS = ["x_prompt", "x_sample", "cache_mla", "state_gdn", "state_conv", "page_table", "norm_mix", "w_in", "conv_w", "a_log",
          "dt_bias", "gdn_norm", "q_a_norm", "w_uq", "kv_a_norm", "w_uk", "w_uv", "q_norm_nope", "q_norm_rope", "k_norm_nope",
          "k_norm_rope", "w_ya", "w_yb", "w_o", "norm_mlp", "w_up", "w_down"]

OUTPUTS = [("y_prompt", (1, TP, D)), ("y_sample", (NS, 1, D)), ("rows_prompt", (1, 1, TP, LW)), ("gdn_prompt", (1, 1, H, P, P)),
           ("conv_prompt", (1, 1, CONVW - 1, 3 * D)), ("rows_sample", (1, NS, 1, LW)), ("gdn_sample", (1, NS, H, P, P)),
           ("conv_sample", (1, NS, CONVW - 1, 3 * D))]


def kernel(**inputs):
    import concourse.bacc as bacc
    from concourse.bass_utils import run_bass_kernel_spmd

    nc = bacc.Bacc("TRN2", target_bir_lowering=False, num_devices=1)
    arrays = {n: np.ascontiguousarray(inputs[n]) for n in INPUTS}
    arrays["consts"] = constants()
    I = {n: nc.dram_tensor(n, a.shape, mybir.dt.from_np(a.dtype), kind="ExternalInput").ap() for n, a in arrays.items()}
    O = {n: nc.dram_tensor(n, shape, F32, kind="ExternalOutput").ap() for n, shape in OUTPUTS}
    build(nc, I, O)
    r = run_bass_kernel_spmd(nc, [arrays], core_ids=[0])
    return tuple(r.results[0][n] for n, _ in OUTPUTS)
```
